# Optimizing a Trainium2 kernel written in Bass

```python
import math
import jax
import jax.numpy as jnp
from jax import lax
import numpy as np

D_MODEL = 2048
BATCH = 1
SEQ = 256
DEPTH = 1
DEC_BATCH = 8
DEC_SEQ = 1
PAST_LEN = 1024
PAGE_SIZE = 128

A_HEADS = 8
A_DH = 128
A_W = A_HEADS * A_DH
MOBA_BLOCK = 256
MOBA_TOPK = 3
MOBA_Q_CHUNK = 32
T5_BUCKETS = 32
T5_MAX_DIST = 128
R_HEADS = 4
R_DK = 256
R_DV = 256
R_KW = R_HEADS * R_DK
R_VW = R_HEADS * R_DV
RET_CHUNK = 128
RET_ROPE_BASE = 10000.0
M_HEADS = 4
M_DH = 256
M_W = M_HEADS * M_DH
N_MEM = 256
D_FF = 5632
EPS = 1e-6
NEG_INF = -1e30
IN_SECTIONS = (A_W, A_W, A_W, R_KW, R_KW, R_VW, R_VW, M_W)
SPLIT_POINTS = tuple(int(s) for s in np.cumsum(IN_SECTIONS)[:-1])
IN_COLS = int(sum(IN_SECTIONS))

kernel_name = "hybrid_moba_retention_memory_decoder_step"

def rmsnorm(x, g):
    xf = x.astype(jnp.float32)
    y = xf * lax.rsqrt(jnp.mean(xf * xf, axis=-1, keepdims=True) + EPS)
    return (y * g.astype(jnp.float32)).astype(x.dtype)

def head_rmsnorm(x):
    return x * lax.rsqrt(jnp.mean(x * x, axis=-1, keepdims=True) + EPS)

def ffn_half(x, g, w1, w3, w2):
    h = rmsnorm(x, g)
    return x + 0.5 * ((jax.nn.silu(h @ w1) * (h @ w3)) @ w2)

def t5_bucket(n):
    n = jnp.maximum(n, 0)
    max_exact = T5_BUCKETS // 2
    nf = jnp.maximum(n, 1).astype(jnp.float32)
    large = max_exact + (jnp.log(nf / max_exact) / math.log(T5_MAX_DIST / max_exact)
                         * (T5_BUCKETS - max_exact)).astype(jnp.int32)
    return jnp.where(n < max_exact, n, jnp.minimum(large, T5_BUCKETS - 1))

def rotate(x, pos):
    d = x.shape[-1]
    half = d // 2
    inv = 1.0 / (RET_ROPE_BASE ** jnp.linspace(0.0, 1.0, half, dtype=jnp.float32))
    ang = pos.astype(jnp.float32)[:, None] * inv[None, :]
    cos = jnp.cos(ang)[None, :, None, :]
    sin = jnp.sin(ang)[None, :, None, :]
    xf = x.astype(jnp.float32)
    x1, x2 = xf[..., :half], xf[..., half:]
    return jnp.concatenate([x1 * cos - x2 * sin, x1 * sin + x2 * cos], axis=-1)

def moba_attend(q, k, v, q_pos, t5_table):
    B, Sq, H, dh = q.shape
    nb = k.shape[1] // MOBA_BLOCK
    kbh = k.reshape(B, nb, MOBA_BLOCK, H, dh).transpose(0, 3, 1, 2, 4)
    vbh = v.reshape(B, nb, MOBA_BLOCK, H, dh).transpose(0, 3, 1, 2, 4)
    kmean = jnp.mean(kbh.astype(jnp.float32), axis=3)
    n_sel = min(MOBA_TOPK, nb)
    qc = math.gcd(Sq, MOBA_Q_CHUNK)
    n_chunks = Sq // qc
    bias_tab = t5_table.astype(jnp.float32).T
    scale = dh ** -0.5
    b_ix = jnp.arange(B)[:, None, None, None]
    h_ix = jnp.arange(H)[None, :, None, None]
    blk_ar = jnp.arange(MOBA_BLOCK, dtype=jnp.int32)
    blk_ids = jnp.arange(nb, dtype=jnp.int32)

    def one_chunk(args):
        qb, pos = args
        qf = qb.astype(jnp.float32)
        cur = pos // MOBA_BLOCK
        gate = jnp.einsum('bqhd,bhnd->bhqn', qf, kmean)
        past = blk_ids[None, :] < cur[:, None]
        gate = jnp.where(past[None, None], gate, NEG_INF)
        _, sel = lax.top_k(gate, n_sel)
        sel_ok = sel < cur[None, None, :, None]
        ks = kbh[b_ix, h_ix, sel].astype(jnp.float32)
        vs = vbh[b_ix, h_ix, sel].astype(jnp.float32)
        s_sel = jnp.einsum('bqhd,bhqsjd->bhqsj', qf, ks) * scale
        dist_sel = pos[None, None, :, None, None] - (sel[..., None] * MOBA_BLOCK + blk_ar)
        s_sel = s_sel + bias_tab[h_ix[..., None], t5_bucket(dist_sel)]
        s_sel = jnp.where(sel_ok[..., None], s_sel, NEG_INF)
        own = pos[0] // MOBA_BLOCK
        k_own = lax.dynamic_index_in_dim(kbh, own, axis=2, keepdims=False).astype(jnp.float32)
        v_own = lax.dynamic_index_in_dim(vbh, own, axis=2, keepdims=False).astype(jnp.float32)
        dist_own = pos[:, None] - (own * MOBA_BLOCK + blk_ar)[None, :]
        s_own = jnp.einsum('bqhd,bhjd->bhqj', qf, k_own) * scale + bias_tab[:, t5_bucket(dist_own)][None]
        s_own = jnp.where(dist_own[None, None] >= 0, s_own, NEG_INF)
        logits = jnp.concatenate([s_sel.reshape(B, H, qc, n_sel * MOBA_BLOCK), s_own], axis=-1)
        p = jax.nn.softmax(logits, axis=-1)
        p_sel = p[..., :n_sel * MOBA_BLOCK].reshape(B, H, qc, n_sel, MOBA_BLOCK)
        p_own = p[..., n_sel * MOBA_BLOCK:]
        o = (jnp.einsum('bhqsj,bhqsjd->bqhd', p_sel, vs)
             + jnp.einsum('bhqj,bhjd->bqhd', p_own, v_own))
        return o.astype(q.dtype)

    qs = q.reshape(B, n_chunks, qc, H, dh).transpose(1, 0, 2, 3, 4)
    ps = q_pos.reshape(n_chunks, qc)
    out = lax.map(one_chunk, (qs, ps))
    return out.transpose(1, 0, 2, 3, 4).reshape(B, Sq, H, dh)

def retention_scan(q, k, v, s0):
    B, S, H, dk = q.shape
    dv = v.shape[-1]
    c = math.gcd(S, RET_CHUNK)
    n = S // c
    log_g = jnp.log(1.0 - jnp.exp2(-5.0 - jnp.arange(H, dtype=jnp.float32)))
    i = jnp.arange(c, dtype=jnp.float32)
    diff = i[:, None] - i[None, :]
    dmask = jnp.where(diff[None] >= 0, jnp.exp(jnp.maximum(diff, 0.0)[None] * log_g[:, None, None]), 0.0)
    q_dec = jnp.exp((i[:, None] + 1.0) * log_g[None, :])
    k_dec = jnp.exp((c - 1.0 - i)[:, None] * log_g[None, :])
    c_dec = jnp.exp(c * log_g)

    def to_chunks(t):
        return t.reshape(B, n, c, H, t.shape[-1]).transpose(1, 0, 2, 3, 4)

    def step(s, xs):
        qc, kc, vc = xs
        att = jnp.einsum('bihd,bjhd->bhij', qc, kc) * dmask[None]
        o = (jnp.einsum('bhij,bjhe->bihe', att, vc)
             + jnp.einsum('bihd,bhde->bihe', qc * q_dec[None, :, :, None], s))
        s = s * c_dec[None, :, None, None] + jnp.einsum('bjhd,bjhe->bhde', kc * k_dec[None, :, :, None], vc)
        return s, o

    s, o = lax.scan(step, s0, (to_chunks(q), to_chunks(k), to_chunks(v)))
    return o.transpose(1, 0, 2, 3, 4).reshape(B, S, H, dv), s

def mem_attend(q, mk, mv):
    s = jnp.einsum('bqhd,bmhd->bhqm', q.astype(jnp.float32), mk.astype(jnp.float32)) * (M_DH ** -0.5)
    p = jax.nn.softmax(s, axis=-1)
    return jnp.einsum('bhqm,bmhd->bqhd', p, mv.astype(jnp.float32))

def mem_kv(mem, g, w_mem_kv):
    B = mem.shape[0]
    kv = rmsnorm(mem, g) @ w_mem_kv
    mk, mv = jnp.split(kv, 2, axis=-1)
    return mk.reshape(B, N_MEM, M_HEADS, M_DH), mv.reshape(B, N_MEM, M_HEADS, M_DH)

def decoder_layer(x, pos, mk, mv, k_past, v_past, ret_s0, t5_table, lw):
    B, S, _ = x.shape
    x = ffn_half(x, lw['ffn1_norm'], lw['ffn1_w1'], lw['ffn1_w3'], lw['ffn1_w2'])
    h = rmsnorm(x, lw['mix_norm'])
    z = h @ lw['w_in']
    qa, ka, va, qr, kr, vr, gr, qm = jnp.split(z, SPLIT_POINTS, axis=-1)
    qa = qa.reshape(B, S, A_HEADS, A_DH)
    ka = ka.reshape(B, S, A_HEADS, A_DH)
    va = va.reshape(B, S, A_HEADS, A_DH)
    if k_past is None:
        k_cat, v_cat = ka, va
    else:
        k_cat = jnp.concatenate([k_past.astype(ka.dtype), ka], axis=1)
        v_cat = jnp.concatenate([v_past.astype(va.dtype), va], axis=1)
    pad = (-k_cat.shape[1]) % MOBA_BLOCK
    k_cat = jnp.pad(k_cat, ((0, 0), (0, pad), (0, 0), (0, 0)))
    v_cat = jnp.pad(v_cat, ((0, 0), (0, pad), (0, 0), (0, 0)))
    oa = moba_attend(qa, k_cat, v_cat, pos, t5_table)
    qr = rotate(qr.reshape(B, S, R_HEADS, R_DK), pos)
    kr = rotate(kr.reshape(B, S, R_HEADS, R_DK), pos) * (R_DK ** -0.5)
    vr = vr.reshape(B, S, R_HEADS, R_DV).astype(jnp.float32)
    o_r, s_new = retention_scan(qr, kr, vr, ret_s0.astype(jnp.float32))
    o_r = head_rmsnorm(o_r) * jax.nn.silu(gr.astype(jnp.float32)).reshape(B, S, R_HEADS, R_DV)
    om = mem_attend(qm.reshape(B, S, M_HEADS, M_DH), mk, mv)
    gates = jax.nn.sigmoid((h @ lw['w_gate'] + lw['b_gate']).astype(jnp.float32))
    g_a, g_r, g_m = jnp.split(gates, 3, axis=-1)
    merged = (g_a * (oa.reshape(B, S, A_W) @ lw['w_br_moba']).astype(jnp.float32)
              + g_r * (o_r.reshape(B, S, R_VW).astype(x.dtype) @ lw['w_br_ret']).astype(jnp.float32)
              + g_m * (om.reshape(B, S, M_W).astype(x.dtype) @ lw['w_br_mem']).astype(jnp.float32))
    x = x + merged.astype(x.dtype) @ lw['w_out']
    x = ffn_half(x, lw['ffn2_norm'], lw['ffn2_w1'], lw['ffn2_w3'], lw['ffn2_w2'])
    return x, ka, va, s_new

def setup_inputs(seed: int = 0) -> dict:
    key = jax.random.key(seed)
    ks = iter(jax.random.split(key, 48))
    n_pages = PAST_LEN // PAGE_SIZE
    used = DEC_BATCH * n_pages
    n_pool = used + used // 4

    def nrm(shape, scale):
        return jax.random.normal(next(ks), shape, jnp.float32) * scale

    def gain(shape):
        return 1.0 + nrm(shape, 0.05)

    page_table = jax.random.permutation(next(ks), n_pool)[:used].reshape(DEC_BATCH, n_pages).astype(jnp.int32)
    return {
        "x_prompt": nrm((BATCH, SEQ, D_MODEL), 1.0),
        "x_sample": nrm((DEC_BATCH, DEC_SEQ, D_MODEL), 1.0),
        "mem_prompt": nrm((BATCH, N_MEM, D_MODEL), 1.0),
        "cache_k": nrm((DEPTH, n_pool, PAGE_SIZE, A_HEADS, A_DH), 1.0),
        "cache_v": nrm((DEPTH, n_pool, PAGE_SIZE, A_HEADS, A_DH), 1.0),
        "cache_mem_k": nrm((DEPTH, DEC_BATCH, N_MEM, M_HEADS, M_DH), 1.0),
        "cache_mem_v": nrm((DEPTH, DEC_BATCH, N_MEM, M_HEADS, M_DH), 1.0),
        "state_ret": nrm((DEPTH, DEC_BATCH, R_HEADS, R_DK, R_DV), 0.1),
        "page_table": page_table,
        "t5_table": nrm((T5_BUCKETS, A_HEADS), 0.5),
        "ffn1_norm": gain((DEPTH, D_MODEL)),
        "ffn1_w1": nrm((DEPTH, D_MODEL, D_FF), D_MODEL ** -0.5),
        "ffn1_w3": nrm((DEPTH, D_MODEL, D_FF), D_MODEL ** -0.5),
        "ffn1_w2": nrm((DEPTH, D_FF, D_MODEL), D_FF ** -0.5),
        "mix_norm": gain((DEPTH, D_MODEL)),
        "mem_norm": gain((DEPTH, D_MODEL)),
        "w_in": nrm((DEPTH, D_MODEL, IN_COLS), D_MODEL ** -0.5),
        "w_mem_kv": nrm((DEPTH, D_MODEL, 2 * M_W), D_MODEL ** -0.5),
        "w_gate": nrm((DEPTH, D_MODEL, 3 * D_MODEL), D_MODEL ** -0.5),
        "b_gate": nrm((DEPTH, 3 * D_MODEL), 0.1),
        "w_br_moba": nrm((DEPTH, A_W, D_MODEL), A_W ** -0.5),
        "w_br_ret": nrm((DEPTH, R_VW, D_MODEL), R_VW ** -0.5),
        "w_br_mem": nrm((DEPTH, M_W, D_MODEL), M_W ** -0.5),
        "w_out": nrm((DEPTH, D_MODEL, D_MODEL), D_MODEL ** -0.5),
        "ffn2_norm": gain((DEPTH, D_MODEL)),
        "ffn2_w1": nrm((DEPTH, D_MODEL, D_FF), D_MODEL ** -0.5),
        "ffn2_w3": nrm((DEPTH, D_MODEL, D_FF), D_MODEL ** -0.5),
        "ffn2_w2": nrm((DEPTH, D_FF, D_MODEL), D_FF ** -0.5),
        "final_norm": gain((D_MODEL,)),
    }

def reference(x_prompt, x_sample, mem_prompt, cache_k, cache_v, cache_mem_k, cache_mem_v, state_ret,
              page_table, t5_table, ffn1_norm, ffn1_w1, ffn1_w3, ffn1_w2, mix_norm, mem_norm, w_in,
              w_mem_kv, w_gate, b_gate, w_br_moba, w_br_ret, w_br_mem, w_out, ffn2_norm, ffn2_w1,
              ffn2_w3, ffn2_w2, final_norm):
    B, S, _ = x_prompt.shape
    DB, DS, _ = x_sample.shape
    past_len = page_table.shape[1] * PAGE_SIZE
    pos_p = jnp.arange(S, dtype=jnp.int32)
    pos_s = past_len + jnp.arange(DS, dtype=jnp.int32)
    xp, xs = x_prompt, x_sample
    kp_l, vp_l, mkp_l, mvp_l, sp_l, ks_l, vs_l, ss_l = [], [], [], [], [], [], [], []
    for l in range(DEPTH):
        lw = dict(ffn1_norm=ffn1_norm[l], ffn1_w1=ffn1_w1[l], ffn1_w3=ffn1_w3[l], ffn1_w2=ffn1_w2[l],
                  mix_norm=mix_norm[l], w_in=w_in[l], w_gate=w_gate[l], b_gate=b_gate[l],
                  w_br_moba=w_br_moba[l], w_br_ret=w_br_ret[l], w_br_mem=w_br_mem[l], w_out=w_out[l],
                  ffn2_norm=ffn2_norm[l], ffn2_w1=ffn2_w1[l], ffn2_w3=ffn2_w3[l], ffn2_w2=ffn2_w2[l])
        mk_p, mv_p = mem_kv(mem_prompt, mem_norm[l], w_mem_kv[l])
        s0_p = jnp.zeros((B, R_HEADS, R_DK, R_DV), jnp.float32)
        xp, k_new_p, v_new_p, s_new_p = decoder_layer(xp, pos_p, mk_p, mv_p, None, None, s0_p, t5_table, lw)
        k_past = cache_k[l][page_table].reshape(DB, past_len, A_HEADS, A_DH)
        v_past = cache_v[l][page_table].reshape(DB, past_len, A_HEADS, A_DH)
        xs, k_new_s, v_new_s, s_new_s = decoder_layer(xs, pos_s, cache_mem_k[l], cache_mem_v[l], k_past, v_past,
                                                      state_ret[l], t5_table, lw)
        kp_l.append(k_new_p)
        vp_l.append(v_new_p)
        mkp_l.append(mk_p)
        mvp_l.append(mv_p)
        sp_l.append(s_new_p)
        ks_l.append(k_new_s)
        vs_l.append(v_new_s)
        ss_l.append(s_new_s)
    y_prompt = rmsnorm(xp, final_norm)
    y_sample = rmsnorm(xs, final_norm)
    return (y_prompt, y_sample, jnp.stack(kp_l), jnp.stack(vp_l), jnp.stack(mkp_l), jnp.stack(mvp_l),
            jnp.stack(sp_l), jnp.stack(ks_l), jnp.stack(vs_l), jnp.stack(ss_l))


_drawn_inputs = setup_inputs


def setup_inputs(seed=0):
    import zlib

    import numpy as np

    out = dict(_drawn_inputs(seed))
    spreads = {}
    factors = {'b_gate': 4.43, 'ffn2_norm': 3.003}
    for name, (base, spread) in spreads.items():
        noise = np.random.default_rng([zlib.crc32(name.encode()), seed]).standard_normal(out[name].shape)
        drawn = base * np.exp(spread * noise) if base else spread * noise
        out[name] = jnp.asarray(drawn.astype(out[name].dtype))
    for name, factor in factors.items():
        out[name] = (out[name] * factor).astype(out[name].dtype)
    return out
```

```python
import numpy as np
import concourse.bass as bass
import concourse.mybir as mybir

F32 = mybir.dt.float32
F32R = mybir.dt.float32r
I32 = mybir.dt.int32
ALU = mybir.AluOpType
ACT = mybir.ActivationFunctionType
AX = mybir.AxisListType

P = 128
D_MODEL, SEQ, DEC, PAST, PAGE = 2048, 256, 8, 1024, 128
A_HEADS, A_DH, MOBA_BLOCK, MOBA_TOPK, T5_BUCKETS, T5_MAX_DIST = 8, 128, 256, 3, 32, 128
R_HEADS, R_DK, R_DV, ROPE_BASE = 4, 256, 256, 10000.0
M_HEADS, M_DH, N_MEM = 4, 256, 256
BR_W = 1024
D_FF, EPS, NEG_INF = 5632, 1e-6, -1e30
N = SEQ + DEC
KT = D_MODEL // P
BT = BR_W // P
UK, UC = 8, 256
NPAGES = PAST // PAGE
N_BLOCKS = PAST // MOBA_BLOCK
HID = 16
FFN_BLOCKS = [(0, 16), (16, 16), (32, 12)]

B_MEM = 0
B_FFN1 = B_MEM + 2
FFN_BODIES = sum(n // 4 + 2 for _, n in FFN_BLOCKS)
B_IN = B_FFN1 + FFN_BODIES
B_IN_R, B_IN_A, B_IN_M = B_IN, B_IN + 4, B_IN + 7
B_GATE = B_IN + 8
B_OUT = B_GATE + 12
B_FFN2 = B_OUT + 2
B_END = B_FFN2 + FFN_BODIES
C_QA, C_QR, C_QM = 0, 3 * BR_W, 7 * BR_W

GAMMA = [1.0 - 2.0 ** (-5 - h) for h in range(R_HEADS)]

CONSTS = ["ident", "cos", "sin", "decay", "kdecay", "bucket_prompt", "bucket_decode"]


def t5_bucket(n):
    exact = T5_BUCKETS // 2
    nf = np.maximum(n, 1).astype(np.float32)
    large = exact + (np.log(nf / exact) / np.float32(np.log(T5_MAX_DIST / exact))
                     * (T5_BUCKETS - exact)).astype(np.int32)
    return np.where(n < exact, n, np.minimum(large, T5_BUCKETS - 1))


def constants():
    half = R_DK // 2
    inv = (1.0 / (np.float32(ROPE_BASE) ** np.linspace(0.0, 1.0, half, dtype=np.float32))).astype(np.float32)
    pos = np.concatenate([np.arange(SEQ), np.full(DEC, PAST)]).astype(np.float32)
    ang = (inv[:, None] * pos[None, :]).astype(np.float32)
    log_g = np.log(np.array(GAMMA))
    i = np.arange(SEQ)
    diff = i[None, :] - i[:, None]
    decay = np.where(diff[None] >= 0, np.exp(np.maximum(diff, 0)[None] * log_g[:, None, None]), 0.0)
    decay = decay.reshape(R_HEADS, 2, P, SEQ).transpose(2, 0, 1, 3)
    decay = np.concatenate([decay[:, :, 0], decay[:, :, 1, P:]], axis=2)
    kdecay = np.exp((SEQ - 1 - i)[None, :] * log_g[:, None]).reshape(R_HEADS, 2, P).transpose(2, 0, 1)
    eye = np.eye(T5_BUCKETS, dtype=np.float32)
    return {
        "ident": np.eye(P, dtype=np.float32),
        "cos": np.cos(ang).astype(np.float32),
        "sin": np.sin(ang).astype(np.float32),
        "decay": np.ascontiguousarray(decay).astype(np.float32),
        "kdecay": np.ascontiguousarray(kdecay).astype(np.float32),
        "bucket_prompt": np.ascontiguousarray(eye[:, t5_bucket(SEQ - 1 - np.arange(SEQ))]),
        "bucket_decode": np.ascontiguousarray(eye[:, t5_bucket(PAST - np.arange(PAST))]),
    }


def build(nc, d, o, sem, PS, block):

    base = -(-nc.sbuf_base // 64) * 64

    def at(name, shape, offset, dt=F32):
        return nc.alloc_sbuf_tensor_at(name, [P, *shape], dt, offset=base + offset)

    ROWT = N * 4
    A_X = 0
    A_H = A_X + KT * ROWT
    A_HID = A_H + 2 * KT * ROWT
    A_RAW = A_HID + 2 * HID * ROWT
    A_SPLIT = A_RAW + 4 * UK * UC * 4
    A_EV = A_SPLIT + 4 * UK * UC * 4
    A_SMALL = A_EV + 8 * ROWT
    A_MID = A_SMALL + 1856

    xT = at("xT", [KT, N], A_X)
    hH = at("hH", [KT, N], A_H, F32R)
    hL = at("hL", [KT, N], A_H + KT * ROWT, F32R)
    hidH = at("hidH", [HID, N], A_HID, F32R)
    hidL = at("hidL", [HID, N], A_HID + HID * ROWT, F32R)
    raw = at("raw", [4, UK, UC], A_RAW)
    splitH = at("splitH", [2, UK, UC], A_SPLIT, F32R)
    splitL = at("splitL", [2, UK, UC], A_SPLIT + 2 * UK * UC * 4, F32R)
    EV = at("EV", [8, N], A_EV)
    off = A_SMALL

    def small(name, shape, dt=F32):
        nonlocal off
        t = at(name, shape, off, dt)
        off += -(-int(np.prod(shape)) * 4 // 32) * 32
        assert off <= A_MID
        return t

    ident = small("ident_s", [P])
    ones = small("ones", [P])
    gT = small("gT", [P])
    ptab = small("ptab", [DEC * NPAGES], I32)
    bias0 = small("bias0", [A_HEADS])
    TAIL = A_MID + 48128
    rs = at("rs", [N], TAIL)
    rt = at("rt", [N], TAIL + ROWT)
    ry = at("ry", [N], TAIL + 2 * ROWT)
    MX = small("MX", [2, 2, 2])
    G_FFN1, G_MIX, G_MEM, G_FFN2, G_FINAL, G_BIAS = 0, 16, 32, 48, 64, 80

    xtok = at("xtok", [2, D_MODEL], A_MID)
    mtok = at("mtok", [2, D_MODEL], A_MID + 16384)
    stok = at("stok", [D_MODEL], A_MID + 32768)
    memT = at("memT", [KT, N_MEM], A_HID)
    grow = at("grow", [P], A_EV)
    mkT0 = at("mkT0", [BT, N_MEM], A_MID)
    mvT0 = at("mvT0", [BT, N_MEM], A_MID + 8192)
    mkTok = at("mkTok", [2, BR_W], A_MID + 16384)
    mvTok0 = at("mvTok0", [2, BR_W], A_MID + 24576)
    T8 = BT * ROWT
    HB = A_HID + 2 * BT * ROWT
    orH = at("orH", [BT, N], A_HID, F32R)
    orL = at("orL", [BT, N], A_HID + T8, F32R)
    qrT = at("qrT", [BT, N], A_MID)
    krT = at("krT", [BT, N], A_MID + T8)
    grT = at("grT", [BT, N], A_MID + 2 * T8)
    vrT = at("vrT", [BT, N], A_MID + 3 * T8)
    vrTok = at("vrTok", [2, BR_W], A_MID + 4 * T8)
    decay = at("decay_s", [R_HEADS, SEQ + P], A_MID + 4 * T8 + 8192)
    cosT = at("cosT", [N], HB)
    sinT = at("sinT", [N], HB + ROWT)
    kdecay = at("kdecay_s", [R_HEADS, 2], HB + 2 * ROWT)
    vrS = at("vrS", [BR_W], HB + 2 * ROWT + 64)
    st = at("st", [2, 2, R_DV], HB + 2 * ROWT + 64)
    krTok = at("krTok", [2, BR_W], HB + 2 * ROWT + 64 + 4096)
    vB = at("vB", [2, BR_W], HB + 2 * ROWT + 64 + 4096)
    orS = at("orS", [BT, DEC], HB + 2 * ROWT + 64 + 4096 + 8192)
    orS2 = at("orS2", [BT, DEC], HB + 2 * ROWT + 64 + 4096 + 8192 + 256)
    state = [at("state0", [R_HEADS, 2, R_DV], A_MID + 3 * T8),
             at("state1", [R_HEADS, 2, R_DV], A_MID + 4 * T8 + 8192)]
    sqb = at("sqb", [2, 2, SEQ], A_EV)
    attb = at("attb", [2, 2, SEQ], A_EV + 4096)
    oaH = at("oaH", [BT, N], HB, F32R)
    oaL = at("oaL", [BT, N], HB + T8, F32R)
    qaT = at("qaT", [BT, N], A_MID)
    kaT = at("kaT", [BT, N], A_MID + T8)
    vaT = at("vaT", [BT, N], A_MID + 2 * T8)
    vaTok = at("vaTok", [2, BR_W], A_MID + 3 * T8)
    rows = at("rows", [3, BR_W], A_MID + 3 * T8 + 8192)
    kaTok = at("kaTok", [2, BR_W], A_EV)
    bias = at("bias", [2, 2, SEQ], A_MID + 3 * T8 + 8192 + 12288)
    AD = A_MID + 16384
    kvA = at("kvA", [4, BR_W], A_MID)
    qBA = at("qBA", [2, BR_W], AD)
    SMALL_D = A_MID + 3 * T8 + 8192 + 12288
    vaS = at("vaS", [BT, DEC], SMALL_D + 4096)
    own = at("own", [BT, DEC], SMALL_D + 4352)
    biasD = at("biasD", [NPAGES, A_HEADS], SMALL_D + 4608)
    DEC_A = A_MID + 3 * T8
    omH = at("omH", [BT, N], A_MID + 2 * KT * ROWT, F32R)
    omL = at("omL", [BT, N], A_MID + 2 * KT * ROWT + T8, F32R)
    qmT = at("qmT", [BT, N], A_MID)
    mkT = at("mkT", [BT, N_MEM], A_MID + T8)
    mvTok = at("mvTok", [2, BR_W], A_MID + T8 + 8192)
    qmS = at("qmS", [BR_W], A_MID + T8 + 16384)
    kvM = at("kvM", [4, BR_W], A_MID + T8)
    qBM = at("qBM", [2, BR_W], A_MID)
    mgH = at("mgH", [KT, N], A_MID, F32R)
    mgL = at("mgL", [KT, N], A_MID + KT * ROWT, F32R)
    assert A_MID + 3 * KT * ROWT <= nc.sbuf_usable_end - base
    t5w = at("t5w", [A_HEADS], A_EV)
    bkp = at("bkp", [SEQ], A_EV + 64)
    bkd = at("bkd", [PAST], A_EV + 1088)
    t5row = at("t5row", [2 * SEQ], A_EV + 5184)

    def dec_tiles(kind, where, pages, heads):
        w = DEC * pages * heads * 4
        t = {n: at(f"{kind}_{n}", [DEC, pages, heads], where + k * w) for k, n in enumerate(("S", "L"))}
        g = where + 2 * w
        for k, n in enumerate(("mp", "mx", "se", "rd", "om", "eo", "t", "x1")):
            t[n] = at(f"{kind}_{n}", [DEC, heads], g + k * DEC * heads * 4)
        g += 8 * DEC * heads * 4
        t["oS"] = at(f"{kind}_oS", [BT, DEC], g)
        t["o2"] = at(f"{kind}_o2", [BT, DEC], g + 256)
        if kind == "A":
            t["gate"] = at("A_gate", [DEC, N_BLOCKS, heads], g + 512)
            t["excl"] = at("A_excl", [DEC, N_BLOCKS, heads], g + 1536)
            t["cmp"] = at("A_cmp", [DEC, heads], g + 2560)
        return t

    DA = dec_tiles("A", DEC_A, NPAGES, A_HEADS)
    DM = dec_tiles("M", A_EV, 2, M_HEADS)

    scratch = {n: nc.dram_tensor(f"scratch_{n}", list(s), F32, kind="Internal").ap() for n, s in {
        "t5": (A_HEADS, P, 2 * SEQ), "qa": (DEC, BR_W), "vr": (DEC, BR_W), "qm": (DEC, BR_W),
        "mkT": (P, BT * N_MEM), "mv": (N_MEM, BR_W)}.items()}

    raw_full = [sem(f"raw_full{u}") for u in range(4)]
    hi_ready, split_ready, unit_used = sem("hi_ready"), sem("split_ready"), sem("unit_used")
    set_free = [sem(f"set_free{c}") for c in range(2)]
    silu_ready, prod_ready, hid_hi = sem("silu_ready"), sem("prod_ready"), sem("hid_hi")
    sig_ready, merge_step = sem("sig_ready"), sem("merge_step")
    rot_step = sem("rot_step")
    sq_ready, sq_used, ms_ready, sqrt_ready, norm_rows, norm_hi, norm_done = map(sem, (
        "sq_ready", "sq_used", "ms_ready", "sqrt_ready", "norm_rows", "norm_hi", "norm_done"))
    dve_link = sem("dve_link")
    ms_in = sem("ms_in")
    act_link = sem("act_link")
    x_in, mem_in, gain_in, ident_in, rot_in, decay_in, t5_in, pt_in = map(sem, (
        "x_in", "mem_in", "gain_in", "ident_in", "rot_in", "decay_in", "t5_in", "pt_in"))
    ones_set, mk_in = sem("ones_set"), sem("mk_in")
    stored = sem("stored")
    kept = sem("kept")
    turned, turn_out = sem("turned"), sem("turn_out")
    att_ps, att_sb, o_ps, o_sq, ms_ps, ms_ev, r_done, kd_ready, s_ps, s_out = map(sem, (
        "att_ps", "att_sb", "o_ps", "o_sq", "ms_ps", "ms_ev", "r_done", "kd_ready", "s_ps", "s_out"))
    r_hi, r_var, r_sqrt, r_res = sem("r_hi"), sem("r_var"), sem("r_sqrt"), sem("r_res")
    st_sent = [sem(f"st_sent{p}") for p in range(2)]
    s_in = [sem(f"s_in{p}") for p in range(2)]
    vb_in = [sem(f"vb_in{p}") for p in range(2)]
    s_scaled, s_new, s_read, s_back, os_out = sem("s_scaled"), sem("s_new"), sem("s_read"), [
        sem(f"s_back{p}") for p in range(2)], sem("os_out")
    a_s, a_p, a_max, a_exp, a_norm, a_pt, a_ptc, a_o, a_hi, a_lo = map(sem, (
        "a_s", "a_p", "a_max", "a_exp", "a_norm", "a_pt", "a_ptc", "a_o", "a_hi", "a_lo"))
    bias_in = [sem(f"bias_in{p}") for p in range(2)]
    t5_ps, t5_ready = sem("t5_ps"), sem("t5_ready")
    kv_full = [sem(f"kv_full{s}") for s in range(4)]
    kv_used = [sem(f"kv_used{s}") for s in range(4)]
    qb_in = [sem(f"qb_in{s}") for s in range(2)]
    kq_ready = sem("kq_ready")
    gate_ps, sum_ps, d_sb, d_exp, d_max, d_maxall, d_logit = map(sem, (
        "gate_ps", "sum_ps", "d_sb", "d_exp", "d_max", "d_maxall", "d_logit"))
    own_ready, r_all_done, samp_sq, samp_ms, samp_var, samp_sqrt, m_done, a_done = map(sem, (
        "own_ready", "r_all_done", "samp_sq", "samp_ms", "samp_var", "samp_sqrt", "m_done", "a_done"))
    d_prob, d_o, d_os = sem("d_prob"), sem("d_o"), sem("d_os")
    y_sent = sem("y_sent")

    turns = []

    def turn(name, srcs, rows, width, dest):
        turns.append((name, srcs, rows, width, dest))

    turn("gain", [(grow[:, :], 0)], P, P, gT[:, :].rearrange("p (a c) -> p a c", a=1))
    for tt in range(2):
        for g in range(4):
            turn("mem", [(mtok[:, tt, (4 * g + k) * P:(4 * g + k + 1) * P], k) for k in range(4)], P, P,
                 memT[:, 4 * g:4 * g + 4, tt * P:(tt + 1) * P])
    for tt in range(2):
        for g in range(4):
            turn("x", [(xtok[:, tt, (4 * g + k) * P:(4 * g + k + 1) * P], k) for k in range(4)], P, P,
                 xT[:, 4 * g:4 * g + 4, tt * P:(tt + 1) * P])
    turn("x", [(stok[0:DEC, k * P:(k + 1) * P], k) for k in range(KT)], P, DEC, xT[:, :, SEQ:N])

    def turn_tokens(name, src, dest):
        for tt in range(2):
            for g in range(2):
                turn(name, [(src[:, 4 * g + k, tt * P:(tt + 1) * P], k) for k in range(4)], P, P,
                     dest[:, tt, g * 512:(g + 1) * 512].rearrange("p (a c) -> p a c", a=4))

    def turn_samples(name, src, dest):
        for g in range(2):
            turn(name, [(src[:, 4 * g + k, SEQ:N], k) for k in range(4)], DEC, P,
                 dest[g * 512:(g + 1) * 512])

    turn_tokens("mem_kv", mkT0, mkTok)
    turn_tokens("mem_kv", mvT0, mvTok0)
    turn_tokens("r", vrT, vrTok)
    turn_tokens("r", krT, krTok)

    class RowDest:
        def __init__(self, t, *ix):
            self.t, self.ix = t, ix

        def __getitem__(self, cols):
            return self.t[(slice(0, DEC), *self.ix, cols)].rearrange("p (a c) -> p a c", a=4)

    turn_samples("r", vrT, RowDest(vrS))
    turn_tokens("a", vaT, vaTok)
    turn_tokens("a", kaT, kaTok)
    turn_samples("a", kaT, RowDest(rows, 0))
    turn_samples("a", vaT, RowDest(rows, 1))
    turn_samples("a", qaT, RowDest(rows, 2))
    turn_samples("m", qmT, RowDest(qmS))
    ytok = at("ytok", [2, D_MODEL], A_MID)
    ystok = at("ystok", [D_MODEL], A_MID + 16384)
    yT = at("yT", [KT, N], A_HID)
    for tt in range(2):
        for g in range(4):
            turn("y", [(yT[:, 4 * g + k, tt * P:(tt + 1) * P], k) for k in range(4)], P, P,
                 ytok[:, tt, g * 512:(g + 1) * 512].rearrange("p (a c) -> p a c", a=4))
    for g in range(4):
        turn("y", [(yT[:, 4 * g + k, SEQ:N], k) for k in range(4)], DEC, P,
             ystok[0:DEC, g * 512:(g + 1) * 512].rearrange("p (a c) -> p a c", a=4))

    def turns_of(name):
        return [(q, t) for q, t in enumerate(turns) if t[0] == name]

    def turns_until(name):
        return turns_of(name)[-1][0] + 1

    def pe_turns(pe, name):
        for q, (_, srcs, rows_out, width, _) in turns_of(name):
            if q >= 2:
                pe.wait_ge(turn_out, q - 1)
            for src, block in srcs:
                n = src.shape[0]
                last = nc.tensor.transpose(PS[0:rows_out, q % 2, block * width:(block + 1) * width],
                                           src, ident[0:n, 0:n])
            last.then_inc(turned, 1)

    def act_turns(act, name):
        for q, (_, srcs, rows_out, width, dest) in turns_of(name):
            act.wait_ge(turned, q + 1)
            nc.scalar.activation(dest, PS[0:rows_out, q % 2, 0:len(srcs) * width].rearrange(
                "p (a c) -> p a c", a=len(srcs)), ACT.Copy).then_inc(turn_out, 1)

    def wait_count(eng, s, n):
        if not (isinstance(n, int) and n <= 0):
            eng.wait_ge(s, n)

    def first_apart(eng, n, body):
        body(0)
        with eng.Fori(1, n) as i:
            body(i)

    def sp_unit(sp, B, c, u, src):
        if not (isinstance(B, int) and B == 0 and c == 0):
            sp.wait_ge(split_ready, 8 * B + 4 * c + u - 3)
        nk = src.shape[0] // P
        sp.dma_start(raw[:, u, 0:nk, :], src.rearrange("(k p) c -> p k c", p=P)).then_inc(raw_full[u], 16)

    def sp_wide(sp, B, W, col):
        for c in range(2):
            for u in range(4):
                sp_unit(sp, B, c, u, W[(u % 2) * UK * P:(u % 2 + 1) * UK * P,
                                       bass.ds(col + 512 * c + UC * (u // 2), UC)])

    def sp_ffn(sp, B0, w1, w3, w2):
        B = B0
        for t0, n in FFN_BLOCKS:
            with sp.Fori(0, n // 4) as i:
                for c in range(2):
                    for u in range(4):
                        W = w1 if u < 2 else w3
                        sp_unit(sp, i + B, c, u, W[(u % 2) * UK * P:(u % 2 + 1) * UK * P,
                                                   bass.ds(i * 512 + (t0 * P + UC * c), UC)])
            B += n // 4
            nk = n // 2
            with sp.Fori(0, 2) as i:
                for c in range(2):
                    for u in range(4):
                        k0 = t0 + (u % 2) * nk
                        sp_unit(sp, i + B, c, u, w2[k0 * P:(k0 + nk) * P,
                                                    bass.ds(i * 1024 + (512 * c + UC * (u // 2)), UC)])
            B += 2

    def sp_gates(sp):
        with sp.Fori(0, 4) as i:
            for s in range(6):
                b, c, br = s // 2, s % 2, s % 3
                col = i * 512 + UC * (s // 3)
                for u in range(4):
                    if u < 2:
                        src = d["w_gate"][u * UK * P:(u + 1) * UK * P, bass.ds(col + br * D_MODEL, UC)]
                    else:
                        src = d[("w_br_moba", "w_br_ret", "w_br_mem")[br]][
                            (u - 2) * 4 * P:(u - 1) * 4 * P, bass.ds(col, UC)]
                    sp_unit(sp, i * 3 + (B_GATE + b), c, u, src)

    def act_split(act, B, c, u, nk=UK):
        act.wait_ge(raw_full[u], 32 * B + 16 * (c + 1))
        if not (isinstance(B, int) and B == 0 and c == 0 and u < 2):
            act.wait_ge(unit_used, 8 * B + 4 * c + u - 1)
        nc.scalar.activation(splitH[:, u % 2, 0:nk, :], raw[:, u, 0:nk, :], ACT.Copy).then_inc(hi_ready, 1)

    def dve_split(dve, B, c, u, nk=UK):
        dve.wait_ge(hi_ready, 8 * B + 4 * c + u + 1)
        nc.vector.tensor_tensor(splitL[:, u % 2, 0:nk, :], raw[:, u, 0:nk, :],
                                splitH[:, u % 2, 0:nk, :].bitcast(F32), ALU.subtract).then_inc(split_ready, 1)

    def split_body(split, eng, B, evac, nks=(8, 8, 8, 8), last=False):
        for c in range(2):
            split(eng, B, c, 2, nks[2])
            split(eng, B, c, 3, nks[3])
            if not (last and c == 1):
                nB, n_c = (B, 1) if c == 0 else (B + 1, 0)
                split(eng, nB, n_c, 0)
                split(eng, nB, n_c, 1)
            evac(B, c)

    def pe_unit(pe, B, c, u, rhs, tiles, n, start, stop):
        H, L = rhs
        pe.wait_ge(split_ready, 8 * B + 4 * c + u + 1)
        for m in range(2):
            out = PS[:, 4 * c + 2 * (u // 2) + m, 0:n]
            for j, k in enumerate(tiles):
                w_hi = splitH[:, u % 2, j, m * P:(m + 1) * P]
                w_lo = splitL[:, u % 2, j, m * P:(m + 1) * P]
                first, final = start and j == 0, stop and j == len(tiles) - 1
                nc.tensor.matmul(out, w_hi, H[:, k, 0:n], start=first, stop=False)
                nc.tensor.matmul(out, w_hi, L[:, k, 0:n], start=False, stop=False)
                last = nc.tensor.matmul(out, w_lo, H[:, k, 0:n], start=False, stop=final)
        last.then_inc(unit_used, 1)

    def pe_step_free(pe, B, c):
        wait_count(pe, set_free[c], B)

    def pe_drained(pe, B):
        pe.wait_ge(set_free[0], B)
        pe.wait_ge(set_free[1], B)

    def pe_wide(pe, B, rhs, n=N, nk=UK):
        for c in range(2):
            pe_step_free(pe, B, c)
            for u in range(4):
                pe_unit(pe, B, c, u, rhs, range((u % 2) * nk, (u % 2 + 1) * nk), n, u % 2 == 0, u % 2 == 1)

    def pe_ffn(pe, B0):
        B = B0
        for _, n in FFN_BLOCKS:
            pe_drained(pe, B)
            with pe.Fori(0, n // 4) as i:
                pe_wide(pe, i + B, (hH, hL))
            B += n // 4
            pe_drained(pe, B)
            with pe.Fori(0, 2) as i:
                pe_wide(pe, i + B, (hidH, hidL), nk=n // 2)
            B += 2

    def pe_gates(pe):
        with pe.Fori(0, 4) as i:
            for s in range(6):
                B, c = i * 3 + (B_GATE + s // 2), s % 2
                pe_step_free(pe, B, c)
                o_br = ((oaH, oaL), (orH, orL), (omH, omL))[s % 3]
                for u in range(4):
                    if u < 2:
                        pe_unit(pe, B, c, u, (hH, hL), range(u * UK, (u + 1) * UK), N, u == 0, u == 1)
                    else:
                        pe_unit(pe, B, c, u, o_br, range((u - 2) * 4, (u - 1) * 4), N, u == 2, u == 3)

    def step_made(eng, B, c):
        eng.wait_ge(unit_used, 8 * B + 4 * c + 4)

    def ffn_evac_act(act, up0, B0, i):
        def evac(B, c):
            step_made(act, B, c)
            nc.scalar.activation(EV[:, 2 * c:2 * c + 2, :], PS[:, 4 * c:4 * c + 2, 0:N],
                                 ACT.Silu).then_inc(silu_ready, 1)
        return evac

    def ffn_up_evac_dve(dve, up0, i):
        def evac(B, c):
            n = i * 2 + (up0 + c + 1)
            dve.wait_ge(silu_ready, n)
            prod = EV[:, 4 + 2 * c:6 + 2 * c, :]
            nc.vector.tensor_tensor(prod, EV[:, 2 * c:2 * c + 2, :], PS[:, 4 * c + 2:4 * c + 4, 0:N],
                                    ALU.mult).then_inc(prod_ready, 1)
            hi = hidH[:, bass.ds(i * 4 + 2 * c, 2), :]
            dve.wait_ge(prod_ready, n)
            nc.vector.tensor_copy(hi, prod).then_inc(hid_hi, 1)
            dve.wait_ge(hid_hi, n)
            nc.vector.tensor_tensor(hidL[:, bass.ds(i * 4 + 2 * c, 2), :], prod, hi.bitcast(F32),
                                    ALU.subtract).then_inc(set_free[c], 1)
        return evac

    def add_evac_dve(dve, i, scale):
        def evac(B, c):
            step_made(dve, B, c)
            x4 = xT[:, bass.ds(i * 8 + 4 * c, 4), :]
            nc.vector.scalar_tensor_tensor(x4, PS[:, 4 * c:4 * c + 4, 0:N], scale, x4,
                                           ALU.mult, ALU.add).then_inc(set_free[c], 1)
        return evac

    def none(B, c):
        pass

    FFN_UPS = 2 * sum(n // 4 for _, n in FFN_BLOCKS)

    def split_ffn(split, eng, B0, which, final):
        B, ups = B0, which * FFN_UPS
        on_act = split is act_split
        for blk, (_, n) in enumerate(FFN_BLOCKS):
            with eng.Fori(0, n // 4) as i:
                ev = ffn_evac_act(eng, ups, B, i) if on_act else ffn_up_evac_dve(eng, ups, i)
                split_body(split, eng, i + B, ev)
            B += n // 4
            ups += n // 2
            last = final and blk == len(FFN_BLOCKS) - 1
            with eng.Fori(0, 1 if last else 2) as i:
                split_body(split, eng, i + B, none if on_act else add_evac_dve(eng, i, 0.5))
            if last:
                split_body(split, eng, B + 1, none if on_act else add_evac_dve(eng, 1, 0.5), last=True)
            B += 2

    NORMS = {"mem": 0, "ffn1": 1, "mix": 2, "ffn2": 3, "final": 4}

    def norm_args(name):
        return {"mem": (memT, N_MEM, G_MEM), "ffn1": (xT, N, G_FFN1), "mix": (xT, N, G_MIX),
                "ffn2": (xT, N, G_FFN2), "final": (xT, N, G_FINAL)}[name]

    def act_norm(act, name):
        src, n, _ = norm_args(name)
        q = NORMS[name]
        for r in range(4):
            if 4 * q + r >= 2:
                act.wait_ge(sq_used, 4 * q + r - 1)
            nc.scalar.activation(EV[:, 4 * (r % 2):4 * (r % 2) + 4, 0:n], src[:, 4 * r:4 * r + 4, 0:n],
                                 ACT.Square).then_inc(sq_ready, 1)
        act.wait_ge(ms_ready, q + 1)
        nc.scalar.activation(rt[:, 0:n], rs[:, 0:n], ACT.Sqrt).then_inc(sqrt_ready, 1)

    def pe_norm(pe, name):
        _, n, _ = norm_args(name)
        q = NORMS[name]
        for r in range(4):
            pe.wait_ge(sq_ready, 4 * q + r + 1)
            for k in range(4):
                last = nc.tensor.matmul(PS[:, 7, 0:n], ones[:, :], EV[:, 4 * (r % 2) + k, 0:n],
                                        start=r == 0 and k == 0, stop=r == 3 and k == 3)
            last.then_inc(sq_used, 1)

    def refine(link, y, m, t):
        link(nc.vector.tensor_tensor(t, y, y, ALU.mult))
        link(nc.vector.scalar_tensor_tensor(t, t, -0.5, m, ALU.mult, ALU.mult))
        link(nc.vector.scalar_tensor_tensor(y, t, 1.5, y, ALU.add, ALU.mult))

    def dve_norm(dve, link, name, out=None):
        src, n, g = norm_args(name)
        q = NORMS[name]
        dve.wait_ge(sq_used, 4 * q + 4)
        nc.vector.tensor_scalar(rs[:, 0:n], PS[:, 7, 0:n], 1.0 / D_MODEL, EPS, ALU.mult,
                                ALU.add).then_inc(ms_ready, 1)
        dve.wait_ge(sqrt_ready, q + 1)
        link(nc.vector.reciprocal(ry[:, 0:n], rt[:, 0:n]))
        refine(link, ry[:, 0:n], rs[:, 0:n], rt[:, 0:n])
        for r in range(4):
            half = EV[:, 4 * (r % 2):4 * (r % 2) + 4, 0:n] if out is None else out[:, 4 * r:4 * r + 4, 0:n]
            for k in range(4):
                last = nc.vector.scalar_tensor_tensor(half[:, k, :], src[:, 4 * r + k, 0:n],
                                                      gT[:, g + 4 * r + k:g + 4 * r + k + 1],
                                                      ry[:, 0:n], ALU.mult, ALU.mult)
            if out is None:
                link(last)
                hi = hH[:, 4 * r:4 * r + 4, 0:n]
                link(nc.vector.tensor_copy(hi, half))
                last = nc.vector.tensor_tensor(hL[:, 4 * r:4 * r + 4, 0:n], half, hi.bitcast(F32), ALU.subtract)
                if r < 3:
                    link(last)
        last.then_inc(norm_done, 1)

    def pe_retention(pe):
        def att(h):
            if h >= 2:
                pe.wait_ge(att_sb, h - 1)
            for jt in range(2):
                for dt in range(2):
                    last = nc.tensor.matmul(PS[:, 2 + h % 2, jt * SEQ + jt * P:(jt + 1) * SEQ],
                                            krT[:, 2 * h + dt, jt * P:(jt + 1) * P],
                                            qrT[:, 2 * h + dt, jt * P:SEQ], start=dt == 0, stop=dt == 1)
            last.then_inc(att_ps, 1)

        att(0)
        for h in range(R_HEADS):
            if h + 1 < R_HEADS:
                att(h + 1)
            pe.wait_ge(att_sb, h + 1)
            for et in range(2):
                v = lambda jt: vrTok[:, jt, h * R_DV + et * P:h * R_DV + (et + 1) * P]
                nc.tensor.matmul(PS[:, 4, et * SEQ:(et + 1) * SEQ], v(0), attb[:, h % 2, 0, :],
                                 start=True, stop=False)
                last = nc.tensor.matmul(PS[:, 4, et * SEQ + P:(et + 1) * SEQ], v(1), attb[:, h % 2, 1, P:SEQ],
                                        start=False, stop=True)
            last.then_inc(o_ps, 1)
            pe.wait_ge(kd_ready, h + 1)
            if h >= 1:
                pe.wait_ge(s_out, h)
            for dt in range(2):
                for jt in range(2):
                    c0 = h * R_DK + dt * P
                    last = nc.tensor.matmul(PS[:, 6, dt * R_DV:(dt + 1) * R_DV], krTok[:, jt, c0:c0 + P],
                                            vrTok[:, jt, h * R_DV:(h + 1) * R_DV], start=jt == 0, stop=jt == 1)
            last.then_inc(s_ps, 1)
            pe.wait_ge(o_sq, h + 1)
            for et in range(2):
                last = nc.tensor.matmul(PS[:, 5, 0:SEQ], ones[:, :], sqb[:, h % 2, et, :],
                                        start=et == 0, stop=et == 1)
            last.then_inc(ms_ps, 1)
            pe.wait_ge(r_done, h + 1)

    def act_retention(act):
        for h in range(R_HEADS):
            act.wait_ge(o_ps, h + 1)
            nc.scalar.activation(sqb[:, h % 2, :, :], PS[:, 4, :].rearrange("p (a c) -> p a c", a=2),
                                 ACT.Square).then_inc(o_sq, 1)
            act.wait_ge(s_ps, h + 1)
            if h >= 2:
                act.wait_ge(st_sent[h % 2], 16 * (h // 2))
            nc.scalar.activation(st[:, h % 2, :, :], PS[:, 6, :].rearrange("p (a c) -> p a c", a=2),
                                 ACT.Copy).then_inc(s_out, 1)
            act.wait_ge(r_var, h + 1)
            nc.scalar.activation(rt[:, 0:SEQ], rs[:, 0:SEQ], ACT.Sqrt).then_inc(r_sqrt, 1)

    def dve_retention(dve, link):
        def att(h):
            dve.wait_ge(att_ps, h + 1)
            nc.vector.tensor_tensor(attb[:, h % 2, 0, :], PS[:, 2 + h % 2, 0:SEQ], decay[:, h, 0:SEQ], ALU.mult)
            nc.vector.tensor_tensor(attb[:, h % 2, 1, P:SEQ], PS[:, 2 + h % 2, SEQ + P:2 * SEQ],
                                    decay[:, h, SEQ:SEQ + P], ALU.mult).then_inc(att_sb, 1)

        att(0)
        for h in range(R_HEADS):
            for jt in range(2):
                kk = krTok[:, jt, h * R_DK:(h + 1) * R_DK]
                last = nc.vector.tensor_scalar(kk, kk, kdecay[:, h, jt:jt + 1], None, ALU.mult)
            last.then_inc(kd_ready, 1)
            if h + 1 < R_HEADS:
                if h >= 1:
                    dve.wait_ge(o_ps, h)
                att(h + 1)
            dve.wait_ge(ms_ps, h + 1)
            nc.vector.tensor_scalar(rs[:, 0:SEQ], PS[:, 5, 0:SEQ], 1.0 / R_DV, EPS, ALU.mult,
                                    ALU.add).then_inc(r_var, 1)
            dve.wait_ge(r_sqrt, h + 1)
            y = ry[:, 0:SEQ]
            link(nc.vector.reciprocal(y, rt[:, 0:SEQ]))
            refine(link, y, rs[:, 0:SEQ], rt[:, 0:SEQ])
            for et in range(2):
                t = sqb[:, h % 2, et, :]
                link(nc.vector.tensor_tensor(t, PS[:, 4, et * SEQ:(et + 1) * SEQ], y, ALU.mult))
                link(nc.vector.tensor_tensor(t, t, grT[:, 2 * h + et, 0:SEQ], ALU.mult))
                link(nc.vector.tensor_copy(orH[:, 2 * h + et, 0:SEQ], t))
                last = nc.vector.tensor_tensor(orL[:, 2 * h + et, 0:SEQ], t,
                                               orH[:, 2 * h + et, 0:SEQ].bitcast(F32), ALU.subtract)
            last.then_inc(r_done, 1)

    def pool_states(pool):
        def body(i):
            for p in range(2):
                b = i * 2 + p
                wait_count(pool, s_back[p], i * 16)
                wait_count(pool, s_read, i * 2)
                pool.dma_start(state[p][:, :, :, :], d["state_ret"][bass.ds(b, 1), :, :, :].rearrange(
                    "a h (t p) e -> p (a h) t e", p=P)).then_inc(s_in[p], 16)
                pool.dma_start(vB[:, p, :], scratch["vr"][bass.ds(b, 1), :].to_broadcast([P, BR_W])
                               ).then_inc(vb_in[p], 16)

        first_apart(pool, DEC // 2, body)

    def act_states(act):
        with act.Fori(0, DEC // 2) as i:
            for p in range(2):
                act.wait_ge(s_in[p], i * 16 + 16)
                for h in range(R_HEADS):
                    last = nc.scalar.activation(state[p][:, h, :, :], state[p][:, h, :, :], ACT.Copy,
                                                scale=GAMMA[h])
                last.then_inc(s_scaled, 1)
            for p in range(2):
                act.wait_ge(s_new, i * 2 + (p + 1))
                act.dma_start(o["ret_state_sample"][bass.ds(i * 2 + p, 1), :, :, :].rearrange(
                    "a h (t p) e -> p (a h) t e", p=P), state[p][:, :, :, :]).then_inc(s_back[p], 16)

    def dve_states(dve):
        with dve.Fori(0, DEC // 2) as i:
            for p in range(2):
                dve.wait_ge(s_scaled, i * 2 + (p + 1))
                dve.wait_ge(vb_in[p], i * 16 + 16)
                for h in range(R_HEADS):
                    for dt in range(2):
                        s = state[p][:, h, dt, :]
                        last = nc.vector.scalar_tensor_tensor(
                            s, vB[:, p, h * R_DV:(h + 1) * R_DV],
                            krT[:, 2 * h + dt, bass.ds(i * 2 + (SEQ + p), 1)], s, ALU.mult, ALU.add)
                last.then_inc(s_new, 1)
            for p in range(2):
                dve.wait_ge(s_read, i * 2 + (p + 1))
                nc.vector.tensor_copy(orS[:, :, bass.ds(i * 2 + p, 1)],
                                      PS[:, p, 0:BT].rearrange("p (a c) -> p a c", c=1)).then_inc(os_out, 1)

    def pe_states(pe):
        def body(i):
            for p in range(2):
                pe.wait_ge(s_new, i * 2 + (p + 1))
                wait_count(pe, os_out, i * 2)
                for h in range(R_HEADS):
                    for et in range(2):
                        for dt in range(2):
                            last = nc.tensor.matmul(
                                PS[:, p, 2 * h + et:2 * h + et + 1], state[p][:, h, dt, et * P:(et + 1) * P],
                                qrT[:, 2 * h + dt, bass.ds(i * 2 + (SEQ + p), 1)],
                                start=dt == 0, stop=dt == 1)
                last.then_inc(s_read, 1)


        first_apart(pe, DEC // 2, body)

    class Kind:
        def __init__(self, name, heads, dt, et, causal, qT, kT, vtok, oH, oL, scale, q0):
            self.name, self.heads, self.dt, self.et, self.causal = name, heads, dt, et, causal
            self.qT, self.kT, self.vtok, self.oH, self.oL, self.scale = qT, kT, vtok, oH, oL, scale
            self.q0 = q0

        def keys(self, it):
            return P * (it + 1) if self.causal else SEQ

    KA = Kind("A", A_HEADS, 1, 1, True, qaT, kaT, vaTok, oaH, oaL, A_DH ** -0.5, 0)
    KM = Kind("M", M_HEADS, 2, 2, False, qmT, mkT, mvTok, omH, omL, M_DH ** -0.5, A_HEADS)

    def pe_attend(pe, K):
        def scores(h):
            q = K.q0 + h
            if q >= 2:
                pe.wait_ge(a_p, q - 1)
            for it in range(2):
                for dt in range(K.dt):
                    last = nc.tensor.matmul(PS[:, q % 2, it * SEQ:it * SEQ + K.keys(it)],
                                            K.qT[:, K.dt * h + dt, it * P:(it + 1) * P],
                                            K.kT[:, K.dt * h + dt, 0:K.keys(it)],
                                            start=dt == 0, stop=dt == K.dt - 1)
            last.then_inc(a_s, 1)

        def rest(h):
            q = K.q0 + h
            pe.wait_ge(a_norm, q + 1)
            if q >= 2:
                pe.wait_ge(a_ptc, q - 1)
            for it in range(2):
                for jt in range(K.keys(it) // P):
                    last = nc.tensor.transpose(PS[:, 2 + q % 2, jt * SEQ + it * P:jt * SEQ + (it + 1) * P],
                                               sqb[:, q % 2, it, jt * P:(jt + 1) * P], ident[:, :])
            last.then_inc(a_pt, 1)
            pe.wait_ge(a_ptc, q + 1)
            if q >= 2:
                pe.wait_ge(a_lo, q - 1)
            for et in range(K.et):
                c0 = (h * K.et + et) * P
                for jt in range(2):
                    i0 = jt * P if K.causal else 0
                    last = nc.tensor.matmul(PS[:, 4 + q % 2, et * SEQ + i0:(et + 1) * SEQ],
                                            K.vtok[:, jt, c0:c0 + P], attb[:, q % 2, jt, i0:SEQ],
                                            start=jt == 0, stop=jt == 1)
            last.then_inc(a_o, 1)

        scores(0)
        for h in range(K.heads):
            if h + 1 < K.heads:
                scores(h + 1)
            rest(h)

    def dve_attend(dve, link, K):
        def soft(h):
            q = K.q0 + h
            dve.wait_ge(a_s, q + 1)
            if q >= 2:
                dve.wait_ge(a_pt, q - 1)
            if K.causal:
                dve.wait_ge(bias_in[h % 2], 32 * (h // 2 + 1))
            for it in range(2):
                n = K.keys(it)
                s, ps = sqb[:, q % 2, it, 0:n], PS[:, q % 2, it * SEQ:it * SEQ + n]
                if K.causal:
                    last = nc.vector.scalar_tensor_tensor(s, ps, K.scale, bias[:, h % 2, it, 0:n],
                                                          ALU.mult, ALU.add)
                else:
                    last = nc.vector.tensor_scalar(s, ps, K.scale, None, ALU.mult)
            last.then_inc(a_p, 1)
            dve.wait_ge(a_p, q + 1)
            if q >= 2:
                dve.wait_ge(a_norm, q - 1)
            for it in range(2):
                last = nc.vector.tensor_reduce(MX[:, q % 2, 0, it:it + 1], sqb[:, q % 2, it, 0:K.keys(it)],
                                               AX.X, ALU.max, negate=True)
            last.then_inc(a_max, 1)

        def norm(h):
            q = K.q0 + h
            dve.wait_ge(a_exp, q + 1)
            link(nc.vector.reciprocal(MX[:, q % 2, 1, :], MX[:, q % 2, 1, :]))
            for it in range(2):
                s = sqb[:, q % 2, it, 0:K.keys(it)]
                last = nc.vector.tensor_scalar(s, s, MX[:, q % 2, 1, it:it + 1], None, ALU.mult)
            last.then_inc(a_norm, 1)

        def lo(h):
            q = K.q0 + h
            dve.wait_ge(a_hi, q + 1)
            t = slice(K.et * h, K.et * (h + 1))
            nc.vector.tensor_tensor(K.oL[:, t, 0:SEQ], PS[:, 4 + q % 2, 0:K.et * SEQ].rearrange(
                "p (a c) -> p a c", a=K.et), K.oH[:, t, 0:SEQ].bitcast(F32), ALU.subtract).then_inc(a_lo, 1)

        soft(0)
        for h in range(K.heads):
            norm(h)
            if h + 1 < K.heads:
                soft(h + 1)
            lo(h)

    def act_attend(act, K):
        def exps(h):
            q = K.q0 + h
            act.wait_ge(a_max, q + 1)
            for it in range(2):
                s = sqb[:, q % 2, it, 0:K.keys(it)]
                last = nc.scalar.activation(s, s, ACT.Exp, bias=MX[:, q % 2, 0, it:it + 1],
                                            accum_out=MX[:, q % 2, 1, it:it + 1])
            last.then_inc(a_exp, 1)

        def turn_copy(h):
            q = K.q0 + h
            act.wait_ge(a_pt, q + 1)
            if q >= 2:
                act.wait_ge(a_o, q - 1)
            if K.causal:
                nc.scalar.activation(attb[:, q % 2, 0, :], PS[:, 2 + q % 2, 0:SEQ], ACT.Copy)
                last = nc.scalar.activation(attb[:, q % 2, 1, P:SEQ], PS[:, 2 + q % 2, SEQ + P:2 * SEQ], ACT.Copy)
            else:
                last = nc.scalar.activation(attb[:, q % 2, :, :], PS[:, 2 + q % 2, :].rearrange(
                    "p (a c) -> p a c", a=2), ACT.Copy)
            last.then_inc(a_ptc, 1)

        def hi(h):
            q = K.q0 + h
            act.wait_ge(a_o, q + 1)
            nc.scalar.activation(K.oH[:, K.et * h:K.et * (h + 1), 0:SEQ], PS[:, 4 + q % 2, 0:K.et * SEQ].rearrange(
                "p (a c) -> p a c", a=K.et), ACT.Copy).then_inc(a_hi, 1)

        exps(0)
        for h in range(K.heads):
            turn_copy(h)
            if h + 1 < K.heads:
                exps(h + 1)
            hi(h)

    class Decode:
        def __init__(self, name, pages, heads, kv, qB, t, qscr, base, scale, oT, oL):
            self.name, self.pages, self.heads, self.kv, self.qB, self.t = name, pages, heads, kv, qB, t
            self.qscr, self.base, self.scale, self.oH, self.oL = qscr, base, scale, oT, oL
            self.dh = BR_W // heads
            self.et = self.dh // P
            self.q = 0 if name == "A" else 1

    DKA = Decode("A", NPAGES, A_HEADS, kvA, qBA, DA, "qa", 0, A_DH ** -0.5, oaH, oaL)
    DKM = Decode("M", 2, M_HEADS, kvM, qBM, DM, "qm", 2 * DEC * NPAGES, M_DH ** -0.5, omH, omL)

    def pool_decode(pool, K, values):
        def body(i):
            for p in range(2):
                b = i * 2 + p
                if not values:
                    wait_count(pool, kq_ready, i * 2 * K.pages + K.q * DEC * NPAGES)
                    pool.dma_start(K.qB[:, p, :], scratch[K.qscr][bass.ds(b, 1), :].to_broadcast([P, BR_W])
                                   ).then_inc(qb_in[p], 16)
                for g in range(K.pages):
                    n = p * K.pages + g
                    at_n = K.base + values * DEC * K.pages + n
                    s = n % 4
                    wait_count(pool, kv_used[s], i * (2 * K.pages // 4) + at_n // 4)
                    if K.name == "A":
                        page = pool.value_load(ptab[0:1, bass.ds(i * 2 * K.pages + n, 1)],
                                               min_val=0, max_val=d["cache_k"].shape[0] - 1)
                        src = d["cache_v" if values else "cache_k"][bass.ds(page, 1), :, :].rearrange(
                            "a p c -> (a p) c")
                    else:
                        src = d["cache_mem_v" if values else "cache_mem_k"][
                            bass.ds(b, 1), g * P:(g + 1) * P, :].rearrange("a p c -> (a p) c")
                    pool.dma_start(K.kv[:, s, :], src).then_inc(kv_full[s], 16)

        first_apart(pool, DEC // 2, body)

    def dve_scores(dve, K):
        with dve.Fori(0, DEC // 2) as i:
            for p in range(2):
                dve.wait_ge(qb_in[p], i * 16 + 64 * K.q + 16)
                for g in range(K.pages):
                    n = p * K.pages + g
                    s = n % 4
                    dve.wait_ge(kv_full[s], i * (16 * (2 * K.pages // 4)) + 16 * ((K.base + n) // 4 + 1))
                    last = nc.vector.tensor_tensor(K.kv[:, s, :], K.kv[:, s, :], K.qB[:, p, :], ALU.mult)
                    last.then_inc(kq_ready, 1)
                    dve.wait_ge(kq_ready, i * 2 * K.pages + (K.q * DEC * NPAGES + n + 1))
                    nc.vector.tensor_reduce(
                        K.t["S"][:, bass.ds(i * 2 + p, 1), g, :].rearrange("p a h -> p (a h)"),
                        K.kv[:, s, :].rearrange("p (h c) -> p h c", h=K.heads), AX.X, ALU.add
                    ).then_inc(kv_used[s], 1)

    def dve_softmax(dve, link, K):
        t = K.t
        w = DEC * K.heads
        S, L = t["S"], t["L"]
        by = lambda x: x[:, :, :].unsqueeze(2).to_broadcast([P, DEC, K.pages, K.heads])
        if K.name == "A":
            dve.wait_ge(gate_ps, 1)
            g2 = PS[:, 0, 0:DEC * NPAGES * A_HEADS].rearrange("p (b n two h) -> p b n two h", b=DEC, two=2, h=A_HEADS)
            for n in range(N_BLOCKS):
                nc.vector.tensor_copy(t["gate"][:, :, n, :], g2[:, :, n, 0, :])
            link(nc.vector.tensor_copy(t["excl"][:, :, 0, :], g2[:, :, 0, 1, :]))
            for n in range(N_BLOCKS):
                last = nc.vector.tensor_tensor(t["gate"][:, :, n, :], t["gate"][:, :, n, :], g2[:, :, n, 1, :], ALU.add)
            link(last)
            assert N_BLOCKS == MOBA_TOPK + 1
            for n in range(N_BLOCKS):
                first = True
                for m in range(N_BLOCKS):
                    if m == n:
                        continue
                    dst = t["excl"][:, :, n, :] if first else t["cmp"][:, :, :]
                    link(nc.vector.tensor_tensor(dst, t["gate"][:, :, m, :], t["gate"][:, :, n, :],
                                                 ALU.is_ge if m < n else ALU.is_gt))
                    if not first:
                        link(nc.vector.tensor_tensor(t["excl"][:, :, n, :], t["excl"][:, :, n, :],
                                                     t["cmp"][:, :, :], ALU.mult))
                    first = False
            for b in range(DEC):
                last = nc.vector.scalar_tensor_tensor(L[:, b, :, :], S[:, b, :, :], K.scale, biasD[:, :, :],
                                                      ALU.mult, ALU.add)
            link(last)
            for g in range(NPAGES):
                last = nc.vector.scalar_tensor_tensor(L[:, :, g, :], t["excl"][:, :, g * PAGE // MOBA_BLOCK, :],
                                                      NEG_INF, L[:, :, g, :], ALU.mult, ALU.add)
            link(last)
        else:
            link(nc.vector.tensor_scalar(L[:, :, :, :], S[:, :, :, :], K.scale, None, ALU.mult))
        nc.vector.tensor_reduce(t["mp"][:, :, :], L[:, :, :, :].rearrange("p b g h -> p b h g"),
                                AX.X, ALU.max).then_inc(d_max, 1)
        dve.wait_ge(d_maxall, K.q + 1)
        if K.name == "A":
            link(nc.vector.tensor_scalar(t["om"][:, :, :], PS[:, 1, 0:w].rearrange("p (h b) -> p b h", h=A_HEADS),
                                         K.scale, None, ALU.mult))
            link(nc.vector.tensor_tensor(t["om"][:, :, :], t["om"][:, :, :],
                                         bias0[:, :].unsqueeze(1).to_broadcast([P, DEC, A_HEADS]), ALU.add))
            link(nc.vector.tensor_tensor(t["mx"][:, :, :], t["mx"][:, :, :], t["om"][:, :, :], ALU.max))
            link(nc.vector.tensor_tensor(t["om"][:, :, :], t["om"][:, :, :], t["mx"][:, :, :], ALU.subtract))
        for g in range(K.pages):
            last = nc.vector.tensor_tensor(L[:, :, g, :], L[:, :, g, :], t["mx"][:, :, :], ALU.subtract)
        last.then_inc(d_logit, 1)
        dve.wait_ge(d_exp, K.q + 1)
        nc.vector.tensor_reduce(t["se"][:, :, :], L[:, :, :, :].rearrange("p b g h -> p b h g"),
                                AX.X, ALU.add).then_inc(d_sb, 1)
        dve.wait_ge(sum_ps, K.q + 1)
        tot = PS[:, 3, 0:w].rearrange("p (b h) -> p b h", b=DEC)
        if K.name == "A":
            link(nc.vector.tensor_tensor(t["rd"][:, :, :], tot, t["eo"][:, :, :], ALU.add))
        else:
            link(nc.vector.tensor_copy(t["rd"][:, :, :], tot))
        link(nc.vector.reciprocal(t["x1"][:, :, :], t["rd"][:, :, :]))
        for g in range(K.pages):
            last = nc.vector.tensor_tensor(L[:, :, g, :], L[:, :, g, :], t["x1"][:, :, :], ALU.mult)
        last.then_inc(d_prob, 1)

    def act_softmax(act, K):
        act.wait_ge(d_logit, K.q + 1)
        last = nc.scalar.activation(K.t["L"][:, :, :, :], K.t["L"][:, :, :, :], ACT.Exp)
        if K.name == "A":
            last = nc.scalar.activation(K.t["eo"][:, :, :], K.t["om"][:, :, :], ACT.Exp)
        last.then_inc(d_exp, 1)

    def pool_softmax(pool, K):
        pool.wait_ge(d_max, K.q + 1)
        nc.gpsimd.partition_all_reduce(K.t["mx"][:, :, :].rearrange("p b h -> p (b h)"),
                                       K.t["mp"][:, :, :].rearrange("p b h -> p (b h)"), P,
                                       bass.bass_isa.ReduceOp.max).then_inc(d_maxall, 1)

    def pe_softmax(pe, K):
        w = DEC * K.heads
        if K.name == "A":
            for s in range(4):
                pe.wait_ge(kv_used[s], (K.base + DEC * K.pages) // 4)
            nc.tensor.matmul(PS[:, 1, 0:w], ones[:, :], own[:, :, :].rearrange("p h b -> p (h b)"),
                             start=True, stop=True)
            nc.tensor.matmul(PS[:, 0, 0:DEC * K.pages * K.heads], ones[:, :],
                             K.t["S"][:, :, :, :].rearrange("p b g h -> p (b g h)"), start=True, stop=True
                             ).then_inc(gate_ps, 1)
        pe.wait_ge(d_sb, K.q + 1)
        nc.tensor.matmul(PS[:, 3, 0:w], ones[:, :], K.t["se"][:, :, :].rearrange("p b h -> p (b h)"),
                         start=True, stop=True).then_inc(sum_ps, 1)

    def pe_values(pe, K):
        pe.wait_ge(d_prob, K.q + 1)
        def body(i):
            for p in range(2):
                wait_count(pe, d_os, i * 2 + 8 * K.q)
                for g in range(K.pages):
                    n = p * K.pages + g
                    s = n % 4
                    pe.wait_ge(kv_full[s], i * (16 * (2 * K.pages // 4)) + 16 * (
                        (K.base + DEC * K.pages + n) // 4 + 1))
                    for t in range(BT):
                        last = nc.tensor.matmul(
                            PS[:, 4 + p, t:t + 1], K.kv[:, s, t * P:(t + 1) * P],
                            K.t["L"][:, bass.ds(i * 2 + p, 1), g, t // K.et:t // K.et + 1].rearrange("p a h -> p (a h)"),
                            start=g == 0 and t == 0, stop=g == K.pages - 1, skip_group_check=True)
                    last.then_inc(kv_used[s], 1)

        first_apart(pe, DEC // 2, body)

    def dve_values(dve, K):
        s = (2 * K.pages - 1) % 4
        with dve.Fori(0, DEC // 2) as i:
            for p in range(2):
                n = K.base + DEC * K.pages + (p + 1) * K.pages - 1
                dve.wait_ge(kv_used[n % 4], i * (2 * K.pages // 4) + (n // 4 + 1))
                nc.vector.tensor_copy(K.t["oS"][:, :, bass.ds(i * 2 + p, 1)],
                                      PS[:, 4 + p, 0:BT].rearrange("p (a c) -> p a c", c=1)).then_inc(d_os, 1)

    def dve_decode_out(dve, link, K):
        t = K.t
        dve.wait_ge(d_os, 8 * K.q + 8)
        o_s = t["oS"][:, :, :]
        if K.name == "A":
            link(nc.vector.tensor_tensor(t["eo"][:, :, :], t["eo"][:, :, :], t["x1"][:, :, :], ALU.mult))
            link(nc.vector.tensor_tensor(t["o2"][:, :, :], vaS[:, :, :], t["eo"][:, :, :].rearrange("p b h -> p h b"),
                                         ALU.mult))
            link(nc.vector.tensor_tensor(o_s, o_s, t["o2"][:, :, :], ALU.add))
        link(nc.vector.tensor_copy(K.oH[:, :, SEQ:N], o_s))
        link(nc.vector.tensor_tensor(K.oL[:, :, SEQ:N], o_s, K.oH[:, :, SEQ:N].bitcast(F32), ALU.subtract))

    def copy_evac(eng, dst, sc=True):
        def evac(B, c):
            step_made(eng, B, c)
            d4 = dst[:, 4 * c:4 * c + 4, :]
            n = d4.shape[-1]
            nc.scalar.activation(d4, PS[:, 4 * c:4 * c + 4, 0:n], ACT.Copy).then_inc(set_free[c], 1)
        return evac

    def silu_evac(eng, dst):
        def evac(B, c):
            step_made(eng, B, c)
            nc.scalar.activation(dst[:, 4 * c:4 * c + 4, :], PS[:, 4 * c:4 * c + 4, 0:N],
                                 ACT.Silu).then_inc(set_free[c], 1)
        return evac

    def rotate_evac(dve, link, dst, scale):
        def evac(B, c):
            step_made(dve, B, c)
            ps = PS[:, 4 * c:4 * c + 4, 0:N].rearrange("p (h two) n -> p h two n", two=2)
            out = dst[:, 4 * c:4 * c + 4, :].rearrange("p (h two) n -> p h two n", two=2)
            for h in range(2):
                e = [EV[:, 4 * h + k, :] for k in range(4)]
                m = lambda dest, half, tab: nc.vector.scalar_tensor_tensor(
                    dest, ps[:, h, half, :], scale, tab[:, :], ALU.mult, ALU.mult)
                m(e[0], 0, cosT)
                m(e[1], 1, sinT)
                m(e[2], 0, sinT)
                link(m(e[3], 1, cosT))
                nc.vector.tensor_tensor(out[:, h, 0, :], e[0], e[1], ALU.subtract)
                last = nc.vector.tensor_tensor(out[:, h, 1, :], e[2], e[3], ALU.add)
                if h == 0:
                    link(last)
            last.then_inc(set_free[c], 1)
        return evac

    def gate_evac_act(act, i, s):
        def evac(B, c):
            step_made(act, B, c)
            for m in range(2):
                g = bass.ds(i * 4 + (G_BIAS + KT * (s % 3) + 2 * (s // 3) + m), 1)
                last = nc.scalar.activation(EV[:, 2 * c + m, :], PS[:, 4 * c + m, 0:N], ACT.Sigmoid,
                                            bias=gT[:, g])
            last.then_inc(sig_ready, 1)
        return evac

    def gate_evac_dve(dve, i, s):
        MS = 4
        def evac(B, c):
            br, p = s % 3, s // 3
            dve.wait_ge(sig_ready, i * 6 + (s + 1))
            if br == 0:
                wait_count(dve, merge_step, i * 2 * MS + MS * p)
                nc.vector.tensor_tensor(EV[:, 4:6, :], EV[:, 2 * c:2 * c + 2, :],
                                        PS[:, 4 * c + 2:4 * c + 4, 0:N], ALU.mult).then_inc(set_free[c], 1)
                return
            n = lambda k: i * 2 * MS + (MS * p + k)
            if br == 2:
                dve.wait_ge(merge_step, n(1))
            nc.vector.tensor_tensor(EV[:, 6:8, :], EV[:, 2 * c:2 * c + 2, :],
                                    PS[:, 4 * c + 2:4 * c + 4, 0:N], ALU.mult).then_inc(set_free[c], 1)
            dve.wait_ge(set_free[c], B + 1)
            if br == 1:
                dve.wait_ge(set_free[1 - c], B + c)
            nc.vector.tensor_tensor(EV[:, 4:6, :], EV[:, 4:6, :], EV[:, 6:8, :], ALU.add).then_inc(merge_step, 1)
            if br == 2:
                hi = mgH[:, bass.ds(i * 4 + 2 * p, 2), :]
                dve.wait_ge(merge_step, n(2))
                nc.vector.tensor_copy(hi, EV[:, 4:6, :]).then_inc(merge_step, 1)
                dve.wait_ge(merge_step, n(3))
                nc.vector.tensor_tensor(mgL[:, bass.ds(i * 4 + 2 * p, 2), :], EV[:, 4:6, :],
                                        hi.bitcast(F32), ALU.subtract).then_inc(merge_step, 1)
        return evac

    def split_gates(split, eng):
        def body(i):
            for s in range(6):
                B, c = i * 3 + (B_GATE + s // 2), s % 2
                split(eng, B, c, 2, 4)
                split(eng, B, c, 3, 4)
                nB, n_c = (B, 1) if c == 0 else (B + 1, 0)
                split(eng, nB, n_c, 0)
                split(eng, nB, n_c, 1)
                (gate_evac_act if split is act_split else gate_evac_dve)(eng, i, s)(B, c)

        if split is act_split:
            with eng.Fori(0, 4) as i:
                body(i)
        else:
            first_apart(eng, 4, body)

    class Link:

        def __init__(self, eng, s):
            self.eng, self.s, self.n = eng, s, 0

        def __call__(self, inst):
            self.n += 1
            inst.then_inc(self.s, 1)
            self.eng.wait_ge(self.s, self.n)
            return inst

    @block.sync
    def _(sp):
        sp.dma_start(ident[:, :], d["ident"]).then_inc(ident_in, 16)
        for k, name in enumerate(("ffn1_norm", "mix_norm", "mem_norm", "ffn2_norm", "final_norm")):
            sp.dma_start(grow[KT * k:KT * (k + 1), :], d[name].rearrange("(k p) -> k p", p=P)).then_inc(gain_in, 16)
        sp.dma_start(grow[G_BIAS:P, :], d["b_gate"].rearrange("(k p) -> k p", p=P)).then_inc(gain_in, 16)
        sp.dma_start(mtok[:, :, :], d["mem_prompt"].rearrange("(t p) c -> p t c", p=P)).then_inc(mem_in, 16)
        sp.dma_start(xtok[:, :, :], d["x_prompt"].rearrange("(t p) c -> p t c", p=P)).then_inc(x_in, 16)
        sp.dma_start(stok[0:DEC, :], d["x_sample"]).then_inc(x_in, 16)
        sp_wide(sp, 0, d["w_mem_kv"], 0)
        sp_wide(sp, 1, d["w_mem_kv"], BR_W)
        sp_ffn(sp, B_FFN1, d["ffn1_w1"], d["ffn1_w3"], d["ffn1_w2"])
        with sp.Fori(0, 4) as i:
            sp_wide(sp, i + B_IN_R, d["w_in"], i * BR_W + C_QR)
        with sp.Fori(0, 3) as i:
            sp_wide(sp, i + B_IN_A, d["w_in"], i * BR_W + C_QA)
        sp_wide(sp, B_IN_M, d["w_in"], C_QM)
        sp_gates(sp)
        with sp.Fori(0, 2) as i:
            sp_wide(sp, i + B_OUT, d["w_out"], i * BR_W)
        sp_ffn(sp, B_FFN2, d["ffn2_w1"], d["ffn2_w3"], d["ffn2_w2"])
        y0 = turns_of("y")[0][0]
        sp.wait_ge(turn_out, y0 + 8)
        sp.dma_start(o["y_prompt"].rearrange("(t p) c -> p t c", p=P), ytok[:, :, :]).then_inc(y_sent, 16)
        sp.wait_ge(turn_out, y0 + 12)
        sp.dma_start(o["y_sample"], ystok[0:DEC, :]).then_inc(y_sent, 16)
        sp.wait_ge(y_sent, 32)

    @block.gpsimd
    def _(pool):
        nc.gpsimd.memset(ones[:, :], 1.0).then_inc(ones_set, 1)
        pool.dma_start(ptab[0:1, :], d["page_table"]).then_inc(pt_in, 16)
        pool.wait_ge(pt_in, 16)
        pool.wait_ge(turn_out, turns_until("mem_kv"))
        pool.dma_start(o["mem_k_prompt"].rearrange("(t p) c -> p t c", p=P), mkTok[:, :, :]).then_inc(stored, 16)
        pool.dma_start(o["mem_v_prompt"].rearrange("(t p) c -> p t c", p=P), mvTok0[:, :, :]).then_inc(stored, 16)
        pool.dma_start(scratch["mv"].rearrange("(t p) c -> p t c", p=P), mvTok0[:, :, :]).then_inc(kept, 16)
        pool.dma_start(scratch["mkT"], mkT0[:, :, :].rearrange("p a c -> p (a c)")).then_inc(kept, 16)
        pool.wait_ge(kept, 32)
        pool.wait_ge(stored, 32)
        pool.wait_ge(unit_used, 8 * B_IN)
        pool.dma_start(cosT[:, :], d["cos"]).then_inc(rot_in, 16)
        pool.dma_start(sinT[:, :], d["sin"]).then_inc(rot_in, 16)
        pool.dma_start(kdecay[:, :, :], d["kdecay"]).then_inc(decay_in, 16)
        pool.dma_start(decay[:, :, :], d["decay"]).then_inc(decay_in, 16)
        pool.wait_ge(turn_out, turns_until("r"))
        pool.dma_start(scratch["vr"], vrS[0:DEC, :]).then_inc(kept, 16)
        pool.wait_ge(kept, 48)
        for h in range(R_HEADS):
            pool.wait_ge(s_out, h + 1)
            pool.dma_start(o["ret_state_prompt"][h].rearrange("(t p) e -> p t e", p=P),
                           st[:, h % 2, :, :]).then_inc(st_sent[h % 2], 16)
        pool.wait_ge(st_sent[0], 32)
        pool.wait_ge(st_sent[1], 32)
        pool.wait_ge(r_done, R_HEADS)
        pool_states(pool)
        pool.wait_ge(s_back[0], 64)
        pool.wait_ge(s_back[1], 64)
        pool.wait_ge(r_all_done, 1)
        pool.dma_start(t5w[0:T5_BUCKETS, :], d["t5_table"]).then_inc(t5_in, 16)
        pool.dma_start(bkp[0:T5_BUCKETS, :], d["bucket_prompt"]).then_inc(t5_in, 16)
        pool.dma_start(bkd[0:T5_BUCKETS, :], d["bucket_decode"]).then_inc(t5_in, 16)
        pool.wait_ge(t5_ready, 1)
        pool.dma_start(scratch["t5"], t5row[0:A_HEADS, :].unsqueeze(1).to_broadcast([A_HEADS, P, 2 * SEQ])
                       ).then_inc(kept, 16)
        pool.wait_ge(kept, 64)
        pool.wait_ge(turn_out, turns_until("a"))
        pool.dma_start(o["v_prompt"].rearrange("(t p) c -> p t c", p=P), vaTok[:, :, :]).then_inc(stored, 16)
        pool.dma_start(o["k_prompt"].rearrange("(t p) c -> p t c", p=P), kaTok[:, :, :]).then_inc(stored, 16)
        pool.dma_start(o["k_sample"], rows[0:DEC, 0, :]).then_inc(stored, 16)
        pool.dma_start(o["v_sample"], rows[0:DEC, 1, :]).then_inc(stored, 16)
        pool.dma_start(scratch["qa"], rows[0:DEC, 2, :]).then_inc(kept, 16)
        for h in range(A_HEADS):
            if h >= 2:
                pool.wait_ge(a_p, h - 1)
            for it in range(2):
                diag = bass.AP(tensor=scratch["t5"].tensor, offset=h * P * 2 * SEQ + SEQ - 1 - it * P,
                               ap=[[2 * SEQ - 1, P], [1, SEQ]])
                pool.dma_start(bias[:, h % 2, it, :], diag).then_inc(bias_in[h % 2], 16)
        pool.wait_ge(kept, 80)
        pool.wait_ge(stored, 96)
        pool.wait_ge(a_lo, A_HEADS)
        pool_decode(pool, DKA, 0)
        pool_softmax(pool, DKA)
        pool_decode(pool, DKA, 1)
        pool.wait_ge(a_done, 1)
        pool.dma_start(mkT[:, :, :].rearrange("p a c -> p (a c)"), scratch["mkT"]).then_inc(mk_in, 16)
        pool.dma_start(mvTok[:, :, :], scratch["mv"].rearrange("(t p) c -> p t c", p=P)).then_inc(mk_in, 16)
        pool.wait_ge(turn_out, turns_until("m"))
        pool.dma_start(scratch["qm"], qmS[0:DEC, :]).then_inc(kept, 16)
        pool.wait_ge(kept, 96)
        pool.wait_ge(a_lo, A_HEADS + M_HEADS)
        pool_decode(pool, DKM, 0)
        pool_softmax(pool, DKM)
        pool_decode(pool, DKM, 1)

    @block.tensor
    def _(pe):
        pe.wait_ge(ident_in, 16)
        pe.wait_ge(gain_in, 96)
        pe_turns(pe, "gain")
        pe.wait_ge(mem_in, 16)
        pe_turns(pe, "mem")
        pe.wait_ge(x_in, 32)
        pe_turns(pe, "x")
        pe.wait_ge(ones_set, 1)
        pe_norm(pe, "mem")
        pe.wait_ge(norm_done, 1)
        pe.wait_ge(turn_out, turns_until("x"))
        pe_wide(pe, 0, (hH, hL), N_MEM)
        pe_wide(pe, 1, (hH, hL), N_MEM)
        pe_drained(pe, 2)
        pe_turns(pe, "mem_kv")
        pe.wait_ge(turn_out, turns_until("mem_kv"))
        pe_norm(pe, "ffn1")
        pe.wait_ge(norm_done, 2)
        pe_ffn(pe, B_FFN1)
        pe_drained(pe, B_IN)
        pe_norm(pe, "mix")
        pe.wait_ge(norm_done, 3)
        with pe.Fori(0, 4) as i:
            pe_wide(pe, i + B_IN_R, (hH, hL))
        pe_drained(pe, B_IN_A)
        pe_turns(pe, "r")
        pe.wait_ge(turn_out, turns_until("r"))
        pe_retention(pe)
        pe.wait_ge(s_out, R_HEADS)
        pe_states(pe)
        pe.wait_ge(samp_sq, 1)
        for et in range(2):
            last = nc.tensor.matmul(PS[:, 5, 0:R_HEADS * DEC], ones[:, :],
                                    orS2[:, et:BT:2, :], start=et == 0, stop=et == 1)
        last.then_inc(samp_ms, 1)
        pe.wait_ge(r_all_done, 1)
        with pe.Fori(0, 3) as i:
            pe_wide(pe, i + B_IN_A, (hH, hL))
        pe_drained(pe, B_IN_M)
        pe.wait_ge(t5_in, 48)
        nc.tensor.matmul(PS[0:A_HEADS, 3, 0:SEQ], t5w[0:T5_BUCKETS, :], bkp[0:T5_BUCKETS, :], start=True, stop=True)
        for g in range(NPAGES):
            nc.tensor.matmul(PS[:, 2, A_HEADS * g:A_HEADS * (g + 1)], bkd[0:T5_BUCKETS, g * P:(g + 1) * P],
                             t5w[0:T5_BUCKETS, :], start=True, stop=True)
        nc.tensor.matmul(PS[:, 2, 64:64 + A_HEADS], ones[0:1, :], t5w[0:1, :],
                         start=True, stop=True).then_inc(t5_ps, 1)
        pe_turns(pe, "a")
        pe.wait_ge(turn_out, turns_until("a"))
        pe.wait_ge(t5_ready, 2)
        pe_attend(pe, KA)
        pe.wait_ge(own_ready, 1)
        pe.wait_ge(a_lo, A_HEADS)
        pe_softmax(pe, DKA)
        pe_values(pe, DKA)
        pe.wait_ge(a_done, 1)
        pe_wide(pe, B_IN_M, (hH, hL))
        pe_drained(pe, B_GATE)
        pe_turns(pe, "m")
        pe.wait_ge(turn_out, turns_until("m"))
        pe.wait_ge(mk_in, 32)
        pe_attend(pe, KM)
        pe.wait_ge(a_lo, A_HEADS + M_HEADS)
        pe_softmax(pe, DKM)
        pe_values(pe, DKM)
        pe.wait_ge(m_done, 1)
        pe_gates(pe)
        pe_drained(pe, B_OUT)
        pe.wait_ge(merge_step, 4 * KT // 2)
        with pe.Fori(0, 2) as i:
            pe_wide(pe, i + B_OUT, (mgH, mgL))
        pe_drained(pe, B_FFN2)
        pe_norm(pe, "ffn2")
        pe.wait_ge(norm_done, 4)
        pe_ffn(pe, B_FFN2)
        pe_drained(pe, B_END)
        pe_norm(pe, "final")
        pe.wait_ge(norm_done, 5)
        pe_turns(pe, "y")

    @block.scalar
    def _(act):
        act_turns(act, "gain")
        act_turns(act, "mem")
        act_turns(act, "x")
        act.wait_ge(turn_out, turns_until("x"))
        act_norm(act, "mem")
        act_split(act, 0, 0, 0)
        act_split(act, 0, 0, 1)
        split_body(act_split, act, 0, copy_evac(act, mkT0))
        split_body(act_split, act, 1, copy_evac(act, mvT0))
        act_turns(act, "mem_kv")
        act_norm(act, "ffn1")
        split_ffn(act_split, act, B_FFN1, 0, False)
        act.wait_ge(set_free[0], B_IN)
        act.wait_ge(set_free[1], B_IN)
        act_norm(act, "mix")
        act.wait_ge(stored, 32)
        act.wait_ge(kept, 32)
        split_body(act_split, act, B_IN_R, none)
        split_body(act_split, act, B_IN_R + 1, none)
        split_body(act_split, act, B_IN_R + 2, copy_evac(act, vrT))
        split_body(act_split, act, B_IN_R + 3, silu_evac(act, grT))
        act_turns(act, "r")
        act.wait_ge(kept, 48)
        act_retention(act)
        act_states(act)
        act.wait_ge(samp_var, 1)
        nc.scalar.activation(rt[:, 0:R_HEADS * DEC], rs[:, 0:R_HEADS * DEC], ACT.Sqrt).then_inc(samp_sqrt, 1)
        act.wait_ge(r_all_done, 1)
        split_body(act_split, act, B_IN_A, copy_evac(act, qaT))
        split_body(act_split, act, B_IN_A + 1, copy_evac(act, kaT))
        split_body(act_split, act, B_IN_A + 2, copy_evac(act, vaT))
        act.wait_ge(s_back[0], 64)
        act.wait_ge(s_back[1], 64)
        act.wait_ge(kept, 64)
        act_turns(act, "a")
        act_attend(act, KA)
        act_softmax(act, DKA)
        act.wait_ge(a_done, 1)
        split_body(act_split, act, B_IN_M, copy_evac(act, qmT))
        act_turns(act, "m")
        act_attend(act, KM)
        act_softmax(act, DKM)
        split_gates(act_split, act)
        with act.Fori(0, 2) as i:
            split_body(act_split, act, i + B_OUT, none)
        act.wait_ge(set_free[0], B_FFN2)
        act.wait_ge(set_free[1], B_FFN2)
        act_norm(act, "ffn2")
        split_ffn(act_split, act, B_FFN2, 1, True)
        act.wait_ge(set_free[0], B_END)
        act.wait_ge(set_free[1], B_END)
        act_norm(act, "final")
        act_turns(act, "y")

    @block.vector
    def _(dve):
        link = Link(dve, dve_link)
        dve.wait_ge(turn_out, turns_until("x"))
        dve_norm(dve, link, "mem")
        dve_split(dve, 0, 0, 0)
        dve_split(dve, 0, 0, 1)
        split_body(dve_split, dve, 0, none)
        split_body(dve_split, dve, 1, none)
        dve_norm(dve, link, "ffn1")
        split_ffn(dve_split, dve, B_FFN1, 0, False)
        dve.wait_ge(set_free[0], B_IN)
        dve.wait_ge(set_free[1], B_IN)
        dve_norm(dve, link, "mix")
        dve.wait_ge(rot_in, 32)
        dve.wait_ge(stored, 32)
        dve.wait_ge(kept, 32)
        split_body(dve_split, dve, B_IN_R, rotate_evac(dve, link, qrT, 1.0))
        split_body(dve_split, dve, B_IN_R + 1, rotate_evac(dve, link, krT, R_DK ** -0.5))
        split_body(dve_split, dve, B_IN_R + 2, none)
        split_body(dve_split, dve, B_IN_R + 3, none)
        dve.wait_ge(decay_in, 32)
        dve.wait_ge(turn_out, turns_until("r"))
        dve_retention(dve, link)
        dve_states(dve)
        dve.wait_ge(os_out, DEC)
        dve.wait_ge(s_back[0], 64)
        dve.wait_ge(s_back[1], 64)
        w = R_HEADS * DEC
        nc.vector.tensor_tensor(orS2[:, :, :], orS[:, :, :], orS[:, :, :], ALU.mult).then_inc(samp_sq, 1)
        dve.wait_ge(samp_ms, 1)
        nc.vector.tensor_scalar(rs[:, 0:w], PS[:, 5, 0:w], 1.0 / R_DV, EPS, ALU.mult, ALU.add).then_inc(samp_var, 1)
        dve.wait_ge(samp_sqrt, 1)
        link(nc.vector.reciprocal(ry[:, 0:w], rt[:, 0:w]))
        refine(link, ry[:, 0:w], rs[:, 0:w], rt[:, 0:w])
        for et in range(2):
            last = nc.vector.tensor_tensor(orS2[:, et:BT:2, :], orS[:, et:BT:2, :],
                                           ry[:, 0:w].rearrange("p (h b) -> p h b", h=R_HEADS), ALU.mult)
        link(last)
        link(nc.vector.tensor_tensor(orS2[:, :, :], orS2[:, :, :], grT[:, :, SEQ:N], ALU.mult))
        link(nc.vector.tensor_copy(orH[:, :, SEQ:N], orS2[:, :, :]))
        nc.vector.tensor_tensor(orL[:, :, SEQ:N], orS2[:, :, :], orH[:, :, SEQ:N].bitcast(F32),
                                ALU.subtract).then_inc(r_all_done, 1)
        for k in range(3):
            split_body(dve_split, dve, B_IN_A + k, none)
        dve.wait_ge(t5_ps, 1)
        nc.vector.memset(t5row[0:A_HEADS, SEQ:2 * SEQ], NEG_INF)
        nc.vector.tensor_copy(biasD[:, :, :].rearrange("p g h -> p (g h)"), PS[:, 2, 0:64])
        nc.vector.tensor_copy(bias0[:, :], PS[:, 2, 64:64 + A_HEADS])
        link(nc.vector.tensor_copy(t5row[0:A_HEADS, 0:SEQ], PS[0:A_HEADS, 3, 0:SEQ]))
        nc.vector.tensor_copy(vaS[:, :, :], vaT[:, :, SEQ:N]).then_inc(t5_ready, 1)
        nc.vector.tensor_tensor(own[:, :, :], qaT[:, :, SEQ:N], kaT[:, :, SEQ:N], ALU.mult).then_inc(own_ready, 1)
        dve.wait_ge(own_ready, 1)
        nc.vector.tensor_copy(MX[:, 0, 0, :], own[:, 0, 0:2]).then_inc(t5_ready, 1)
        dve.wait_ge(kept, 80)
        dve.wait_ge(stored, 96)
        dve_attend(dve, link, KA)
        dve.wait_ge(kept, 80)
        dve_scores(dve, DKA)
        for s in range(4):
            dve.wait_ge(kv_used[s], DEC * NPAGES // 4)
        dve_softmax(dve, link, DKA)
        dve_values(dve, DKA)
        dve_decode_out(dve, link, DKA)
        nc.vector.tensor_copy(MX[:, 0, 0, :], own[:, 0, 0:2]).then_inc(a_done, 1)
        split_body(dve_split, dve, B_IN_M, none)
        dve_attend(dve, link, KM)
        dve_scores(dve, DKM)
        for s in range(4):
            dve.wait_ge(kv_used[s], (DKM.base + DEC * 2) // 4)
        dve_softmax(dve, link, DKM)
        dve_values(dve, DKM)
        dve_decode_out(dve, link, DKM)
        nc.vector.tensor_copy(MX[:, 0, 0, :], DM["oS"][:, 0, 0:2]).then_inc(m_done, 1)
        split_gates(dve_split, dve)
        with dve.Fori(0, 2) as i:
            split_body(dve_split, dve, i + B_OUT, add_evac_dve(dve, i, 1.0))
        dve.wait_ge(set_free[0], B_FFN2)
        dve.wait_ge(set_free[1], B_FFN2)
        dve_norm(dve, link, "ffn2")
        split_ffn(dve_split, dve, B_FFN2, 1, True)
        dve.wait_ge(set_free[0], B_END)
        dve.wait_ge(set_free[1], B_END)
        dve_norm(dve, link, "final", yT)


_INS = {
    "x_prompt": (SEQ, D_MODEL), "x_sample": (DEC, D_MODEL), "mem_prompt": (N_MEM, D_MODEL),
    "cache_k": (-1, PAGE, BR_W), "cache_v": (-1, PAGE, BR_W),
    "cache_mem_k": (DEC, N_MEM, BR_W), "cache_mem_v": (DEC, N_MEM, BR_W),
    "state_ret": (DEC, R_HEADS, R_DK, R_DV), "page_table": (1, DEC * NPAGES), "t5_table": (T5_BUCKETS, A_HEADS),
    "ffn1_norm": (D_MODEL,), "ffn1_w1": (D_MODEL, D_FF), "ffn1_w3": (D_MODEL, D_FF), "ffn1_w2": (D_FF, D_MODEL),
    "mix_norm": (D_MODEL,), "mem_norm": (D_MODEL,), "w_in": (D_MODEL, 8 * BR_W), "w_mem_kv": (D_MODEL, 2 * BR_W),
    "w_gate": (D_MODEL, 3 * D_MODEL), "b_gate": (3 * D_MODEL,), "w_br_moba": (BR_W, D_MODEL),
    "w_br_ret": (BR_W, D_MODEL), "w_br_mem": (BR_W, D_MODEL), "w_out": (D_MODEL, D_MODEL),
    "ffn2_norm": (D_MODEL,), "ffn2_w1": (D_MODEL, D_FF), "ffn2_w3": (D_MODEL, D_FF), "ffn2_w2": (D_FF, D_MODEL),
    "final_norm": (D_MODEL,),
}
_OUTS = {
    "y_prompt": ((SEQ, D_MODEL), (1, SEQ, D_MODEL)), "y_sample": ((DEC, D_MODEL), (DEC, 1, D_MODEL)),
    "k_prompt": ((SEQ, BR_W), (1, 1, SEQ, A_HEADS, A_DH)), "v_prompt": ((SEQ, BR_W), (1, 1, SEQ, A_HEADS, A_DH)),
    "mem_k_prompt": ((N_MEM, BR_W), (1, 1, N_MEM, M_HEADS, M_DH)),
    "mem_v_prompt": ((N_MEM, BR_W), (1, 1, N_MEM, M_HEADS, M_DH)),
    "ret_state_prompt": ((R_HEADS, R_DK, R_DV), (1, 1, R_HEADS, R_DK, R_DV)),
    "k_sample": ((DEC, BR_W), (1, DEC, 1, A_HEADS, A_DH)), "v_sample": ((DEC, BR_W), (1, DEC, 1, A_HEADS, A_DH)),
    "ret_state_sample": ((DEC, R_HEADS, R_DK, R_DV), (1, DEC, R_HEADS, R_DK, R_DV)),
}


def kernel(**inputs):
    from contextlib import ExitStack
    import concourse.bacc as bacc
    from concourse.bass_utils import run_bass_kernel_spmd

    nc = bacc.Bacc("TRN2", target_bir_lowering=False, num_devices=1)
    arrays = {n: np.ascontiguousarray(inputs[n]).reshape(s) for n, s in _INS.items()}
    arrays.update(constants())
    d = {n: nc.dram_tensor(n, a.shape, mybir.dt.from_np(a.dtype), kind="ExternalInput").ap()
         for n, a in arrays.items()}
    o = {n: nc.dram_tensor(f"out_{n}", s, F32, kind="ExternalOutput").ap() for n, (s, _) in _OUTS.items()}
    with ExitStack() as ctx:
        PS = ctx.enter_context(nc.psum_tensor("PS", [P, 8, 512], F32))
        build(nc, d, o, lambda name: ctx.enter_context(nc.semaphore(name)), PS,
              ctx.enter_context(nc.Block()))
    r = run_bass_kernel_spmd(nc, [arrays], core_ids=[0])
    return tuple(r.results[0][f"out_{n}"].reshape(s) for n, (_, s) in _OUTS.items())
```

```python
import numpy as np
import concourse.bass as bass
import concourse.mybir as mybir

F32 = mybir.dt.float32
F32R = mybir.dt.float32r
I32 = mybir.dt.int32
ALU = mybir.AluOpType
ACT = mybir.ActivationFunctionType
AX = mybir.AxisListType

P = 128
D_MODEL, SEQ, DEC, PAST, PAGE = 2048, 256, 8, 1024, 128
A_HEADS, A_DH, MOBA_BLOCK, MOBA_TOPK, T5_BUCKETS, T5_MAX_DIST = 8, 128, 256, 3, 32, 128
R_HEADS, R_DK, R_DV, ROPE_BASE = 4, 256, 256, 10000.0
M_HEADS, M_DH, N_MEM = 4, 256, 256
BR_W = 1024
D_FF, EPS, NEG_INF = 5632, 1e-6, -1e30
N = SEQ + DEC
KT = D_MODEL // P
BT = BR_W // P
UK, UC = 8, 256
NPAGES = PAST // PAGE
N_BLOCKS = PAST // MOBA_BLOCK
HID = 16
FFN_BLOCKS = [(0, 16), (16, 16), (32, 12)]

B_MEM = 0
B_FFN1 = B_MEM + 2
FFN_BODIES = sum(n // 4 + 2 for _, n in FFN_BLOCKS)
B_IN = B_FFN1 + FFN_BODIES
DVE_PAGES, PE_PAGES = (0, 1, 2, 4, 5, 6), (3, 7)
B_IN_R, B_IN_M, B_IN_A = B_IN, B_IN + 4, B_IN + 5
B_GATE = B_IN + 8
B_OUT = B_GATE + 12
B_FFN2 = B_OUT + 2
B_END = B_FFN2 + FFN_BODIES
C_QA, C_QR, C_QM = 0, 3 * BR_W, 7 * BR_W

GAMMA = [1.0 - 2.0 ** (-5 - h) for h in range(R_HEADS)]

CONSTS = ["ident", "cos", "sin", "decay", "kdecay", "bucket_prompt", "bucket_decode"]


def t5_bucket(n):
    exact = T5_BUCKETS // 2
    nf = np.maximum(n, 1).astype(np.float32)
    large = exact + (np.log(nf / exact) / np.float32(np.log(T5_MAX_DIST / exact))
                     * (T5_BUCKETS - exact)).astype(np.int32)
    return np.where(n < exact, n, np.minimum(large, T5_BUCKETS - 1))


def constants():
    half = R_DK // 2
    inv = (1.0 / (np.float32(ROPE_BASE) ** np.linspace(0.0, 1.0, half, dtype=np.float32))).astype(np.float32)
    pos = np.concatenate([np.arange(SEQ), np.full(DEC, PAST)]).astype(np.float32)
    ang = (inv[:, None] * pos[None, :]).astype(np.float32)
    log_g = np.log(np.array(GAMMA))
    i = np.arange(SEQ)
    diff = i[None, :] - i[:, None]
    decay = np.where(diff[None] >= 0, np.exp(np.maximum(diff, 0)[None] * log_g[:, None, None]), 0.0)
    decay = decay.reshape(R_HEADS, 2, P, SEQ).transpose(2, 0, 1, 3)
    decay = np.concatenate([decay[:, :, 0], decay[:, :, 1, P:]], axis=2)
    kdecay = np.exp((SEQ - 1 - i)[None, :] * log_g[:, None]).reshape(R_HEADS, 2, P).transpose(2, 0, 1)
    eye = np.eye(T5_BUCKETS, dtype=np.float32)
    return {
        "ident": np.eye(P, dtype=np.float32),
        "cos": np.cos(ang).astype(np.float32),
        "sin": np.sin(ang).astype(np.float32),
        "decay": np.ascontiguousarray(decay).astype(np.float32),
        "kdecay": np.ascontiguousarray(kdecay).astype(np.float32),
        "bucket_prompt": np.ascontiguousarray(eye[:, t5_bucket(SEQ - 1 - np.arange(SEQ))]),
        "bucket_decode": np.ascontiguousarray(eye[:, t5_bucket(PAST - np.arange(PAST))]),
    }


def build(nc, d, o, sem, PS, block):

    base = -(-nc.sbuf_base // 64) * 64

    def at(name, shape, offset, dt=F32):
        return nc.alloc_sbuf_tensor_at(name, [P, *shape], dt, offset=base + offset)

    ROWT = N * 4
    A_X = 0
    A_H = A_X + KT * ROWT
    A_HID = A_H + 2 * KT * ROWT
    A_RAW = A_HID + 2 * HID * ROWT
    A_SPLIT = A_RAW + 4 * UK * UC * 4
    A_EV = A_SPLIT + 4 * UK * UC * 4
    A_SMALL = A_EV + 8 * ROWT
    A_MID = A_SMALL + 1856

    xT = at("xT", [KT, N], A_X)
    hH = at("hH", [KT, N], A_H, F32R)
    hL = at("hL", [KT, N], A_H + KT * ROWT, F32R)
    hidH = at("hidH", [HID, N], A_HID, F32R)
    hidL = at("hidL", [HID, N], A_HID + HID * ROWT, F32R)
    raw = at("raw", [4, UK, UC], A_RAW)
    splitH = at("splitH", [2, UK, UC], A_SPLIT, F32R)
    splitL = at("splitL", [2, UK, UC], A_SPLIT + 2 * UK * UC * 4, F32R)
    EV = at("EV", [8, N], A_EV)
    off = A_SMALL

    def small(name, shape, dt=F32):
        nonlocal off
        t = at(name, shape, off, dt)
        off += -(-int(np.prod(shape)) * 4 // 32) * 32
        assert off <= A_MID
        return t

    ident = small("ident_s", [P])
    ones = small("ones", [P])
    gT = small("gT", [P])
    ptab = small("ptab", [DEC * NPAGES], I32)
    bias0 = small("bias0", [A_HEADS])
    TAIL = A_MID + 48128
    rs = at("rs", [N], TAIL)
    rt = at("rt", [N], TAIL + ROWT)
    ry = at("ry", [N], TAIL + 2 * ROWT)
    MX = small("MX", [2, 2, 2])
    G_FFN1, G_MIX, G_MEM, G_FFN2, G_FINAL, G_BIAS = 0, 16, 32, 48, 64, 80

    xtok = at("xtok", [2, D_MODEL], A_MID)
    mtok = at("mtok", [2, D_MODEL], A_MID + 16384)
    stok = at("stok", [D_MODEL], A_MID + 32768)
    memT = at("memT", [KT, N_MEM], A_HID)
    grow = at("grow", [P], A_EV)
    mkT0 = at("mkT0", [BT, N_MEM], A_MID)
    mvT0 = at("mvT0", [BT, N_MEM], A_MID + 8192)
    mkTok = at("mkTok", [2, BR_W], A_MID + 16384)
    mvTok0 = at("mvTok0", [2, BR_W], A_MID + 24576)
    T8 = BT * ROWT
    HB = A_HID + 2 * BT * ROWT
    orH = at("orH", [BT, N], A_HID, F32R)
    orL = at("orL", [BT, N], A_HID + T8, F32R)
    qrT = at("qrT", [BT, N], A_MID)
    krT = at("krT", [BT, N], A_MID + T8)
    grT = at("grT", [BT, N], A_MID + 2 * T8)
    vrT = at("vrT", [BT, N], A_MID + 3 * T8)
    vrTok = at("vrTok", [2, BR_W], A_MID + 4 * T8)
    decay = at("decay_s", [R_HEADS, SEQ + P], A_MID + 4 * T8 + 8192)
    cosT = at("cosT", [N], HB)
    sinT = at("sinT", [N], HB + ROWT)
    kdecay = at("kdecay_s", [R_HEADS, 2], HB + 2 * ROWT)
    vrS = at("vrS", [BR_W], HB + 2 * ROWT + 64)
    st = at("st", [2, 2, R_DV], HB + 2 * ROWT + 64)
    krTok = at("krTok", [2, BR_W], HB + 2 * ROWT + 64 + 4096)
    vB = at("vB", [2, BR_W], HB + 2 * ROWT + 64 + 4096)
    orS = at("orS", [BT, DEC], HB + 2 * ROWT + 64 + 4096 + 8192)
    orS2 = at("orS2", [BT, DEC], HB + 2 * ROWT + 64 + 4096 + 8192 + 256)
    state = [at("state0", [R_HEADS, 2, R_DV], A_MID + 3 * T8),
             at("state1", [R_HEADS, 2, R_DV], A_MID + 4 * T8 + 8192)]
    sqb = at("sqb", [2, 2, SEQ], A_EV)
    attb = at("attb", [2, 2, SEQ], A_EV + 4096)
    oaH = at("oaH", [BT, N], A_MID + 34816, F32R)
    oaL = at("oaL", [BT, N], A_MID + 34816 + T8, F32R)
    qaT = at("qaT", [BT, N], A_MID)
    kaT = at("kaT", [BT, N], A_MID + T8)
    vaT = at("vaT", [BT, N], A_MID + 2 * T8)
    vaTok = at("vaTok", [2, BR_W], A_MID + 3 * T8)
    rows = at("rows", [3, BR_W], A_X)
    kaTok = at("kaTok", [2, BR_W], A_EV)
    bias = at("bias", [2, 2, SEQ], A_X + 12288)
    vaS = at("vaS", [BT, DEC], A_MID + 4 * T8)
    own = at("own", [BT, DEC], A_MID + 4 * T8 + 256)
    biasD = at("biasD", [NPAGES, A_HEADS], A_MID + 4 * T8 + 512)
    kvA = at("kvA", [4, BR_W], A_MID)
    qBA = at("qBA", [2, BR_W], A_MID + 16384)
    pvSum = at("pvSum", [2, BR_W], A_MID + 16384)
    DEC_A = A_MID + 24576
    Sb = at("Sb", [2, NPAGES, A_HEADS], A_EV + 4 * ROWT)
    accT = at("accT", [KT, N], A_X)
    omH = at("omH", [BT, N], HB, F32R)
    omL = at("omL", [BT, N], HB + T8, F32R)
    qmT = at("qmT", [BT, N], A_MID)
    mkT = at("mkT", [BT, N_MEM], A_MID + T8)
    mvTok = at("mvTok", [2, BR_W], A_MID + T8 + 8192)
    qmS = at("qmS", [BR_W], A_MID + T8 + 16384)
    kvM = at("kvM", [4, BR_W], A_MID + T8)
    qBM = at("qBM", [2, BR_W], A_MID)
    mgH = at("mgH", [KT, N], A_MID, F32R)
    mgL = at("mgL", [KT, N], A_MID + KT * ROWT, F32R)
    assert A_MID + 34816 + 2 * T8 <= nc.sbuf_usable_end - base
    t5w = at("t5w", [A_HEADS], A_EV)
    bkp = at("bkp", [SEQ], A_EV + 64)
    bkd = at("bkd", [PAST], A_EV + 1088)
    t5row = at("t5row", [2 * SEQ], A_EV + 5184)

    def dec_tiles(kind, where, pages, heads):
        w = DEC * pages * heads * 4
        t = {n: at(f"{kind}_{n}", [DEC, pages, heads], where + k * w) for k, n in enumerate(("S", "L"))}
        g = where + 2 * w
        for k, n in enumerate(("mp", "mx", "se", "rd", "om", "eo", "t", "x1")):
            t[n] = at(f"{kind}_{n}", [DEC, heads], g + k * DEC * heads * 4)
        g += 8 * DEC * heads * 4
        t["oS"] = at(f"{kind}_oS", [BT, DEC], g)
        t["o2"] = at(f"{kind}_o2", [BT, DEC], g + 256)
        if kind == "A":
            t["gate"] = at("A_gate", [DEC, N_BLOCKS, heads], g + 512)
            t["excl"] = at("A_excl", [DEC, N_BLOCKS, heads], g + 1536)
            t["cmp"] = at("A_cmp", [DEC, heads], g + 2560)
        return t

    DA = dec_tiles("A", DEC_A, NPAGES, A_HEADS)
    DM = dec_tiles("M", A_EV, 2, M_HEADS)

    scratch = {n: nc.dram_tensor(f"scratch_{n}", list(s), F32, kind="Internal").ap() for n, s in {
        "t5": (A_HEADS, P, 2 * SEQ), "qa": (DEC, BR_W), "vr": (DEC, BR_W), "qm": (DEC, BR_W),
        "mkT": (P, BT * N_MEM), "mv": (N_MEM, BR_W), "x": (P, KT * N)}.items()}

    raw_full = [sem(f"raw_full{u}") for u in range(4)]
    hi_ready, split_ready, unit_used = sem("hi_ready"), sem("split_ready"), sem("unit_used")
    set_free = [sem(f"set_free{c}") for c in range(2)]
    silu_ready, prod_ready, hid_hi = sem("silu_ready"), sem("prod_ready"), sem("hid_hi")
    sig_ready, merge_step = sem("sig_ready"), sem("merge_step")
    rot_step = sem("rot_step")
    sq_ready, sq_used, ms_ready, sqrt_ready, norm_rows, norm_hi, norm_done = map(sem, (
        "sq_ready", "sq_used", "ms_ready", "sqrt_ready", "norm_rows", "norm_hi", "norm_done"))
    dve_link = sem("dve_link")
    x_in, mem_in, gain_in, ident_in, rot_in, decay_in, t5_in, pt_in = map(sem, (
        "x_in", "mem_in", "gain_in", "ident_in", "rot_in", "decay_in", "t5_in", "pt_in"))
    ones_set, mk_in = sem("ones_set"), sem("mk_in")
    stored = sem("stored")
    kept = sem("kept")
    turned, turn_out = sem("turned"), sem("turn_out")
    att_ps, att_sb, o_ps, o_sq, ms_ps, ms_ev, r_done, kd_ready, s_ps, s_out = map(sem, (
        "att_ps", "att_sb", "o_ps", "o_sq", "ms_ps", "ms_ev", "r_done", "kd_ready", "s_ps", "s_out"))
    r_hi, r_var, r_sqrt, r_res = sem("r_hi"), sem("r_var"), sem("r_sqrt"), sem("r_res")
    st_sent = [sem(f"st_sent{p}") for p in range(2)]
    s_in = [sem(f"s_in{p}") for p in range(2)]
    vb_in = [sem(f"vb_in{p}") for p in range(2)]
    s_scaled, s_new, s_read, s_back, os_out = sem("s_scaled"), sem("s_new"), sem("s_read"), [
        sem(f"s_back{p}") for p in range(2)], sem("os_out")
    a_s, a_p, a_max, a_exp, a_norm, a_pt, a_ptc, a_o, a_hi, a_lo = map(sem, (
        "a_s", "a_p", "a_max", "a_exp", "a_norm", "a_pt", "a_ptc", "a_o", "a_hi", "a_lo"))
    bias_in = [sem(f"bias_in{p}") for p in range(2)]
    t5_ps, t5_ready = sem("t5_ps"), sem("t5_ready")
    kv_full = [sem(f"kv_full{s}") for s in range(4)]
    kv_used = [sem(f"kv_used{s}") for s in range(4)]
    page_full = [sem(f"page_full{s}") for s in range(4)]
    q_in = [sem(f"q_in{s}") for s in range(2)]
    qb_in = [sem(f"qb_in{s}") for s in range(2)]
    kq_ready = sem("kq_ready")
    gate_ps, sum_ps, d_sb, d_exp, d_max, d_maxall, d_logit = map(sem, (
        "gate_ps", "sum_ps", "d_sb", "d_exp", "d_max", "d_maxall", "d_logit"))
    own_ready, r_all_done, samp_sq, samp_ms, samp_var, samp_sqrt, m_done, a_done = map(sem, (
        "own_ready", "r_all_done", "samp_sq", "samp_ms", "samp_var", "samp_sqrt", "m_done", "a_done"))
    d_prob, d_os = sem("d_prob"), sem("d_os")
    p_in_place, sample_summed = sem("p_in_place"), sem("sample_summed")
    s_in_place, os_copied, x_kept, x_back = sem("s_in_place"), sem("os_copied"), sem("x_kept"), sem("x_back")
    y_sent = sem("y_sent")

    turns = []

    def turn(name, srcs, rows, width, dest):
        turns.append((name, srcs, rows, width, dest))

    turn("gain", [(grow[:, :], 0)], P, P, gT[:, :].rearrange("p (a c) -> p a c", a=1))
    for tt in range(2):
        for g in range(4):
            turn("mem", [(mtok[:, tt, (4 * g + k) * P:(4 * g + k + 1) * P], k) for k in range(4)], P, P,
                 memT[:, 4 * g:4 * g + 4, tt * P:(tt + 1) * P])
    for tt in range(2):
        for g in range(4):
            turn("x", [(xtok[:, tt, (4 * g + k) * P:(4 * g + k + 1) * P], k) for k in range(4)], P, P,
                 xT[:, 4 * g:4 * g + 4, tt * P:(tt + 1) * P])
    turn("x", [(stok[0:DEC, k * P:(k + 1) * P], k) for k in range(KT)], P, DEC, xT[:, :, SEQ:N])

    def turn_tokens(name, src, dest):
        for tt in range(2):
            for g in range(2):
                turn(name, [(src[:, 4 * g + k, tt * P:(tt + 1) * P], k) for k in range(4)], P, P,
                     dest[:, tt, g * 512:(g + 1) * 512].rearrange("p (a c) -> p a c", a=4))

    def turn_samples(name, src, dest):
        for g in range(2):
            turn(name, [(src[:, 4 * g + k, SEQ:N], k) for k in range(4)], DEC, P,
                 dest[g * 512:(g + 1) * 512])

    turn_tokens("mem_kv", mkT0, mkTok)
    turn_tokens("mem_kv", mvT0, mvTok0)
    turn_tokens("r", vrT, vrTok)
    turn_tokens("r", krT, krTok)

    class RowDest:
        def __init__(self, t, *ix):
            self.t, self.ix = t, ix

        def __getitem__(self, cols):
            return self.t[(slice(0, DEC), *self.ix, cols)].rearrange("p (a c) -> p a c", a=4)

    turn_samples("r", vrT, RowDest(vrS))
    turn_samples("m", qmT, RowDest(qmS))
    turn_tokens("a", vaT, vaTok)
    turn_tokens("a", kaT, kaTok)
    turn_samples("a", kaT, RowDest(rows, 0))
    turn_samples("a", vaT, RowDest(rows, 1))
    turn_samples("a", qaT, RowDest(rows, 2))
    ytok = at("ytok", [2, D_MODEL], A_MID)
    ystok = at("ystok", [D_MODEL], A_MID + 16384)
    yT = at("yT", [KT, N], A_HID)
    for tt in range(2):
        for g in range(4):
            turn("y", [(yT[:, 4 * g + k, tt * P:(tt + 1) * P], k) for k in range(4)], P, P,
                 ytok[:, tt, g * 512:(g + 1) * 512].rearrange("p (a c) -> p a c", a=4))
    for g in range(4):
        turn("y", [(yT[:, 4 * g + k, SEQ:N], k) for k in range(4)], DEC, P,
             ystok[0:DEC, g * 512:(g + 1) * 512].rearrange("p (a c) -> p a c", a=4))

    def turns_of(name):
        return [(q, t) for q, t in enumerate(turns) if t[0] == name]

    def turns_until(name):
        return turns_of(name)[-1][0] + 1

    def pe_turns(pe, name):
        for q, (_, srcs, rows_out, width, _) in turns_of(name):
            if q >= 2:
                pe.wait_ge(turn_out, q - 1)
            for src, block in srcs:
                n = src.shape[0]
                last = nc.tensor.transpose(PS[0:rows_out, q % 2, block * width:(block + 1) * width],
                                           src, ident[0:n, 0:n])
            last.then_inc(turned, 1)

    def act_turns(act, name):
        for q, (_, srcs, rows_out, width, dest) in turns_of(name):
            act.wait_ge(turned, q + 1)
            nc.scalar.activation(dest, PS[0:rows_out, q % 2, 0:len(srcs) * width].rearrange(
                "p (a c) -> p a c", a=len(srcs)), ACT.Copy).then_inc(turn_out, 1)

    def wait_count(eng, s, n):
        if not (isinstance(n, int) and n <= 0):
            eng.wait_ge(s, n)

    def first_apart(eng, n, body):
        body(0)
        with eng.Fori(1, n) as i:
            body(i)

    def sp_unit_free(sp, B, c, u):
        if not (isinstance(B, int) and B == 0 and c == 0):
            sp.wait_ge(split_ready, 8 * B + 4 * c + u - 3)

    def sp_unit(sp, B, c, u, src):
        sp_unit_free(sp, B, c, u)
        sp_unit_load(sp, u, src)

    def sp_unit_load(sp, u, src):
        nk = src.shape[0] // P
        sp.dma_start(raw[:, u, 0:nk, :], src.rearrange("(k p) c -> p k c", p=P)).then_inc(raw_full[u], 16)

    def sp_wide(sp, B, W, col):
        for c in range(2):
            for u in range(4):
                sp_unit(sp, B, c, u, W[(u % 2) * UK * P:(u % 2 + 1) * UK * P,
                                       bass.ds(col + 512 * c + UC * (u // 2), UC)])

    def sp_ffn(sp, B0, w1, w3, w2):
        B = B0
        for t0, n in FFN_BLOCKS:
            with sp.Fori(0, n // 4) as i:
                for c in range(2):
                    for u in range(4):
                        W = w1 if u < 2 else w3
                        sp_unit(sp, i + B, c, u, W[(u % 2) * UK * P:(u % 2 + 1) * UK * P,
                                                   bass.ds(i * 512 + (t0 * P + UC * c), UC)])
            B += n // 4
            nk = n // 2
            with sp.Fori(0, 2) as i:
                for c in range(2):
                    for u in range(4):
                        k0 = t0 + (u % 2) * nk
                        sp_unit(sp, i + B, c, u, w2[k0 * P:(k0 + nk) * P,
                                                    bass.ds(i * 1024 + (512 * c + UC * (u // 2)), UC)])
            B += 2

    BRANCHES = [("w_br_ret", 1, (orH, orL)), ("w_br_mem", 2, (omH, omL)), ("w_br_moba", 0, (oaH, oaL))]

    def sp_gate_unit(sp, r, i, c, u):
        sp_unit_free(sp, i + (B_GATE + 4 * r), c, u)
        sp_gate_load(sp, r, i, c, u)

    def sp_gate_load(sp, r, i, c, u):
        name, section, _ = BRANCHES[r]
        col = i * 2 * UC + UC * c
        if u < 2:
            src = d["w_gate"][u * UK * P:(u + 1) * UK * P, bass.ds(col + section * D_MODEL, UC)]
        else:
            src = d[name][(u - 2) * 4 * P:(u - 1) * 4 * P, bass.ds(col, UC)]
        sp_unit_load(sp, u, src)

    def sp_page_number(sp, i, c, g):
        return sp.value_load(ptab[0:1, bass.ds(i * 2 * NPAGES + (c * NPAGES + g), 1)],
                             min_val=0, max_val=d["cache_k"].shape[0] - 1)

    def sp_page(sp, values, page, i4, c, g):
        s = g % 4
        n0 = DKA.base // 4 + values * DEC * NPAGES // 4
        sp.wait_ge(kv_used[s], i4 + (n0 + 2 * c + g // 4))
        sp.dma_start(kvA[:, s, :], d["cache_v" if values else "cache_k"][bass.ds(page, 1), :, :].rearrange(
            "a p c -> (a p) c")).then_inc(page_full[s], 16)

    def sp_gates(sp):
        for u in range(4):
            sp_gate_unit(sp, 0, 0, 0, u)
        sp.wait_ge(kept, 96)
        sp.wait_ge(a_lo, A_HEADS + M_HEADS)
        for r in range(2):
            def body(i):
                i4 = i * 4 if isinstance(i, int) else sp.snap(i * 4)
                for c in range(2):
                    if r == 0:
                        sp.wait_ge(kv_used[3], i4 + (DKA.base // 4 + 2 * c - 2))
                        sp.dma_start(qBA[:, c, :], scratch["qa"][bass.ds(i * 2 + c, 1), :].to_broadcast(
                            [P, BR_W])).then_inc(q_in[c], 16)
                    for u in range(4):
                        nr, ni, nc_ = (r, i, 1) if c == 0 else (r + 1, 0, 0) if isinstance(i, int) else (r, i + 1, 0)
                        sp_unit_free(sp, ni + (B_GATE + 4 * nr), nc_, u)
                        pages = [sp_page_number(sp, i, c, 2 * u + j) for j in range(2)]
                        sp_gate_load(sp, nr, ni, nc_, u)
                        sp_page(sp, r, pages[0], i4, c, 2 * u)
                        sp_page(sp, r, pages[1], i4, c, 2 * u + 1)
            with sp.Fori(0, 3) as i:
                body(i)
            body(3)
        for u in range(4):
            sp_gate_unit(sp, 2, 0, 1, u)
        with sp.Fori(1, 4) as i:
            for c in range(2):
                for u in range(4):
                    sp_gate_unit(sp, 2, i, c, u)

    def act_split(act, B, c, u, nk=UK):
        act.wait_ge(raw_full[u], 32 * B + 16 * (c + 1))
        if not (isinstance(B, int) and B == 0 and c == 0 and u < 2):
            act.wait_ge(unit_used, 8 * B + 4 * c + u - 1)
        nc.scalar.activation(splitH[:, u % 2, 0:nk, :], raw[:, u, 0:nk, :], ACT.Copy).then_inc(hi_ready, 1)

    def dve_split(dve, B, c, u, nk=UK):
        dve.wait_ge(hi_ready, 8 * B + 4 * c + u + 1)
        nc.vector.tensor_tensor(splitL[:, u % 2, 0:nk, :], raw[:, u, 0:nk, :],
                                splitH[:, u % 2, 0:nk, :].bitcast(F32), ALU.subtract).then_inc(split_ready, 1)

    def split_body(split, eng, B, evac, nks=(8, 8, 8, 8), last=False):
        for c in range(2):
            split(eng, B, c, 2, nks[2])
            split(eng, B, c, 3, nks[3])
            if not (last and c == 1):
                nB, n_c = (B, 1) if c == 0 else (B + 1, 0)
                split(eng, nB, n_c, 0)
                split(eng, nB, n_c, 1)
            evac(B, c)

    def pe_unit(pe, B, c, u, rhs, tiles, n, start, stop):
        H, L = rhs
        pe.wait_ge(split_ready, 8 * B + 4 * c + u + 1)
        for m in range(2):
            out = PS[:, 4 * c + 2 * (u // 2) + m, 0:n]
            for j, k in enumerate(tiles):
                w_hi = splitH[:, u % 2, j, m * P:(m + 1) * P]
                w_lo = splitL[:, u % 2, j, m * P:(m + 1) * P]
                first, final = start and j == 0, stop and j == len(tiles) - 1
                nc.tensor.matmul(out, w_hi, H[:, k, 0:n], start=first, stop=False)
                nc.tensor.matmul(out, w_hi, L[:, k, 0:n], start=False, stop=False)
                last = nc.tensor.matmul(out, w_lo, H[:, k, 0:n], start=False, stop=final)
        last.then_inc(unit_used, 1)

    def pe_step_free(pe, B, c):
        wait_count(pe, set_free[c], B)

    def pe_drained(pe, B):
        pe.wait_ge(set_free[0], B)
        pe.wait_ge(set_free[1], B)

    def pe_wide(pe, B, rhs, n=N, nk=UK):
        for c in range(2):
            pe_step_free(pe, B, c)
            for u in range(4):
                pe_unit(pe, B, c, u, rhs, range((u % 2) * nk, (u % 2 + 1) * nk), n, u % 2 == 0, u % 2 == 1)

    def pe_ffn(pe, B0):
        B = B0
        for _, n in FFN_BLOCKS:
            pe_drained(pe, B)
            with pe.Fori(0, n // 4) as i:
                pe_wide(pe, i + B, (hH, hL))
            B += n // 4
            pe_drained(pe, B)
            with pe.Fori(0, 2) as i:
                pe_wide(pe, i + B, (hidH, hidL), nk=n // 2)
            B += 2

    def pe_gates(pe, r):
        def body(i):
            for c in range(2):
                B = i + (B_GATE + 4 * r)
                pe_step_free(pe, B, c)
                for u in range(4):
                    if u < 2:
                        pe_unit(pe, B, c, u, (hH, hL), range(u * UK, (u + 1) * UK), N, u == 0, u == 1)
                    else:
                        if r == 1 and u == 2:
                            pe.wait_ge(os_copied, i * 2 + (c + 1))
                        pe_unit(pe, B, c, u, BRANCHES[r][2], range((u - 2) * 4, (u - 1) * 4), N, u == 2, u == 3)
                    if r == 1 and u == 0 and not (isinstance(i, int) and c == 0):
                        pe_sample_end(pe, i, c - 1)
                    if r == 1 and u == 1:
                        pe.wait_ge(set_free[1 - c], B + c)
                        pe_page(pe, i, c, PE_PAGES[0])

        if r == 1:
            first_apart(pe, 4, body)
            pe_sample_end(pe, 3, 1)
        else:
            with pe.Fori(0, 4) as i:
                body(i)

    def pe_page(pe, i, k, g):
        s = g % 4
        pe.wait_ge(page_full[s], i * 64 + 16 * (DEC * NPAGES // 4 + 2 * k + g // 4 + 1))
        for h in range(A_HEADS):
            last = nc.tensor.matmul(
                PS[:, 4 * (1 - k % 2) + 3, h:h + 1], kvA[:, s, h * P:(h + 1) * P],
                DA["L"][:, bass.ds(i * 2 + k, 1), g, h:h + 1].rearrange("p a h -> p (a h)"),
                start=g == PE_PAGES[0] and h == 0, stop=False, skip_group_check=True)
        last.then_inc(kv_used[s], 1)

    def pe_sample_end(pe, i, k):
        pe_page(pe, i, k, PE_PAGES[1])
        pe.wait_ge(kv_used[2], i * 4 + (DKA.base // 4 + DEC * NPAGES // 4 + 2 * k + 2))
        for h in range(A_HEADS):
            last = nc.tensor.matmul(PS[:, 4 * (1 - k % 2) + 3, h:h + 1], pvSum[:, k % 2, h * P:(h + 1) * P],
                                    ones[:, 0:1], start=False, stop=True, skip_group_check=True)
        last.then_inc(sample_summed, 1)

    def step_made(eng, B, c):
        eng.wait_ge(unit_used, 8 * B + 4 * c + 4)

    def ffn_evac_act(act, up0, B0, i):
        def evac(B, c):
            step_made(act, B, c)
            nc.scalar.activation(EV[:, 2 * c:2 * c + 2, :], PS[:, 4 * c:4 * c + 2, 0:N],
                                 ACT.Silu).then_inc(silu_ready, 1)
        return evac

    def ffn_up_evac_dve(dve, up0, i):
        def evac(B, c):
            n = i * 2 + (up0 + c + 1)
            dve.wait_ge(silu_ready, n)
            prod = EV[:, 4 + 2 * c:6 + 2 * c, :]
            nc.vector.tensor_tensor(prod, EV[:, 2 * c:2 * c + 2, :], PS[:, 4 * c + 2:4 * c + 4, 0:N],
                                    ALU.mult).then_inc(prod_ready, 1)
            hi = hidH[:, bass.ds(i * 4 + 2 * c, 2), :]
            dve.wait_ge(prod_ready, n)
            nc.vector.tensor_copy(hi, prod).then_inc(hid_hi, 1)
            dve.wait_ge(hid_hi, n)
            nc.vector.tensor_tensor(hidL[:, bass.ds(i * 4 + 2 * c, 2), :], prod, hi.bitcast(F32),
                                    ALU.subtract).then_inc(set_free[c], 1)
        return evac

    def add_evac_dve(dve, i, scale):
        def evac(B, c):
            step_made(dve, B, c)
            x4 = xT[:, bass.ds(i * 8 + 4 * c, 4), :]
            nc.vector.scalar_tensor_tensor(x4, PS[:, 4 * c:4 * c + 4, 0:N], scale, x4,
                                           ALU.mult, ALU.add).then_inc(set_free[c], 1)
        return evac

    def none(B, c):
        pass

    FFN_UPS = 2 * sum(n // 4 for _, n in FFN_BLOCKS)

    def split_ffn(split, eng, B0, which, final):
        B, ups = B0, which * FFN_UPS
        on_act = split is act_split
        for blk, (_, n) in enumerate(FFN_BLOCKS):
            with eng.Fori(0, n // 4) as i:
                ev = ffn_evac_act(eng, ups, B, i) if on_act else ffn_up_evac_dve(eng, ups, i)
                split_body(split, eng, i + B, ev)
            B += n // 4
            ups += n // 2
            last = final and blk == len(FFN_BLOCKS) - 1
            with eng.Fori(0, 1 if last else 2) as i:
                split_body(split, eng, i + B, none if on_act else add_evac_dve(eng, i, 0.5))
            if last:
                split_body(split, eng, B + 1, none if on_act else add_evac_dve(eng, 1, 0.5), last=True)
            B += 2

    NORMS = {"mem": 0, "ffn1": 1, "mix": 2, "ffn2": 3, "final": 4}

    def norm_args(name):
        return {"mem": (memT, N_MEM, G_MEM), "ffn1": (xT, N, G_FFN1), "mix": (xT, N, G_MIX),
                "ffn2": (xT, N, G_FFN2), "final": (xT, N, G_FINAL)}[name]

    def act_norm(act, name):
        src, n, _ = norm_args(name)
        q = NORMS[name]
        for r in range(4):
            if 4 * q + r >= 2:
                act.wait_ge(sq_used, 4 * q + r - 1)
            nc.scalar.activation(EV[:, 4 * (r % 2):4 * (r % 2) + 4, 0:n], src[:, 4 * r:4 * r + 4, 0:n],
                                 ACT.Square).then_inc(sq_ready, 1)
        act.wait_ge(ms_ready, q + 1)
        nc.scalar.activation(rt[:, 0:n], rs[:, 0:n], ACT.Sqrt).then_inc(sqrt_ready, 1)

    def pe_norm(pe, name):
        _, n, _ = norm_args(name)
        q = NORMS[name]
        for r in range(4):
            pe.wait_ge(sq_ready, 4 * q + r + 1)
            for k in range(4):
                last = nc.tensor.matmul(PS[:, 7, 0:n], ones[:, :], EV[:, 4 * (r % 2) + k, 0:n],
                                        start=r == 0 and k == 0, stop=r == 3 and k == 3)
            last.then_inc(sq_used, 1)

    def refine(link, y, m, t):
        link(nc.vector.tensor_tensor(t, y, y, ALU.mult))
        link(nc.vector.scalar_tensor_tensor(t, t, -0.5, m, ALU.mult, ALU.mult))
        link(nc.vector.scalar_tensor_tensor(y, t, 1.5, y, ALU.add, ALU.mult))

    def dve_norm(dve, link, name, out=None):
        src, n, g = norm_args(name)
        q = NORMS[name]
        dve.wait_ge(sq_used, 4 * q + 4)
        nc.vector.tensor_scalar(rs[:, 0:n], PS[:, 7, 0:n], 1.0 / D_MODEL, EPS, ALU.mult,
                                ALU.add).then_inc(ms_ready, 1)
        dve.wait_ge(sqrt_ready, q + 1)
        link(nc.vector.reciprocal(ry[:, 0:n], rt[:, 0:n]))
        refine(link, ry[:, 0:n], rs[:, 0:n], rt[:, 0:n])
        for r in range(4):
            half = EV[:, 4 * (r % 2):4 * (r % 2) + 4, 0:n] if out is None else out[:, 4 * r:4 * r + 4, 0:n]
            for k in range(4):
                last = nc.vector.scalar_tensor_tensor(half[:, k, :], src[:, 4 * r + k, 0:n],
                                                      gT[:, g + 4 * r + k:g + 4 * r + k + 1],
                                                      ry[:, 0:n], ALU.mult, ALU.mult)
            if out is None:
                link(last)
                hi = hH[:, 4 * r:4 * r + 4, 0:n]
                link(nc.vector.tensor_copy(hi, half))
                last = nc.vector.tensor_tensor(hL[:, 4 * r:4 * r + 4, 0:n], half, hi.bitcast(F32), ALU.subtract)
                if r < 3:
                    link(last)
        last.then_inc(norm_done, 1)

    def pe_retention(pe):
        def att(h):
            if h >= 2:
                pe.wait_ge(att_sb, h - 1)
            for jt in range(2):
                for dt in range(2):
                    last = nc.tensor.matmul(PS[:, 2 + h % 2, jt * SEQ + jt * P:(jt + 1) * SEQ],
                                            krT[:, 2 * h + dt, jt * P:(jt + 1) * P],
                                            qrT[:, 2 * h + dt, jt * P:SEQ], start=dt == 0, stop=dt == 1)
            last.then_inc(att_ps, 1)

        att(0)
        for h in range(R_HEADS):
            if h + 1 < R_HEADS:
                att(h + 1)
            pe.wait_ge(att_sb, h + 1)
            for et in range(2):
                v = lambda jt: vrTok[:, jt, h * R_DV + et * P:h * R_DV + (et + 1) * P]
                nc.tensor.matmul(PS[:, 4, et * SEQ:(et + 1) * SEQ], v(0), attb[:, h % 2, 0, :],
                                 start=True, stop=False)
                last = nc.tensor.matmul(PS[:, 4, et * SEQ + P:(et + 1) * SEQ], v(1), attb[:, h % 2, 1, P:SEQ],
                                        start=False, stop=True)
            last.then_inc(o_ps, 1)
            pe.wait_ge(kd_ready, h + 1)
            if h >= 1:
                pe.wait_ge(s_out, h)
            for dt in range(2):
                for jt in range(2):
                    c0 = h * R_DK + dt * P
                    last = nc.tensor.matmul(PS[:, 6, dt * R_DV:(dt + 1) * R_DV], krTok[:, jt, c0:c0 + P],
                                            vrTok[:, jt, h * R_DV:(h + 1) * R_DV], start=jt == 0, stop=jt == 1)
            last.then_inc(s_ps, 1)
            pe.wait_ge(o_sq, h + 1)
            for et in range(2):
                last = nc.tensor.matmul(PS[:, 5, 0:SEQ], ones[:, :], sqb[:, h % 2, et, :],
                                        start=et == 0, stop=et == 1)
            last.then_inc(ms_ps, 1)
            pe.wait_ge(r_done, h + 1)

    def act_retention(act):
        for h in range(R_HEADS):
            act.wait_ge(o_ps, h + 1)
            nc.scalar.activation(sqb[:, h % 2, :, :], PS[:, 4, :].rearrange("p (a c) -> p a c", a=2),
                                 ACT.Square).then_inc(o_sq, 1)
            act.wait_ge(s_ps, h + 1)
            if h >= 2:
                act.wait_ge(st_sent[h % 2], 16 * (h // 2))
            nc.scalar.activation(st[:, h % 2, :, :], PS[:, 6, :].rearrange("p (a c) -> p a c", a=2),
                                 ACT.Copy).then_inc(s_out, 1)
            act.wait_ge(r_var, h + 1)
            nc.scalar.activation(rt[:, 0:SEQ], rs[:, 0:SEQ], ACT.Sqrt).then_inc(r_sqrt, 1)

    def dve_retention(dve, link):
        def att(h):
            dve.wait_ge(att_ps, h + 1)
            nc.vector.tensor_tensor(attb[:, h % 2, 0, :], PS[:, 2 + h % 2, 0:SEQ], decay[:, h, 0:SEQ], ALU.mult)
            nc.vector.tensor_tensor(attb[:, h % 2, 1, P:SEQ], PS[:, 2 + h % 2, SEQ + P:2 * SEQ],
                                    decay[:, h, SEQ:SEQ + P], ALU.mult).then_inc(att_sb, 1)

        att(0)
        for h in range(R_HEADS):
            for jt in range(2):
                kk = krTok[:, jt, h * R_DK:(h + 1) * R_DK]
                last = nc.vector.tensor_scalar(kk, kk, kdecay[:, h, jt:jt + 1], None, ALU.mult)
            last.then_inc(kd_ready, 1)
            if h + 1 < R_HEADS:
                if h >= 1:
                    dve.wait_ge(o_ps, h)
                att(h + 1)
            dve.wait_ge(ms_ps, h + 1)
            nc.vector.tensor_scalar(rs[:, 0:SEQ], PS[:, 5, 0:SEQ], 1.0 / R_DV, EPS, ALU.mult,
                                    ALU.add).then_inc(r_var, 1)
            dve.wait_ge(r_sqrt, h + 1)
            y = ry[:, 0:SEQ]
            link(nc.vector.reciprocal(y, rt[:, 0:SEQ]))
            refine(link, y, rs[:, 0:SEQ], rt[:, 0:SEQ])
            for et in range(2):
                t = sqb[:, h % 2, et, :]
                link(nc.vector.tensor_tensor(t, PS[:, 4, et * SEQ:(et + 1) * SEQ], y, ALU.mult))
                link(nc.vector.tensor_tensor(t, t, grT[:, 2 * h + et, 0:SEQ], ALU.mult))
                link(nc.vector.tensor_copy(orH[:, 2 * h + et, 0:SEQ], t))
                last = nc.vector.tensor_tensor(orL[:, 2 * h + et, 0:SEQ], t,
                                               orH[:, 2 * h + et, 0:SEQ].bitcast(F32), ALU.subtract)
            last.then_inc(r_done, 1)

    def pool_states(pool):
        def body(i):
            for p in range(2):
                b = i * 2 + p
                wait_count(pool, s_back[p], i * 16)
                wait_count(pool, s_read, i * 2)
                pool.dma_start(state[p][:, :, :, :], d["state_ret"][bass.ds(b, 1), :, :, :].rearrange(
                    "a h (t p) e -> p (a h) t e", p=P)).then_inc(s_in[p], 16)
                pool.dma_start(vB[:, p, :], scratch["vr"][bass.ds(b, 1), :].to_broadcast([P, BR_W])
                               ).then_inc(vb_in[p], 16)

        first_apart(pool, DEC // 2, body)

    def act_states(act):
        with act.Fori(0, DEC // 2) as i:
            for p in range(2):
                act.wait_ge(s_in[p], i * 16 + 16)
                for h in range(R_HEADS):
                    last = nc.scalar.activation(state[p][:, h, :, :], state[p][:, h, :, :], ACT.Copy,
                                                scale=GAMMA[h])
                last.then_inc(s_scaled, 1)
            for p in range(2):
                act.wait_ge(s_new, i * 2 + (p + 1))
                act.dma_start(o["ret_state_sample"][bass.ds(i * 2 + p, 1), :, :, :].rearrange(
                    "a h (t p) e -> p (a h) t e", p=P), state[p][:, :, :, :]).then_inc(s_back[p], 16)

    def dve_states(dve):
        with dve.Fori(0, DEC // 2) as i:
            for p in range(2):
                dve.wait_ge(s_scaled, i * 2 + (p + 1))
                dve.wait_ge(vb_in[p], i * 16 + 16)
                for h in range(R_HEADS):
                    for dt in range(2):
                        s = state[p][:, h, dt, :]
                        last = nc.vector.scalar_tensor_tensor(
                            s, vB[:, p, h * R_DV:(h + 1) * R_DV],
                            krT[:, 2 * h + dt, bass.ds(i * 2 + (SEQ + p), 1)], s, ALU.mult, ALU.add)
                last.then_inc(s_new, 1)
            for p in range(2):
                dve.wait_ge(s_read, i * 2 + (p + 1))
                nc.vector.tensor_copy(orS[:, :, bass.ds(i * 2 + p, 1)],
                                      PS[:, p, 0:BT].rearrange("p (a c) -> p a c", c=1)).then_inc(os_out, 1)

    def pe_states(pe):
        def body(i):
            for p in range(2):
                pe.wait_ge(s_new, i * 2 + (p + 1))
                wait_count(pe, os_out, i * 2)
                for h in range(R_HEADS):
                    for et in range(2):
                        for dt in range(2):
                            last = nc.tensor.matmul(
                                PS[:, p, 2 * h + et:2 * h + et + 1], state[p][:, h, dt, et * P:(et + 1) * P],
                                qrT[:, 2 * h + dt, bass.ds(i * 2 + (SEQ + p), 1)],
                                start=dt == 0, stop=dt == 1)
                last.then_inc(s_read, 1)


        first_apart(pe, DEC // 2, body)

    class Kind:
        def __init__(self, name, heads, dt, et, causal, qT, kT, vtok, oH, oL, scale, q0):
            self.name, self.heads, self.dt, self.et, self.causal = name, heads, dt, et, causal
            self.qT, self.kT, self.vtok, self.oH, self.oL, self.scale = qT, kT, vtok, oH, oL, scale
            self.q0 = q0

        def keys(self, it):
            return P * (it + 1) if self.causal else SEQ

    KA = Kind("A", A_HEADS, 1, 1, True, qaT, kaT, vaTok, oaH, oaL, A_DH ** -0.5, M_HEADS)
    KM = Kind("M", M_HEADS, 2, 2, False, qmT, mkT, mvTok, omH, omL, M_DH ** -0.5, 0)

    def pe_attend(pe, K):
        def scores(h):
            q = K.q0 + h
            if q >= 2:
                pe.wait_ge(a_p, q - 1)
            for it in range(2):
                for dt in range(K.dt):
                    last = nc.tensor.matmul(PS[:, q % 2, it * SEQ:it * SEQ + K.keys(it)],
                                            K.qT[:, K.dt * h + dt, it * P:(it + 1) * P],
                                            K.kT[:, K.dt * h + dt, 0:K.keys(it)],
                                            start=dt == 0, stop=dt == K.dt - 1)
            last.then_inc(a_s, 1)

        def rest(h):
            q = K.q0 + h
            pe.wait_ge(a_norm, q + 1)
            if q >= 2:
                pe.wait_ge(a_ptc, q - 1)
            for it in range(2):
                for jt in range(K.keys(it) // P):
                    last = nc.tensor.transpose(PS[:, 2 + q % 2, jt * SEQ + it * P:jt * SEQ + (it + 1) * P],
                                               sqb[:, q % 2, it, jt * P:(jt + 1) * P], ident[:, :])
            last.then_inc(a_pt, 1)
            pe.wait_ge(a_ptc, q + 1)
            if q >= 2:
                pe.wait_ge(a_lo, q - 1)
            for et in range(K.et):
                c0 = (h * K.et + et) * P
                for jt in range(2):
                    i0 = jt * P if K.causal else 0
                    last = nc.tensor.matmul(PS[:, 4 + q % 2, et * SEQ + i0:(et + 1) * SEQ],
                                            K.vtok[:, jt, c0:c0 + P], attb[:, q % 2, jt, i0:SEQ],
                                            start=jt == 0, stop=jt == 1)
            last.then_inc(a_o, 1)

        scores(0)
        for h in range(K.heads):
            if h + 1 < K.heads:
                scores(h + 1)
            rest(h)

    def dve_attend(dve, link, K):
        def soft(h):
            q = K.q0 + h
            dve.wait_ge(a_s, q + 1)
            if q >= 2:
                dve.wait_ge(a_pt, q - 1)
            if K.causal:
                dve.wait_ge(bias_in[h % 2], 32 * (h // 2 + 1))
            for it in range(2):
                n = K.keys(it)
                s, ps = sqb[:, q % 2, it, 0:n], PS[:, q % 2, it * SEQ:it * SEQ + n]
                if K.causal:
                    last = nc.vector.scalar_tensor_tensor(s, ps, K.scale, bias[:, h % 2, it, 0:n],
                                                          ALU.mult, ALU.add)
                else:
                    last = nc.vector.tensor_scalar(s, ps, K.scale, None, ALU.mult)
            last.then_inc(a_p, 1)
            dve.wait_ge(a_p, q + 1)
            if q >= 2:
                dve.wait_ge(a_norm, q - 1)
            for it in range(2):
                last = nc.vector.tensor_reduce(MX[:, q % 2, 0, it:it + 1], sqb[:, q % 2, it, 0:K.keys(it)],
                                               AX.X, ALU.max, negate=True)
            last.then_inc(a_max, 1)

        def norm(h):
            q = K.q0 + h
            dve.wait_ge(a_exp, q + 1)
            link(nc.vector.reciprocal(MX[:, q % 2, 1, :], MX[:, q % 2, 1, :]))
            for it in range(2):
                s = sqb[:, q % 2, it, 0:K.keys(it)]
                last = nc.vector.tensor_scalar(s, s, MX[:, q % 2, 1, it:it + 1], None, ALU.mult)
            last.then_inc(a_norm, 1)

        def lo(h):
            q = K.q0 + h
            dve.wait_ge(a_hi, q + 1)
            t = slice(K.et * h, K.et * (h + 1))
            nc.vector.tensor_tensor(K.oL[:, t, 0:SEQ], PS[:, 4 + q % 2, 0:K.et * SEQ].rearrange(
                "p (a c) -> p a c", a=K.et), K.oH[:, t, 0:SEQ].bitcast(F32), ALU.subtract).then_inc(a_lo, 1)

        soft(0)
        for h in range(K.heads):
            norm(h)
            if h + 1 < K.heads:
                soft(h + 1)
            lo(h)

    def act_attend(act, K):
        def exps(h):
            q = K.q0 + h
            act.wait_ge(a_max, q + 1)
            for it in range(2):
                s = sqb[:, q % 2, it, 0:K.keys(it)]
                last = nc.scalar.activation(s, s, ACT.Exp, bias=MX[:, q % 2, 0, it:it + 1],
                                            accum_out=MX[:, q % 2, 1, it:it + 1])
            last.then_inc(a_exp, 1)

        def turn_copy(h):
            q = K.q0 + h
            act.wait_ge(a_pt, q + 1)
            if q >= 2:
                act.wait_ge(a_o, q - 1)
            if K.causal:
                nc.scalar.activation(attb[:, q % 2, 0, :], PS[:, 2 + q % 2, 0:SEQ], ACT.Copy)
                last = nc.scalar.activation(attb[:, q % 2, 1, P:SEQ], PS[:, 2 + q % 2, SEQ + P:2 * SEQ], ACT.Copy)
            else:
                last = nc.scalar.activation(attb[:, q % 2, :, :], PS[:, 2 + q % 2, :].rearrange(
                    "p (a c) -> p a c", a=2), ACT.Copy)
            last.then_inc(a_ptc, 1)

        def hi(h):
            q = K.q0 + h
            act.wait_ge(a_o, q + 1)
            nc.scalar.activation(K.oH[:, K.et * h:K.et * (h + 1), 0:SEQ], PS[:, 4 + q % 2, 0:K.et * SEQ].rearrange(
                "p (a c) -> p a c", a=K.et), ACT.Copy).then_inc(a_hi, 1)

        exps(0)
        for h in range(K.heads):
            turn_copy(h)
            if h + 1 < K.heads:
                exps(h + 1)
            hi(h)

    class Decode:
        def __init__(self, name, pages, heads, kv, qB, t, qscr, base, scale, oT, oL):
            self.name, self.pages, self.heads, self.kv, self.qB, self.t = name, pages, heads, kv, qB, t
            self.qscr, self.base, self.scale, self.oH, self.oL = qscr, base, scale, oT, oL
            self.dh = BR_W // heads
            self.et = self.dh // P
            self.q = 1 if name == "A" else 0

    DKM = Decode("M", 2, M_HEADS, kvM, qBM, DM, "qm", 0, M_DH ** -0.5, omH, omL)
    DKA = Decode("A", NPAGES, A_HEADS, kvA, qBA, DA, "qa", 2 * DEC * 2, A_DH ** -0.5, oaH, oaL)

    def pool_decode(pool, K, values):
        def body(i):
            for p in range(2):
                b = i * 2 + p
                if not values:
                    wait_count(pool, kq_ready, i * 2 * K.pages)
                    pool.dma_start(K.qB[:, p, :], scratch[K.qscr][bass.ds(b, 1), :].to_broadcast([P, BR_W])
                                   ).then_inc(qb_in[p], 16)
                for g in range(K.pages):
                    n = p * K.pages + g
                    at_n = K.base + values * DEC * K.pages + n
                    s = n % 4
                    wait_count(pool, kv_used[s], i * (2 * K.pages // 4) + at_n // 4)
                    src = d["cache_mem_v" if values else "cache_mem_k"][
                        bass.ds(b, 1), g * P:(g + 1) * P, :].rearrange("a p c -> (a p) c")
                    pool.dma_start(K.kv[:, s, :], src).then_inc(kv_full[s], 16)

        first_apart(pool, DEC // 2, body)

    def dve_scores(dve, K):
        with dve.Fori(0, DEC // 2) as i:
            for p in range(2):
                dve.wait_ge(qb_in[p], i * 16 + 16)
                for g in range(K.pages):
                    n = p * K.pages + g
                    s = n % 4
                    dve.wait_ge(kv_full[s], i * (16 * (2 * K.pages // 4)) + 16 * ((K.base + n) // 4 + 1))
                    last = nc.vector.tensor_tensor(K.kv[:, s, :], K.kv[:, s, :], K.qB[:, p, :], ALU.mult)
                    last.then_inc(kq_ready, 1)
                    dve.wait_ge(kq_ready, i * 2 * K.pages + (n + 1))
                    nc.vector.tensor_reduce(
                        K.t["S"][:, bass.ds(i * 2 + p, 1), g, :].rearrange("p a h -> p (a h)"),
                        K.kv[:, s, :].rearrange("p (h c) -> p h c", h=K.heads), AX.X, ALU.add
                    ).then_inc(kv_used[s], 1)

    def dve_softmax(dve, link, K):
        t = K.t
        w = DEC * K.heads
        S, L = t["S"], t["L"]
        by = lambda x: x[:, :, :].unsqueeze(2).to_broadcast([P, DEC, K.pages, K.heads])
        if K.name == "A":
            dve.wait_ge(gate_ps, 1)
            g2 = PS[:, 0, 0:DEC * NPAGES * A_HEADS].rearrange("p (b n two h) -> p b n two h", b=DEC, two=2, h=A_HEADS)
            for n in range(N_BLOCKS):
                nc.vector.tensor_copy(t["gate"][:, :, n, :], g2[:, :, n, 0, :])
            link(nc.vector.tensor_copy(t["excl"][:, :, 0, :], g2[:, :, 0, 1, :]))
            for n in range(N_BLOCKS):
                last = nc.vector.tensor_tensor(t["gate"][:, :, n, :], t["gate"][:, :, n, :], g2[:, :, n, 1, :], ALU.add)
            link(last)
            assert N_BLOCKS == MOBA_TOPK + 1
            for n in range(N_BLOCKS):
                first = True
                for m in range(N_BLOCKS):
                    if m == n:
                        continue
                    dst = t["excl"][:, :, n, :] if first else t["cmp"][:, :, :]
                    link(nc.vector.tensor_tensor(dst, t["gate"][:, :, m, :], t["gate"][:, :, n, :],
                                                 ALU.is_ge if m < n else ALU.is_gt))
                    if not first:
                        link(nc.vector.tensor_tensor(t["excl"][:, :, n, :], t["excl"][:, :, n, :],
                                                     t["cmp"][:, :, :], ALU.mult))
                    first = False
            for b in range(DEC):
                last = nc.vector.scalar_tensor_tensor(L[:, b, :, :], S[:, b, :, :], K.scale, biasD[:, :, :],
                                                      ALU.mult, ALU.add)
            link(last)
            for g in range(NPAGES):
                last = nc.vector.scalar_tensor_tensor(L[:, :, g, :], t["excl"][:, :, g * PAGE // MOBA_BLOCK, :],
                                                      NEG_INF, L[:, :, g, :], ALU.mult, ALU.add)
            link(last)
        else:
            link(nc.vector.tensor_scalar(L[:, :, :, :], S[:, :, :, :], K.scale, None, ALU.mult))
        nc.vector.tensor_reduce(t["mp"][:, :, :], L[:, :, :, :].rearrange("p b g h -> p b h g"),
                                AX.X, ALU.max).then_inc(d_max, 1)
        dve.wait_ge(d_maxall, K.q + 1)
        if K.name == "A":
            link(nc.vector.tensor_scalar(t["om"][:, :, :], PS[:, 1, 0:w].rearrange("p (h b) -> p b h", h=A_HEADS),
                                         K.scale, None, ALU.mult))
            link(nc.vector.tensor_tensor(t["om"][:, :, :], t["om"][:, :, :],
                                         bias0[:, :].unsqueeze(1).to_broadcast([P, DEC, A_HEADS]), ALU.add))
            link(nc.vector.tensor_tensor(t["mx"][:, :, :], t["mx"][:, :, :], t["om"][:, :, :], ALU.max))
            link(nc.vector.tensor_tensor(t["om"][:, :, :], t["om"][:, :, :], t["mx"][:, :, :], ALU.subtract))
        for g in range(K.pages):
            last = nc.vector.tensor_tensor(L[:, :, g, :], L[:, :, g, :], t["mx"][:, :, :], ALU.subtract)
        last.then_inc(d_logit, 1)
        dve.wait_ge(d_exp, K.q + 1)
        nc.vector.tensor_reduce(t["se"][:, :, :], L[:, :, :, :].rearrange("p b g h -> p b h g"),
                                AX.X, ALU.add).then_inc(d_sb, 1)
        dve.wait_ge(sum_ps, K.q + 1)
        tot = PS[:, 3, 0:w].rearrange("p (b h) -> p b h", b=DEC)
        if K.name == "A":
            link(nc.vector.tensor_tensor(t["rd"][:, :, :], tot, t["eo"][:, :, :], ALU.add))
        else:
            link(nc.vector.tensor_copy(t["rd"][:, :, :], tot))
        link(nc.vector.reciprocal(t["x1"][:, :, :], t["rd"][:, :, :]))
        for g in range(K.pages):
            last = nc.vector.tensor_tensor(L[:, :, g, :], L[:, :, g, :], t["x1"][:, :, :], ALU.mult)
        last.then_inc(d_prob, 1)

    def act_softmax(act, K):
        act.wait_ge(d_logit, K.q + 1)
        last = nc.scalar.activation(K.t["L"][:, :, :, :], K.t["L"][:, :, :, :], ACT.Exp)
        if K.name == "A":
            last = nc.scalar.activation(K.t["eo"][:, :, :], K.t["om"][:, :, :], ACT.Exp)
        last.then_inc(d_exp, 1)

    def pool_softmax(pool, K):
        pool.wait_ge(d_max, K.q + 1)
        nc.gpsimd.partition_all_reduce(K.t["mx"][:, :, :].rearrange("p b h -> p (b h)"),
                                       K.t["mp"][:, :, :].rearrange("p b h -> p (b h)"), P,
                                       bass.bass_isa.ReduceOp.max).then_inc(d_maxall, 1)

    def pe_softmax(pe, K):
        w = DEC * K.heads
        if K.name == "A":
            pe.wait_ge(s_in_place, DEC)
            nc.tensor.matmul(PS[:, 1, 0:w], ones[:, :], own[:, :, :].rearrange("p h b -> p (h b)"),
                             start=True, stop=True)
            nc.tensor.matmul(PS[:, 0, 0:DEC * K.pages * K.heads], ones[:, :],
                             K.t["S"][:, :, :, :].rearrange("p b g h -> p (b g h)"), start=True, stop=True
                             ).then_inc(gate_ps, 1)
        pe.wait_ge(d_sb, K.q + 1)
        nc.tensor.matmul(PS[:, 3, 0:w], ones[:, :], K.t["se"][:, :, :].rearrange("p b h -> p (b h)"),
                         start=True, stop=True).then_inc(sum_ps, 1)

    def pe_values(pe, K):
        pe.wait_ge(d_prob, K.q + 1)
        def body(i):
            for p in range(2):
                wait_count(pe, d_os, i * 2 + 8 * K.q)
                for g in range(K.pages):
                    n = p * K.pages + g
                    s = n % 4
                    pe.wait_ge(kv_full[s], i * (16 * (2 * K.pages // 4)) + 16 * (
                        (K.base + DEC * K.pages + n) // 4 + 1))
                    for t in range(BT):
                        last = nc.tensor.matmul(
                            PS[:, 4 + p, t:t + 1], K.kv[:, s, t * P:(t + 1) * P],
                            K.t["L"][:, bass.ds(i * 2 + p, 1), g, t // K.et:t // K.et + 1].rearrange("p a h -> p (a h)"),
                            start=g == 0 and t == 0, stop=g == K.pages - 1, skip_group_check=True)
                    last.then_inc(kv_used[s], 1)

        first_apart(pe, DEC // 2, body)

    def dve_values(dve, K):
        s = (2 * K.pages - 1) % 4
        with dve.Fori(0, DEC // 2) as i:
            for p in range(2):
                n = K.base + DEC * K.pages + (p + 1) * K.pages - 1
                dve.wait_ge(kv_used[n % 4], i * (2 * K.pages // 4) + (n // 4 + 1))
                nc.vector.tensor_copy(K.t["oS"][:, :, bass.ds(i * 2 + p, 1)],
                                      PS[:, 4 + p, 0:BT].rearrange("p (a c) -> p a c", c=1)).then_inc(d_os, 1)

    def dve_decode_out(dve, link, K, done):
        t = K.t
        o_s = t["oS"][:, :, :]
        if K.name == "A":
            link(nc.vector.tensor_tensor(t["eo"][:, :, :], t["eo"][:, :, :], t["x1"][:, :, :], ALU.mult))
            link(nc.vector.tensor_tensor(t["o2"][:, :, :], vaS[:, :, :], t["eo"][:, :, :].rearrange("p b h -> p h b"),
                                         ALU.mult))
            link(nc.vector.tensor_tensor(o_s, o_s, t["o2"][:, :, :], ALU.add))
        link(nc.vector.tensor_copy(K.oH[:, :, SEQ:N], o_s))
        nc.vector.tensor_tensor(K.oL[:, :, SEQ:N], o_s, K.oH[:, :, SEQ:N].bitcast(F32),
                                ALU.subtract).then_inc(done, 1)

    def copy_evac(eng, dst, sc=True):
        def evac(B, c):
            step_made(eng, B, c)
            d4 = dst[:, 4 * c:4 * c + 4, :]
            n = d4.shape[-1]
            nc.scalar.activation(d4, PS[:, 4 * c:4 * c + 4, 0:n], ACT.Copy).then_inc(set_free[c], 1)
        return evac

    def silu_evac(eng, dst):
        def evac(B, c):
            step_made(eng, B, c)
            nc.scalar.activation(dst[:, 4 * c:4 * c + 4, :], PS[:, 4 * c:4 * c + 4, 0:N],
                                 ACT.Silu).then_inc(set_free[c], 1)
        return evac

    def rotate_evac(dve, link, dst, scale):
        def evac(B, c):
            step_made(dve, B, c)
            ps = PS[:, 4 * c:4 * c + 4, 0:N].rearrange("p (h two) n -> p h two n", two=2)
            out = dst[:, 4 * c:4 * c + 4, :].rearrange("p (h two) n -> p h two n", two=2)
            for h in range(2):
                e = [EV[:, 4 * h + k, :] for k in range(4)]
                m = lambda dest, half, tab: nc.vector.scalar_tensor_tensor(
                    dest, ps[:, h, half, :], scale, tab[:, :], ALU.mult, ALU.mult)
                m(e[0], 0, cosT)
                m(e[1], 1, sinT)
                m(e[2], 0, sinT)
                link(m(e[3], 1, cosT))
                nc.vector.tensor_tensor(out[:, h, 0, :], e[0], e[1], ALU.subtract)
                last = nc.vector.tensor_tensor(out[:, h, 1, :], e[2], e[3], ALU.add)
                if h == 0:
                    link(last)
            last.then_inc(set_free[c], 1)
        return evac

    def gate_evac_act(act, i, r):
        def evac(B, c):
            step_made(act, B, c)
            for m in range(2):
                g = bass.ds(i * 4 + (G_BIAS + KT * BRANCHES[r][1] + 2 * c + m), 1)
                last = nc.scalar.activation(EV[:, 2 * c + m, :], PS[:, 4 * c + m, 0:N], ACT.Sigmoid,
                                            bias=gT[:, g])
            last.then_inc(sig_ready, 1)
        return evac

    def gate_evac_dve(dve, i, r):
        def evac(B, c):
            acc = accT[:, bass.ds(i * 4 + 2 * c, 2), :]
            gate, proj = EV[:, 2 * c:2 * c + 2, :], PS[:, 4 * c + 2:4 * c + 4, 0:N]
            dve.wait_ge(sig_ready, i * 2 + (8 * r + c + 1))
            if r == 0:
                nc.vector.tensor_tensor(acc, gate, proj, ALU.mult).then_inc(set_free[c], 1)
                return
            done = i * 2 + c if r == 1 else i * 6 + (8 + 3 * c)
            wait_count(dve, merge_step, done)
            nc.vector.tensor_tensor(EV[:, 6:8, :], gate, proj, ALU.mult).then_inc(set_free[c], 1)
            dve.wait_ge(set_free[c], B + 1)
            nc.vector.tensor_tensor(acc, acc, EV[:, 6:8, :], ALU.add).then_inc(merge_step, 1)
            if r == 2:
                hi = mgH[:, bass.ds(i * 4 + 2 * c, 2), :]
                dve.wait_ge(merge_step, done + 1)
                nc.vector.tensor_copy(hi, acc).then_inc(merge_step, 1)
                dve.wait_ge(merge_step, done + 2)
                nc.vector.tensor_tensor(mgL[:, bass.ds(i * 4 + 2 * c, 2), :], acc,
                                        hi.bitcast(F32), ALU.subtract).then_inc(merge_step, 1)
        return evac

    def dve_page(dve, i, c, g):
        s = g % 4
        n0 = DKA.base // 4
        if g == 0:
            dve.wait_ge(q_in[c], i * 16 + 16)
            wait_count(dve, s_in_place, i * 2 + (c - 1))
        dve.wait_ge(page_full[s], i * 64 + 16 * (2 * c + g // 4 + 1))
        for h in range(A_HEADS):
            k = kvA[:, s, h * P:(h + 1) * P]
            last = nc.vector.tensor_tensor_reduce(k, k, qBA[:, c, h * P:(h + 1) * P], 1.0, 0.0,
                                                  ALU.mult, ALU.add, Sb[:, c, g, h:h + 1])
        last.then_inc(kv_used[s], 1)
        if g == NPAGES - 1:
            dve.wait_ge(kv_used[s], i * 4 + (n0 + 2 * c + 2))
            nc.vector.tensor_copy(DA["S"][:, bass.ds(i * 2 + c, 1), :, :], Sb[:, c:c + 1, :, :]
                                  ).then_inc(s_in_place, 1)

    def dve_value_page(dve, i, c, g):
        s = g % 4
        n0 = DKA.base // 4 + DEC * NPAGES // 4
        if g == 0:
            nc.vector.tensor_copy(Sb[:, c:c + 1, :, :], DA["L"][:, bass.ds(i * 2 + c, 1), :, :]
                                  ).then_inc(p_in_place, 1)
            dve.wait_ge(p_in_place, i * 2 + (c + 1))
        else:
            before = DVE_PAGES[DVE_PAGES.index(g) - 1]
            dve.wait_ge(kv_used[before % 4], i * 4 + (n0 + 2 * c + before // 4 + 1))
        dve.wait_ge(page_full[s], i * 64 + 16 * (DEC * NPAGES // 4 + 2 * c + g // 4 + 1))
        if g == 0:
            last = nc.vector.tensor_tensor(
                pvSum[:, c, :].rearrange("p (h e) -> p h e", h=A_HEADS),
                kvA[:, s, :].rearrange("p (h e) -> p h e", h=A_HEADS),
                Sb[:, c, g, :].unsqueeze(2).to_broadcast([P, A_HEADS, P]), ALU.mult)
        else:
            for h in range(A_HEADS):
                acc = pvSum[:, c, h * P:(h + 1) * P]
                last = nc.vector.scalar_tensor_tensor(acc, kvA[:, s, h * P:(h + 1) * P], Sb[:, c, g, h:h + 1],
                                                      acc, ALU.mult, ALU.add)
        last.then_inc(kv_used[s], 1)

    def dve_sample_out(dve, i, k):
        dve.wait_ge(sample_summed, i * 2 + (k + 1))
        nc.vector.tensor_copy(DA["oS"][:, :, bass.ds(i * 2 + k, 1)],
                              PS[:, 4 * (1 - k % 2) + 3, 0:BT].rearrange("p (a c) -> p a c", c=1)
                              ).then_inc(os_copied, 1)

    def split_gates(split, eng, r):
        on_act = split is act_split

        def body(i):
            B = i + (B_GATE + 4 * r)
            for c in range(2):
                nB, n_c = (B, 1) if c == 0 else (B + 1, 0)
                for j, (b, cc, u, nk) in enumerate(((B, c, 2, 4), (B, c, 3, 4), (nB, n_c, 0, UK), (nB, n_c, 1, UK))):
                    split(eng, b, cc, u, nk)
                    if not on_act and r == 0:
                        dve_page(eng, i, c, 2 * j)
                        dve_page(eng, i, c, 2 * j + 1)
                    if not on_act and r == 1:
                        if j == 0 and not (isinstance(i, int) and c == 0):
                            dve_sample_out(eng, i, c - 1)
                        for g in ((0, 1), (2,), (4, 5), (6,))[j]:
                            dve_value_page(eng, i, c, g)
                (gate_evac_act if on_act else gate_evac_dve)(eng, i, r)(B, c)

        if on_act or r == 2:
            with eng.Fori(0, 4) as i:
                body(i)
        else:
            first_apart(eng, 4, body)
            if r == 1:
                dve_sample_out(eng, 3, 1)

    class Link:

        def __init__(self, eng, s):
            self.eng, self.s, self.n = eng, s, 0

        def __call__(self, inst):
            self.n += 1
            inst.then_inc(self.s, 1)
            self.eng.wait_ge(self.s, self.n)
            return inst

    @block.sync
    def _(sp):
        sp.dma_start(ident[:, :], d["ident"]).then_inc(ident_in, 16)
        for k, name in enumerate(("ffn1_norm", "mix_norm", "mem_norm", "ffn2_norm", "final_norm")):
            sp.dma_start(grow[KT * k:KT * (k + 1), :], d[name].rearrange("(k p) -> k p", p=P)).then_inc(gain_in, 16)
        sp.dma_start(grow[G_BIAS:P, :], d["b_gate"].rearrange("(k p) -> k p", p=P)).then_inc(gain_in, 16)
        sp.dma_start(mtok[:, :, :], d["mem_prompt"].rearrange("(t p) c -> p t c", p=P)).then_inc(mem_in, 16)
        sp.dma_start(xtok[:, :, :], d["x_prompt"].rearrange("(t p) c -> p t c", p=P)).then_inc(x_in, 16)
        sp.dma_start(stok[0:DEC, :], d["x_sample"]).then_inc(x_in, 16)
        sp_wide(sp, 0, d["w_mem_kv"], 0)
        sp_wide(sp, 1, d["w_mem_kv"], BR_W)
        sp_ffn(sp, B_FFN1, d["ffn1_w1"], d["ffn1_w3"], d["ffn1_w2"])
        with sp.Fori(0, 4) as i:
            sp_wide(sp, i + B_IN_R, d["w_in"], i * BR_W + C_QR)
        sp_wide(sp, B_IN_M, d["w_in"], C_QM)
        with sp.Fori(0, 3) as i:
            sp_wide(sp, i + B_IN_A, d["w_in"], i * BR_W + C_QA)
        sp.wait_ge(pt_in, 16)
        sp_gates(sp)
        with sp.Fori(0, 2) as i:
            sp_wide(sp, i + B_OUT, d["w_out"], i * BR_W)
        sp_ffn(sp, B_FFN2, d["ffn2_w1"], d["ffn2_w3"], d["ffn2_w2"])
        y0 = turns_of("y")[0][0]
        sp.wait_ge(turn_out, y0 + 8)
        sp.dma_start(o["y_prompt"].rearrange("(t p) c -> p t c", p=P), ytok[:, :, :]).then_inc(y_sent, 16)
        sp.wait_ge(turn_out, y0 + 12)
        sp.dma_start(o["y_sample"], ystok[0:DEC, :]).then_inc(y_sent, 16)
        sp.wait_ge(y_sent, 32)

    @block.gpsimd
    def _(pool):
        nc.gpsimd.memset(ones[:, :], 1.0).then_inc(ones_set, 1)
        pool.dma_start(ptab[0:1, :], d["page_table"]).then_inc(pt_in, 16)
        pool.wait_ge(pt_in, 16)
        pool.wait_ge(turn_out, turns_until("mem_kv"))
        pool.dma_start(o["mem_k_prompt"].rearrange("(t p) c -> p t c", p=P), mkTok[:, :, :]).then_inc(stored, 16)
        pool.dma_start(o["mem_v_prompt"].rearrange("(t p) c -> p t c", p=P), mvTok0[:, :, :]).then_inc(stored, 16)
        pool.dma_start(scratch["mv"].rearrange("(t p) c -> p t c", p=P), mvTok0[:, :, :]).then_inc(kept, 16)
        pool.dma_start(scratch["mkT"], mkT0[:, :, :].rearrange("p a c -> p (a c)")).then_inc(kept, 16)
        pool.wait_ge(kept, 32)
        pool.wait_ge(stored, 32)
        pool.wait_ge(set_free[0], B_IN)
        pool.wait_ge(set_free[1], B_IN)
        pool.dma_start(scratch["x"], xT[:, :, :].rearrange("p a c -> p (a c)")).then_inc(x_kept, 16)
        pool.dma_start(cosT[:, :], d["cos"]).then_inc(rot_in, 16)
        pool.dma_start(sinT[:, :], d["sin"]).then_inc(rot_in, 16)
        pool.dma_start(kdecay[:, :, :], d["kdecay"]).then_inc(decay_in, 16)
        pool.dma_start(decay[:, :, :], d["decay"]).then_inc(decay_in, 16)
        pool.wait_ge(turn_out, turns_until("r"))
        pool.dma_start(scratch["vr"], vrS[0:DEC, :]).then_inc(kept, 16)
        pool.wait_ge(kept, 48)
        for h in range(R_HEADS):
            pool.wait_ge(s_out, h + 1)
            pool.dma_start(o["ret_state_prompt"][h].rearrange("(t p) e -> p t e", p=P),
                           st[:, h % 2, :, :]).then_inc(st_sent[h % 2], 16)
        pool.wait_ge(st_sent[0], 32)
        pool.wait_ge(st_sent[1], 32)
        pool.wait_ge(r_done, R_HEADS)
        pool_states(pool)
        pool.wait_ge(s_back[0], 64)
        pool.wait_ge(s_back[1], 64)
        pool.wait_ge(r_all_done, 1)
        pool.dma_start(mkT[:, :, :].rearrange("p a c -> p (a c)"), scratch["mkT"]).then_inc(mk_in, 16)
        pool.dma_start(mvTok[:, :, :], scratch["mv"].rearrange("(t p) c -> p t c", p=P)).then_inc(mk_in, 16)
        pool.wait_ge(turn_out, turns_until("m"))
        pool.dma_start(scratch["qm"], qmS[0:DEC, :]).then_inc(kept, 16)
        pool.wait_ge(kept, 64)
        pool.wait_ge(a_lo, M_HEADS)
        pool_decode(pool, DKM, 0)
        pool_softmax(pool, DKM)
        pool_decode(pool, DKM, 1)
        pool.wait_ge(m_done, 1)
        pool.dma_start(t5w[0:T5_BUCKETS, :], d["t5_table"]).then_inc(t5_in, 16)
        pool.dma_start(bkp[0:T5_BUCKETS, :], d["bucket_prompt"]).then_inc(t5_in, 16)
        pool.dma_start(bkd[0:T5_BUCKETS, :], d["bucket_decode"]).then_inc(t5_in, 16)
        pool.wait_ge(t5_ready, 1)
        pool.dma_start(scratch["t5"], t5row[0:A_HEADS, :].unsqueeze(1).to_broadcast([A_HEADS, P, 2 * SEQ])
                       ).then_inc(kept, 16)
        pool.wait_ge(kept, 80)
        pool.wait_ge(turn_out, turns_until("a"))
        pool.dma_start(o["v_prompt"].rearrange("(t p) c -> p t c", p=P), vaTok[:, :, :]).then_inc(stored, 16)
        pool.dma_start(o["k_prompt"].rearrange("(t p) c -> p t c", p=P), kaTok[:, :, :]).then_inc(stored, 16)
        pool.dma_start(o["k_sample"], rows[0:DEC, 0, :]).then_inc(stored, 16)
        pool.dma_start(o["v_sample"], rows[0:DEC, 1, :]).then_inc(stored, 16)
        pool.dma_start(scratch["qa"], rows[0:DEC, 2, :]).then_inc(kept, 16)
        for h in range(A_HEADS):
            if h >= 2:
                pool.wait_ge(a_p, M_HEADS + h - 1)
            for it in range(2):
                diag = bass.AP(tensor=scratch["t5"].tensor, offset=h * P * 2 * SEQ + SEQ - 1 - it * P,
                               ap=[[2 * SEQ - 1, P], [1, SEQ]])
                pool.dma_start(bias[:, h % 2, it, :], diag).then_inc(bias_in[h % 2], 16)
        pool.wait_ge(kept, 96)
        pool.wait_ge(stored, 96)
        pool_softmax(pool, DKA)
        pool.wait_ge(merge_step, 8 + 3 * 8)
        pool.dma_start(xT[:, :, :].rearrange("p a c -> p (a c)"), scratch["x"]).then_inc(x_back, 16)
        pool.wait_ge(x_back, 16)

    @block.tensor
    def _(pe):
        pe.wait_ge(ident_in, 16)
        pe.wait_ge(gain_in, 96)
        pe_turns(pe, "gain")
        pe.wait_ge(mem_in, 16)
        pe_turns(pe, "mem")
        pe.wait_ge(x_in, 32)
        pe_turns(pe, "x")
        pe.wait_ge(ones_set, 1)
        pe_norm(pe, "mem")
        pe.wait_ge(norm_done, 1)
        pe.wait_ge(turn_out, turns_until("x"))
        pe_wide(pe, 0, (hH, hL), N_MEM)
        pe_wide(pe, 1, (hH, hL), N_MEM)
        pe_drained(pe, 2)
        pe_turns(pe, "mem_kv")
        pe.wait_ge(turn_out, turns_until("mem_kv"))
        pe_norm(pe, "ffn1")
        pe.wait_ge(norm_done, 2)
        pe_ffn(pe, B_FFN1)
        pe_drained(pe, B_IN)
        pe_norm(pe, "mix")
        pe.wait_ge(norm_done, 3)
        with pe.Fori(0, 4) as i:
            pe_wide(pe, i + B_IN_R, (hH, hL))
        pe_drained(pe, B_IN_M)
        pe_turns(pe, "r")
        pe.wait_ge(turn_out, turns_until("r"))
        pe_retention(pe)
        pe.wait_ge(s_out, R_HEADS)
        pe_states(pe)
        pe.wait_ge(samp_sq, 1)
        for et in range(2):
            last = nc.tensor.matmul(PS[:, 5, 0:R_HEADS * DEC], ones[:, :],
                                    orS2[:, et:BT:2, :], start=et == 0, stop=et == 1)
        last.then_inc(samp_ms, 1)
        pe.wait_ge(r_all_done, 1)
        pe_wide(pe, B_IN_M, (hH, hL))
        pe_drained(pe, B_IN_A)
        pe_turns(pe, "m")
        pe.wait_ge(turn_out, turns_until("m"))
        pe.wait_ge(mk_in, 32)
        pe_attend(pe, KM)
        pe.wait_ge(a_lo, M_HEADS)
        pe_softmax(pe, DKM)
        pe_values(pe, DKM)
        pe.wait_ge(m_done, 1)
        with pe.Fori(0, 3) as i:
            pe_wide(pe, i + B_IN_A, (hH, hL))
        pe_drained(pe, B_GATE)
        pe.wait_ge(t5_in, 48)
        nc.tensor.matmul(PS[0:A_HEADS, 3, 0:SEQ], t5w[0:T5_BUCKETS, :], bkp[0:T5_BUCKETS, :], start=True, stop=True)
        for g in range(NPAGES):
            nc.tensor.matmul(PS[:, 2, A_HEADS * g:A_HEADS * (g + 1)], bkd[0:T5_BUCKETS, g * P:(g + 1) * P],
                             t5w[0:T5_BUCKETS, :], start=True, stop=True)
        nc.tensor.matmul(PS[:, 2, 64:64 + A_HEADS], ones[0:1, :], t5w[0:1, :],
                         start=True, stop=True).then_inc(t5_ps, 1)
        pe_turns(pe, "a")
        pe.wait_ge(turn_out, turns_until("a"))
        pe.wait_ge(own_ready, 1)
        pe_attend(pe, KA)
        pe.wait_ge(a_lo, M_HEADS + A_HEADS)
        pe_gates(pe, 0)
        pe_drained(pe, B_GATE + 4)
        pe_softmax(pe, DKA)
        pe.wait_ge(d_prob, 2)
        pe_gates(pe, 1)
        pe.wait_ge(a_done, 1)
        pe_gates(pe, 2)
        pe_drained(pe, B_OUT)
        pe.wait_ge(merge_step, 8 + 3 * 8)
        with pe.Fori(0, 2) as i:
            pe_wide(pe, i + B_OUT, (mgH, mgL))
        pe_drained(pe, B_FFN2)
        pe_norm(pe, "ffn2")
        pe.wait_ge(norm_done, 4)
        pe_ffn(pe, B_FFN2)
        pe_drained(pe, B_END)
        pe_norm(pe, "final")
        pe.wait_ge(norm_done, 5)
        pe_turns(pe, "y")

    @block.scalar
    def _(act):
        act_turns(act, "gain")
        act_turns(act, "mem")
        act_turns(act, "x")
        act.wait_ge(turn_out, turns_until("x"))
        act_norm(act, "mem")
        act_split(act, 0, 0, 0)
        act_split(act, 0, 0, 1)
        split_body(act_split, act, 0, copy_evac(act, mkT0))
        split_body(act_split, act, 1, copy_evac(act, mvT0))
        act_turns(act, "mem_kv")
        act_norm(act, "ffn1")
        split_ffn(act_split, act, B_FFN1, 0, False)
        act.wait_ge(set_free[0], B_IN)
        act.wait_ge(set_free[1], B_IN)
        act_norm(act, "mix")
        act.wait_ge(stored, 32)
        act.wait_ge(kept, 32)
        split_body(act_split, act, B_IN_R, none)
        split_body(act_split, act, B_IN_R + 1, none)
        split_body(act_split, act, B_IN_R + 2, copy_evac(act, vrT))
        split_body(act_split, act, B_IN_R + 3, silu_evac(act, grT))
        act_turns(act, "r")
        act.wait_ge(kept, 48)
        act_retention(act)
        act_states(act)
        act.wait_ge(samp_var, 1)
        nc.scalar.activation(rt[:, 0:R_HEADS * DEC], rs[:, 0:R_HEADS * DEC], ACT.Sqrt).then_inc(samp_sqrt, 1)
        act.wait_ge(r_all_done, 1)
        split_body(act_split, act, B_IN_M, copy_evac(act, qmT))
        act_turns(act, "m")
        act_attend(act, KM)
        act_softmax(act, DKM)
        act.wait_ge(m_done, 1)
        act.wait_ge(s_back[0], 64)
        act.wait_ge(s_back[1], 64)
        split_body(act_split, act, B_IN_A, copy_evac(act, qaT))
        split_body(act_split, act, B_IN_A + 1, copy_evac(act, kaT))
        split_body(act_split, act, B_IN_A + 2, copy_evac(act, vaT))
        act.wait_ge(kept, 80)
        act.wait_ge(x_kept, 16)
        act_turns(act, "a")
        act_attend(act, KA)
        split_gates(act_split, act, 0)
        act_softmax(act, DKA)
        split_gates(act_split, act, 1)
        split_gates(act_split, act, 2)
        with act.Fori(0, 2) as i:
            split_body(act_split, act, i + B_OUT, none)
        act.wait_ge(set_free[0], B_FFN2)
        act.wait_ge(set_free[1], B_FFN2)
        act_norm(act, "ffn2")
        split_ffn(act_split, act, B_FFN2, 1, True)
        act.wait_ge(set_free[0], B_END)
        act.wait_ge(set_free[1], B_END)
        act_norm(act, "final")
        act_turns(act, "y")

    @block.vector
    def _(dve):
        link = Link(dve, dve_link)
        dve.wait_ge(turn_out, turns_until("x"))
        dve_norm(dve, link, "mem")
        dve_split(dve, 0, 0, 0)
        dve_split(dve, 0, 0, 1)
        split_body(dve_split, dve, 0, none)
        split_body(dve_split, dve, 1, none)
        dve_norm(dve, link, "ffn1")
        split_ffn(dve_split, dve, B_FFN1, 0, False)
        dve.wait_ge(set_free[0], B_IN)
        dve.wait_ge(set_free[1], B_IN)
        dve_norm(dve, link, "mix")
        dve.wait_ge(rot_in, 32)
        dve.wait_ge(stored, 32)
        dve.wait_ge(kept, 32)
        split_body(dve_split, dve, B_IN_R, rotate_evac(dve, link, qrT, 1.0))
        split_body(dve_split, dve, B_IN_R + 1, rotate_evac(dve, link, krT, R_DK ** -0.5))
        split_body(dve_split, dve, B_IN_R + 2, none)
        split_body(dve_split, dve, B_IN_R + 3, none)
        dve.wait_ge(decay_in, 32)
        dve.wait_ge(turn_out, turns_until("r"))
        dve_retention(dve, link)
        dve_states(dve)
        dve.wait_ge(os_out, DEC)
        dve.wait_ge(s_back[0], 64)
        dve.wait_ge(s_back[1], 64)
        w = R_HEADS * DEC
        nc.vector.tensor_tensor(orS2[:, :, :], orS[:, :, :], orS[:, :, :], ALU.mult).then_inc(samp_sq, 1)
        dve.wait_ge(samp_ms, 1)
        nc.vector.tensor_scalar(rs[:, 0:w], PS[:, 5, 0:w], 1.0 / R_DV, EPS, ALU.mult, ALU.add).then_inc(samp_var, 1)
        dve.wait_ge(samp_sqrt, 1)
        link(nc.vector.reciprocal(ry[:, 0:w], rt[:, 0:w]))
        refine(link, ry[:, 0:w], rs[:, 0:w], rt[:, 0:w])
        for et in range(2):
            last = nc.vector.tensor_tensor(orS2[:, et:BT:2, :], orS[:, et:BT:2, :],
                                           ry[:, 0:w].rearrange("p (h b) -> p h b", h=R_HEADS), ALU.mult)
        link(last)
        link(nc.vector.tensor_tensor(orS2[:, :, :], orS2[:, :, :], grT[:, :, SEQ:N], ALU.mult))
        link(nc.vector.tensor_copy(orH[:, :, SEQ:N], orS2[:, :, :]))
        nc.vector.tensor_tensor(orL[:, :, SEQ:N], orS2[:, :, :], orH[:, :, SEQ:N].bitcast(F32),
                                ALU.subtract).then_inc(r_all_done, 1)
        split_body(dve_split, dve, B_IN_M, none)
        dve_attend(dve, link, KM)
        dve_scores(dve, DKM)
        for s in range(4):
            dve.wait_ge(kv_used[s], DEC * 2 // 4)
        dve_softmax(dve, link, DKM)
        dve_values(dve, DKM)
        dve.wait_ge(d_os, DEC)
        dve_decode_out(dve, link, DKM, m_done)
        for k in range(3):
            split_body(dve_split, dve, B_IN_A + k, none)
        dve.wait_ge(t5_ps, 1)
        nc.vector.memset(t5row[0:A_HEADS, SEQ:2 * SEQ], NEG_INF)
        nc.vector.tensor_copy(biasD[:, :, :].rearrange("p g h -> p (g h)"), PS[:, 2, 0:64])
        nc.vector.tensor_copy(bias0[:, :], PS[:, 2, 64:64 + A_HEADS])
        nc.vector.tensor_copy(t5row[0:A_HEADS, 0:SEQ], PS[0:A_HEADS, 3, 0:SEQ]).then_inc(t5_ready, 1)
        nc.vector.tensor_copy(vaS[:, :, :], vaT[:, :, SEQ:N])
        nc.vector.tensor_tensor(own[:, :, :], qaT[:, :, SEQ:N], kaT[:, :, SEQ:N], ALU.mult).then_inc(own_ready, 1)
        dve.wait_ge(kept, 96)
        dve.wait_ge(stored, 96)
        dve_attend(dve, link, KA)
        dve.wait_ge(x_kept, 16)
        split_gates(dve_split, dve, 0)
        dve.wait_ge(s_in_place, DEC)
        dve_softmax(dve, link, DKA)
        nc.vector.memset(DA["oS"][:, :, :], 0.0).then_inc(os_copied, 1)
        dve.wait_ge(os_copied, 1)
        split_gates(dve_split, dve, 1)
        dve.wait_ge(os_copied, DEC + 1)
        dve_decode_out(dve, link, DKA, a_done)
        split_gates(dve_split, dve, 2)
        dve.wait_ge(x_back, 16)
        with dve.Fori(0, 2) as i:
            split_body(dve_split, dve, i + B_OUT, add_evac_dve(dve, i, 1.0))
        dve.wait_ge(set_free[0], B_FFN2)
        dve.wait_ge(set_free[1], B_FFN2)
        dve_norm(dve, link, "ffn2")
        split_ffn(dve_split, dve, B_FFN2, 1, True)
        dve.wait_ge(set_free[0], B_END)
        dve.wait_ge(set_free[1], B_END)
        dve_norm(dve, link, "final", yT)


_INS = {
    "x_prompt": (SEQ, D_MODEL), "x_sample": (DEC, D_MODEL), "mem_prompt": (N_MEM, D_MODEL),
    "cache_k": (-1, PAGE, BR_W), "cache_v": (-1, PAGE, BR_W),
    "cache_mem_k": (DEC, N_MEM, BR_W), "cache_mem_v": (DEC, N_MEM, BR_W),
    "state_ret": (DEC, R_HEADS, R_DK, R_DV), "page_table": (1, DEC * NPAGES), "t5_table": (T5_BUCKETS, A_HEADS),
    "ffn1_norm": (D_MODEL,), "ffn1_w1": (D_MODEL, D_FF), "ffn1_w3": (D_MODEL, D_FF), "ffn1_w2": (D_FF, D_MODEL),
    "mix_norm": (D_MODEL,), "mem_norm": (D_MODEL,), "w_in": (D_MODEL, 8 * BR_W), "w_mem_kv": (D_MODEL, 2 * BR_W),
    "w_gate": (D_MODEL, 3 * D_MODEL), "b_gate": (3 * D_MODEL,), "w_br_moba": (BR_W, D_MODEL),
    "w_br_ret": (BR_W, D_MODEL), "w_br_mem": (BR_W, D_MODEL), "w_out": (D_MODEL, D_MODEL),
    "ffn2_norm": (D_MODEL,), "ffn2_w1": (D_MODEL, D_FF), "ffn2_w3": (D_MODEL, D_FF), "ffn2_w2": (D_FF, D_MODEL),
    "final_norm": (D_MODEL,),
}
_OUTS = {
    "y_prompt": ((SEQ, D_MODEL), (1, SEQ, D_MODEL)), "y_sample": ((DEC, D_MODEL), (DEC, 1, D_MODEL)),
    "k_prompt": ((SEQ, BR_W), (1, 1, SEQ, A_HEADS, A_DH)), "v_prompt": ((SEQ, BR_W), (1, 1, SEQ, A_HEADS, A_DH)),
    "mem_k_prompt": ((N_MEM, BR_W), (1, 1, N_MEM, M_HEADS, M_DH)),
    "mem_v_prompt": ((N_MEM, BR_W), (1, 1, N_MEM, M_HEADS, M_DH)),
    "ret_state_prompt": ((R_HEADS, R_DK, R_DV), (1, 1, R_HEADS, R_DK, R_DV)),
    "k_sample": ((DEC, BR_W), (1, DEC, 1, A_HEADS, A_DH)), "v_sample": ((DEC, BR_W), (1, DEC, 1, A_HEADS, A_DH)),
    "ret_state_sample": ((DEC, R_HEADS, R_DK, R_DV), (1, DEC, R_HEADS, R_DK, R_DV)),
}


def kernel(**inputs):
    from contextlib import ExitStack
    import concourse.bacc as bacc
    from concourse.bass_utils import run_bass_kernel_spmd

    nc = bacc.Bacc("TRN2", target_bir_lowering=False, num_devices=1)
    arrays = {n: np.ascontiguousarray(inputs[n]).reshape(s) for n, s in _INS.items()}
    arrays.update(constants())
    d = {n: nc.dram_tensor(n, a.shape, mybir.dt.from_np(a.dtype), kind="ExternalInput").ap()
         for n, a in arrays.items()}
    o = {n: nc.dram_tensor(f"out_{n}", s, F32, kind="ExternalOutput").ap() for n, (s, _) in _OUTS.items()}
    with ExitStack() as ctx:
        PS = ctx.enter_context(nc.psum_tensor("PS", [P, 8, 512], F32))
        build(nc, d, o, lambda name: ctx.enter_context(nc.semaphore(name)), PS,
              ctx.enter_context(nc.Block()))
    r = run_bass_kernel_spmd(nc, [arrays], core_ids=[0])
    return tuple(r.results[0][f"out_{n}"].reshape(s) for n, (_, s) in _OUTS.items())
```

```python
import numpy as np
import concourse.bass as bass
import concourse.mybir as mybir

F32 = mybir.dt.float32
F32R = mybir.dt.float32r
I32 = mybir.dt.int32
ALU = mybir.AluOpType
ACT = mybir.ActivationFunctionType
AX = mybir.AxisListType

P = 128
D_MODEL, SEQ, DEC, PAST, PAGE = 2048, 256, 8, 1024, 128
A_HEADS, A_DH, MOBA_BLOCK, MOBA_TOPK, T5_BUCKETS, T5_MAX_DIST = 8, 128, 256, 3, 32, 128
R_HEADS, R_DK, R_DV, ROPE_BASE = 4, 256, 256, 10000.0
M_HEADS, M_DH, N_MEM = 4, 256, 256
BR_W = 1024
D_FF, EPS, NEG_INF = 5632, 1e-6, -1e30
N = SEQ + DEC
KT = D_MODEL // P
BT = BR_W // P
UK, UC = 8, 256
NPAGES = PAST // PAGE
N_BLOCKS = PAST // MOBA_BLOCK
HID = 16
FFN_BLOCKS = [(0, 16), (16, 16), (32, 12)]

B_MEM = 0
B_FFN1 = B_MEM + 2
FFN_BODIES = sum(n // 4 + 2 for _, n in FFN_BLOCKS)
B_IN = B_FFN1 + FFN_BODIES
B_IN_R, B_IN_M, B_IN_A = B_IN, B_IN + 4, B_IN + 5
B_GATE = B_IN + 8
B_OUT = B_GATE + 12
B_FFN2 = B_OUT + 2
B_END = B_FFN2 + FFN_BODIES
DVE_PAGES, PE_PAGES = (0, 1, 2, 4, 5, 6), (3, 7)
C_QA, C_QR, C_QM = 0, 3 * BR_W, 7 * BR_W

GAMMA = [1.0 - 2.0 ** (-5 - h) for h in range(R_HEADS)]


def t5_bucket(n):
    exact = T5_BUCKETS // 2
    nf = np.maximum(n, 1).astype(np.float32)
    large = exact + (np.log(nf / exact) / np.float32(np.log(T5_MAX_DIST / exact))
                     * (T5_BUCKETS - exact)).astype(np.int32)
    return np.where(n < exact, n, np.minimum(large, T5_BUCKETS - 1))


def constants():
    half = R_DK // 2
    inv = (1.0 / (np.float32(ROPE_BASE) ** np.linspace(0.0, 1.0, half, dtype=np.float32))).astype(np.float32)
    pos = np.concatenate([np.arange(SEQ), np.full(DEC, PAST)]).astype(np.float32)
    ang = (inv[:, None] * pos[None, :]).astype(np.float32)
    log_g = np.log(np.array(GAMMA))
    i = np.arange(SEQ)
    diff = i[None, :] - i[:, None]
    decay = np.where(diff[None] >= 0, np.exp(np.maximum(diff, 0)[None] * log_g[:, None, None]), 0.0)
    decay = decay.reshape(R_HEADS, 2, P, SEQ).transpose(2, 0, 1, 3)
    decay = np.concatenate([decay[:, :, 0], decay[:, :, 1, P:]], axis=2)
    kdecay = np.exp((SEQ - 1 - i)[None, :] * log_g[:, None]).reshape(R_HEADS, 2, P).transpose(2, 0, 1)
    eye = np.eye(T5_BUCKETS, dtype=np.float32)
    return {
        "ident": np.eye(P, dtype=np.float32),
        "cos": np.cos(ang).astype(np.float32),
        "sin": np.sin(ang).astype(np.float32),
        "decay": np.ascontiguousarray(decay).astype(np.float32),
        "kdecay": np.ascontiguousarray(kdecay).astype(np.float32),
        "bucket_prompt": np.ascontiguousarray(eye[:, t5_bucket(SEQ - 1 - np.arange(SEQ))]),
        "bucket_decode": np.ascontiguousarray(eye[:, t5_bucket(PAST - np.arange(PAST))]),
    }


def build(nc, d, o, sem, PS, block):

    base = -(-nc.sbuf_base // 64) * 64

    def at(name, shape, offset, dt=F32):
        return nc.alloc_sbuf_tensor_at(name, [P, *shape], dt, offset=base + offset)

    ROWT = N * 4
    A_X = 0
    A_H = A_X + KT * ROWT
    A_HID = A_H + 2 * KT * ROWT
    A_RAW = A_HID + 2 * HID * ROWT
    A_SPLIT = A_RAW + 4 * UK * UC * 4
    A_EV = A_SPLIT + 4 * UK * UC * 4
    A_SMALL = A_EV + 8 * ROWT
    A_MID = A_SMALL + 1856

    xT = at("xT", [KT, N], A_X)
    hH = at("hH", [KT, N], A_H, F32R)
    hL = at("hL", [KT, N], A_H + KT * ROWT, F32R)
    hidH = at("hidH", [HID, N], A_HID, F32R)
    hidL = at("hidL", [HID, N], A_HID + HID * ROWT, F32R)
    raw = at("raw", [4, UK, UC], A_RAW)
    splitH = at("splitH", [2, UK, UC], A_SPLIT, F32R)
    splitL = at("splitL", [2, UK, UC], A_SPLIT + 2 * UK * UC * 4, F32R)
    EV = at("EV", [8, N], A_EV)
    off = A_SMALL

    def small(name, shape, dt=F32):
        nonlocal off
        t = at(name, shape, off, dt)
        off += -(-int(np.prod(shape)) * 4 // 32) * 32
        assert off <= A_MID
        return t

    ident = small("ident_s", [P])
    ones = small("ones", [P])
    gT = small("gT", [P])
    ptab = small("ptab", [DEC * NPAGES], I32)
    bias0 = small("bias0", [A_HEADS])
    TAIL = A_MID + 48128
    rs = at("rs", [N], TAIL)
    rt = at("rt", [N], TAIL + ROWT)
    ry = at("ry", [N], TAIL + 2 * ROWT)
    MX = small("MX", [2, 2, 2])
    G_FFN1, G_MIX, G_MEM, G_FFN2, G_FINAL, G_BIAS = 0, 16, 32, 48, 64, 80

    xtok = at("xtok", [2, D_MODEL], A_MID)
    mtok = at("mtok", [2, D_MODEL], A_MID + 16384)
    stok = at("stok", [D_MODEL], A_MID + 32768)
    memT = at("memT", [KT, N_MEM], A_HID)
    grow = at("grow", [P], A_EV)
    mkT0 = at("mkT0", [BT, N_MEM], A_MID)
    mvT0 = at("mvT0", [BT, N_MEM], A_MID + 8192)
    mkTok = at("mkTok", [2, BR_W], A_MID + 16384)
    mvTok0 = at("mvTok0", [2, BR_W], A_MID + 24576)
    T8 = BT * ROWT
    HB = A_HID + 2 * BT * ROWT
    orH = at("orH", [BT, N], A_HID, F32R)
    orL = at("orL", [BT, N], A_HID + T8, F32R)
    qrT = at("qrT", [BT, N], A_MID)
    krT = at("krT", [BT, N], A_MID + T8)
    grT = at("grT", [BT, N], A_MID + 2 * T8)
    vrT = at("vrT", [BT, N], A_MID + 3 * T8)
    vrTok = at("vrTok", [2, BR_W], A_MID + 4 * T8)
    decay = at("decay_s", [R_HEADS, SEQ + P], A_MID + 4 * T8 + 8192)
    cosT = at("cosT", [N], HB)
    sinT = at("sinT", [N], HB + ROWT)
    kdecay = at("kdecay_s", [R_HEADS, 2], HB + 2 * ROWT)
    vrS = at("vrS", [BR_W], HB + 2 * ROWT + 64)
    st = at("st", [2, 2, R_DV], HB + 2 * ROWT + 64)
    krTok = at("krTok", [2, BR_W], HB + 2 * ROWT + 64 + 4096)
    vB = at("vB", [2, BR_W], HB + 2 * ROWT + 64 + 4096)
    orS = at("orS", [BT, DEC], HB + 2 * ROWT + 64 + 4096 + 8192)
    orS2 = at("orS2", [BT, DEC], HB + 2 * ROWT + 64 + 4096 + 8192 + 256)
    state = [at(f"state{p}", [R_HEADS, 2, R_DV], where) for p, where in enumerate(
        (A_X, A_X + 8192, A_MID + 3 * T8, A_MID + 4 * T8 + 8192))]
    sqb = at("sqb", [2, 2, SEQ], A_EV)
    attb = at("attb", [2, 2, SEQ], A_EV + 4096)
    oaH = at("oaH", [BT, N], A_MID + 34816, F32R)
    oaL = at("oaL", [BT, N], A_MID + 34816 + T8, F32R)
    qaT = at("qaT", [BT, N], A_MID)
    kaT = at("kaT", [BT, N], A_MID + T8)
    vaT = at("vaT", [BT, N], A_MID + 2 * T8)
    vaTok = at("vaTok", [2, BR_W], A_MID + 3 * T8)
    rows = at("rows", [3, BR_W], A_X)
    kaTok = at("kaTok", [2, BR_W], A_EV)
    bias = at("bias", [2, 2, SEQ], A_X + 12288)
    vaS = at("vaS", [BT, DEC], A_MID + 4 * T8)
    own = at("own", [BT, DEC], A_MID + 4 * T8 + 256)
    biasD = at("biasD", [NPAGES, A_HEADS], A_MID + 4 * T8 + 512)
    kvA = at("kvA", [4, BR_W], A_MID)
    qBA = at("qBA", [2, BR_W], A_MID + 16384)
    pvSum = at("pvSum", [2, BR_W], A_MID + 16384)
    DEC_A = A_MID + 24576
    Sb = at("Sb", [2, NPAGES, A_HEADS], A_EV + 4 * ROWT)
    accT = at("accT", [KT, N], A_X)
    omH = at("omH", [BT, N], HB, F32R)
    omL = at("omL", [BT, N], HB + T8, F32R)
    qmT = at("qmT", [BT, N], A_MID)
    mkT = at("mkT", [BT, N_MEM], A_MID + T8)
    mvTok = at("mvTok", [2, BR_W], A_MID + T8 + 8192)
    qmS = at("qmS", [BR_W], A_MID + T8 + 16384)
    kvM = at("kvM", [4, BR_W], A_MID + T8 + 20480)
    qBM = at("qBM", [2, BR_W], A_X)
    mgH = at("mgH", [KT, N], A_MID, F32R)
    mgL = at("mgL", [KT, N], A_MID + KT * ROWT, F32R)
    assert A_MID + 34816 + 2 * T8 <= nc.sbuf_usable_end - base
    t5w = at("t5w", [A_HEADS], A_EV)
    bkp = at("bkp", [SEQ], A_EV + 64)
    bkd = at("bkd", [PAST], A_EV + 1088)
    t5row = at("t5row", [2 * SEQ], A_EV + 5184)

    def dec_tiles(kind, where, pages, heads):
        w = DEC * pages * heads * 4
        t = {n: at(f"{kind}_{n}", [DEC, pages, heads], where + k * w) for k, n in enumerate(("S", "L"))}
        g = where + 2 * w
        for k, n in enumerate(("mp", "mx", "se", "rd", "om", "eo", "t", "x1")):
            t[n] = at(f"{kind}_{n}", [DEC, heads], g + k * DEC * heads * 4)
        g += 8 * DEC * heads * 4
        t["oS"] = at(f"{kind}_oS", [BT, DEC], g)
        t["o2"] = at(f"{kind}_o2", [BT, DEC], g + 256)
        if kind == "A":
            t["gate"] = at("A_gate", [DEC, N_BLOCKS, heads], g + 512)
            t["excl"] = at("A_excl", [DEC, N_BLOCKS, heads], g + 1536)
            t["cmp"] = at("A_cmp", [DEC, heads], g + 2560)
        return t

    DA = dec_tiles("A", DEC_A, NPAGES, A_HEADS)
    DM = dec_tiles("M", A_EV, 2, M_HEADS)

    scratch = {n: nc.dram_tensor(f"scratch_{n}", list(s), F32, kind="Internal").ap() for n, s in {
        "t5": (A_HEADS, P, 2 * SEQ), "qa": (DEC, BR_W), "vr": (DEC, BR_W), "qm": (DEC, BR_W),
        "mkT": (P, BT * N_MEM), "mv": (N_MEM, BR_W), "x": (P, KT * N)}.items()}

    raw_full = [sem(f"raw_full{u}") for u in range(4)]
    hi_ready, split_ready, unit_used = sem("hi_ready"), sem("split_ready"), sem("unit_used")
    set_free = [sem(f"set_free{c}") for c in range(2)]
    silu_ready, prod_ready, hid_hi = sem("silu_ready"), sem("prod_ready"), sem("hid_hi")
    sig_ready, merge_step = sem("sig_ready"), sem("merge_step")
    sq_ready, sq_used, ms_ready, sqrt_ready, norm_rows, norm_hi, norm_done = map(sem, (
        "sq_ready", "sq_used", "ms_ready", "sqrt_ready", "norm_rows", "norm_hi", "norm_done"))
    dve_link = sem("dve_link")
    x_in, mem_in, gain_in, ident_in, rot_in, decay_in, t5_in, pt_in = map(sem, (
        "x_in", "mem_in", "gain_in", "ident_in", "rot_in", "decay_in", "t5_in", "pt_in"))
    ones_set, mk_in = sem("ones_set"), sem("mk_in")
    stored = sem("stored")
    kept = sem("kept")
    turned, turn_out = sem("turned"), sem("turn_out")
    att_ps, att_sb, o_ps, o_sq, ms_ps, r_done, kd_ready, s_ps, s_out = map(sem, (
        "att_ps", "att_sb", "o_ps", "o_sq", "ms_ps", "r_done", "kd_ready", "s_ps", "s_out"))
    r_var, r_sqrt = sem("r_var"), sem("r_sqrt")
    st_sent = [sem(f"st_sent{p}") for p in range(2)]
    s_in = [sem(f"s_in{p}") for p in range(4)]
    vb_in = [sem(f"vb_in{p}") for p in range(2)]
    s_scaled, s_new, s_read, s_back, os_out = sem("s_scaled"), sem("s_new"), sem("s_read"), [
        sem(f"s_back{p}") for p in range(4)], sem("os_out")
    a_s, a_p, a_max, a_exp, a_norm, a_pt, a_ptc, a_o, a_hi, a_lo = map(sem, (
        "a_s", "a_p", "a_max", "a_exp", "a_norm", "a_pt", "a_ptc", "a_o", "a_hi", "a_lo"))
    bias_in = [sem(f"bias_in{p}") for p in range(2)]
    t5_ps, t5_ready = sem("t5_ps"), sem("t5_ready")
    kv_full = [sem(f"kv_full{s}") for s in range(4)]
    kv_used = [sem(f"kv_used{s}") for s in range(4)]
    page_full = [sem(f"page_full{s}") for s in range(4)]
    q_in = [sem(f"q_in{s}") for s in range(2)]
    qb_in = [sem(f"qb_in{s}") for s in range(2)]
    kq_ready = sem("kq_ready")
    gate_ps, sum_ps, d_sb, d_exp, d_max, d_maxall, d_logit = map(sem, (
        "gate_ps", "sum_ps", "d_sb", "d_exp", "d_max", "d_maxall", "d_logit"))
    own_ready, r_all_done, samp_sq, samp_ms, samp_var, samp_sqrt, m_done, a_done = map(sem, (
        "own_ready", "r_all_done", "samp_sq", "samp_ms", "samp_var", "samp_sqrt", "m_done", "a_done"))
    d_prob, d_os = sem("d_prob"), sem("d_os")
    p_in_place, sample_summed = sem("p_in_place"), sem("sample_summed")
    s_in_place, os_copied, x_kept, x_back = sem("s_in_place"), sem("os_copied"), sem("x_kept"), sem("x_back")
    y_sent = sem("y_sent")

    turns = []

    def turn(name, srcs, rows, width, dest):
        turns.append((name, srcs, rows, width, dest))

    turn("gain", [(grow[:, :], 0)], P, P, gT[:, :].rearrange("p (a c) -> p a c", a=1))
    for tt in range(2):
        for g in range(4):
            turn("mem", [(mtok[:, tt, (4 * g + k) * P:(4 * g + k + 1) * P], k) for k in range(4)], P, P,
                 memT[:, 4 * g:4 * g + 4, tt * P:(tt + 1) * P])
    for tt in range(2):
        for g in range(4):
            turn("x", [(xtok[:, tt, (4 * g + k) * P:(4 * g + k + 1) * P], k) for k in range(4)], P, P,
                 xT[:, 4 * g:4 * g + 4, tt * P:(tt + 1) * P])
    turn("x", [(stok[0:DEC, k * P:(k + 1) * P], k) for k in range(KT)], P, DEC, xT[:, :, SEQ:N])

    def turn_tokens(name, src, dest):
        for tt in range(2):
            for g in range(2):
                turn(name, [(src[:, 4 * g + k, tt * P:(tt + 1) * P], k) for k in range(4)], P, P,
                     dest[:, tt, g * 512:(g + 1) * 512].rearrange("p (a c) -> p a c", a=4))

    def turn_samples(name, src, dest):
        for g in range(2):
            turn(name, [(src[:, 4 * g + k, SEQ:N], k) for k in range(4)], DEC, P,
                 dest[g * 512:(g + 1) * 512])

    turn_tokens("mem_kv", mkT0, mkTok)
    turn_tokens("mem_kv", mvT0, mvTok0)
    turn_tokens("r", vrT, vrTok)
    turn_tokens("r", krT, krTok)

    class RowDest:
        def __init__(self, t, *ix):
            self.t, self.ix = t, ix

        def __getitem__(self, cols):
            return self.t[(slice(0, DEC), *self.ix, cols)].rearrange("p (a c) -> p a c", a=4)

    turn_samples("r", vrT, RowDest(vrS))
    turn_samples("m", qmT, RowDest(qmS))
    turn_tokens("a", vaT, vaTok)
    turn_tokens("a", kaT, kaTok)
    turn_samples("a", kaT, RowDest(rows, 0))
    turn_samples("a", vaT, RowDest(rows, 1))
    turn_samples("a", qaT, RowDest(rows, 2))
    ytok = at("ytok", [2, D_MODEL], A_MID)
    ystok = at("ystok", [D_MODEL], A_MID + 16384)
    yT = at("yT", [KT, N], A_HID)
    for tt in range(2):
        for g in range(4):
            turn("y", [(yT[:, 4 * g + k, tt * P:(tt + 1) * P], k) for k in range(4)], P, P,
                 ytok[:, tt, g * 512:(g + 1) * 512].rearrange("p (a c) -> p a c", a=4))
    for g in range(4):
        turn("y", [(yT[:, 4 * g + k, SEQ:N], k) for k in range(4)], DEC, P,
             ystok[0:DEC, g * 512:(g + 1) * 512].rearrange("p (a c) -> p a c", a=4))

    def turns_of(name):
        return [(q, t) for q, t in enumerate(turns) if t[0] == name]

    def turns_until(name):
        return turns_of(name)[-1][0] + 1

    def pe_turns(pe, name):
        for q, (_, srcs, rows_out, width, _) in turns_of(name):
            if q >= 2:
                pe.wait_ge(turn_out, q - 1)
            for src, block in srcs:
                n = src.shape[0]
                last = nc.tensor.transpose(PS[0:rows_out, q % 2, block * width:(block + 1) * width],
                                           src, ident[0:n, 0:n])
            last.then_inc(turned, 1)

    def act_turns(act, name):
        for q, (_, srcs, rows_out, width, dest) in turns_of(name):
            act.wait_ge(turned, q + 1)
            nc.scalar.activation(dest, PS[0:rows_out, q % 2, 0:len(srcs) * width].rearrange(
                "p (a c) -> p a c", a=len(srcs)), ACT.Copy).then_inc(turn_out, 1)

    def wait_count(eng, s, n):
        if not (isinstance(n, int) and n <= 0):
            eng.wait_ge(s, n)

    def first_apart(eng, n, body):
        body(0)
        with eng.Fori(1, n) as i:
            body(i)

    def sp_unit_free(sp, B, c, u):
        if not (isinstance(B, int) and B == 0 and c == 0):
            sp.wait_ge(split_ready, 8 * B + 4 * c + u - 3)

    def sp_unit(sp, B, c, u, src):
        sp_unit_free(sp, B, c, u)
        sp_unit_load(sp, u, src)

    def sp_unit_load(sp, u, src):
        nk = src.shape[0] // P
        sp.dma_start(raw[:, u, 0:nk, :], src.rearrange("(k p) c -> p k c", p=P)).then_inc(raw_full[u], 16)

    def sp_wide_unit(sp, B, W, col, c, u):
        sp_unit(sp, B, c, u, W[(u % 2) * UK * P:(u % 2 + 1) * UK * P,
                               bass.ds(col + 512 * c + UC * (u // 2), UC)])

    def sp_wide(sp, B, W, col, steps=(0, 1)):
        for c in steps:
            for u in range(4):
                sp_wide_unit(sp, B, W, col, c, u)

    def sp_ffn(sp, B0, w1, w3, w2):
        B = B0
        for t0, n in FFN_BLOCKS:
            with sp.Fori(0, n // 4) as i:
                for c in range(2):
                    for u in range(4):
                        W = w1 if u < 2 else w3
                        sp_unit(sp, i + B, c, u, W[(u % 2) * UK * P:(u % 2 + 1) * UK * P,
                                                   bass.ds(i * 512 + (t0 * P + UC * c), UC)])
            B += n // 4
            nk = n // 2
            with sp.Fori(0, 2) as i:
                for c in range(2):
                    for u in range(4):
                        k0 = t0 + (u % 2) * nk
                        sp_unit(sp, i + B, c, u, w2[k0 * P:(k0 + nk) * P,
                                                    bass.ds(i * 1024 + (512 * c + UC * (u // 2)), UC)])
            B += 2

    BRANCHES = [("w_br_ret", 1, (orH, orL)), ("w_br_mem", 2, (omH, omL)), ("w_br_moba", 0, (oaH, oaL))]

    def sp_gate_unit(sp, r, i, c, u):
        sp_unit_free(sp, i + (B_GATE + 4 * r), c, u)
        sp_gate_load(sp, r, i, c, u)

    def sp_gate_load(sp, r, i, c, u):
        name, section, _ = BRANCHES[r]
        col = i * 2 * UC + UC * c
        if u < 2:
            src = d["w_gate"][u * UK * P:(u + 1) * UK * P, bass.ds(col + section * D_MODEL, UC)]
        else:
            src = d[name][(u - 2) * 4 * P:(u - 1) * 4 * P, bass.ds(col, UC)]
        sp_unit_load(sp, u, src)

    def sp_page_number(sp, i, c, g):
        return sp.value_load(ptab[0:1, bass.ds(i * 2 * NPAGES + (c * NPAGES + g), 1)],
                             min_val=0, max_val=d["cache_k"].shape[0] - 1)

    def sp_page(sp, values, page, i4, c, g):
        s = g % 4
        n0 = DKA.base // 4 + values * DEC * NPAGES // 4
        sp.wait_ge(kv_used[s], i4 + (n0 + 2 * c + g // 4))
        sp.dma_start(kvA[:, s, :], d["cache_v" if values else "cache_k"][bass.ds(page, 1), :, :].rearrange(
            "a p c -> (a p) c")).then_inc(page_full[s], 16)

    def sp_gates(sp):
        for u in range(4):
            sp_gate_unit(sp, 0, 0, 0, u)
        sp.wait_ge(kept, 96)
        sp.wait_ge(a_lo, A_HEADS + M_HEADS)
        for r in range(2):
            def body(i):
                i4 = i * 4 if isinstance(i, int) else sp.snap(i * 4)
                for c in range(2):
                    if r == 0:
                        sp.wait_ge(kv_used[3], i4 + (DKA.base // 4 + 2 * c - 2))
                        sp.dma_start(qBA[:, c, :], scratch["qa"][bass.ds(i * 2 + c, 1), :].to_broadcast(
                            [P, BR_W])).then_inc(q_in[c], 16)
                    for u in range(4):
                        nr, ni, n_c = (r, i, 1) if c == 0 else (r + 1, 0, 0) if isinstance(i, int) else (r, i + 1, 0)
                        sp_unit_free(sp, ni + (B_GATE + 4 * nr), n_c, u)
                        pages = [sp_page_number(sp, i, c, 2 * u + j) for j in range(2)]
                        sp_gate_load(sp, nr, ni, n_c, u)
                        sp_page(sp, r, pages[0], i4, c, 2 * u)
                        sp_page(sp, r, pages[1], i4, c, 2 * u + 1)
            with sp.Fori(0, 3) as i:
                body(i)
            body(3)
        for u in range(4):
            sp_gate_unit(sp, 2, 0, 1, u)
        with sp.Fori(1, 4) as i:
            for c in range(2):
                for u in range(4):
                    sp_gate_unit(sp, 2, i, c, u)

    def split_slot(c, u, nk, gate):
        if not gate:
            return u % 2, slice(0, nk)
        return (c, slice(UK // 2 * (u - 2), UK // 2 * (u - 1))) if u >= 2 else (u ^ c, slice(0, nk))

    def act_split(act, B, c, u, nk=UK, gate=False):
        s, tiles = split_slot(c, u, nk, gate)
        act.wait_ge(raw_full[u], 32 * B + 16 * (c + 1))
        if not (isinstance(B, int) and B == 0 and c == 0 and u < 2):
            act.wait_ge(unit_used, 8 * B + 4 * c + ((-2, 0, 1, 1)[u] if gate else u - 1))
        nc.scalar.activation(splitH[:, s, tiles, :], raw[:, u, 0:nk, :], ACT.Copy).then_inc(hi_ready, 1)

    def dve_split(dve, B, c, u, nk=UK, gate=False):
        s, tiles = split_slot(c, u, nk, gate)
        dve.wait_ge(hi_ready, 8 * B + 4 * c + u + 1)
        nc.vector.tensor_tensor(splitL[:, s, tiles, :], raw[:, u, 0:nk, :],
                                splitH[:, s, tiles, :].bitcast(F32), ALU.subtract).then_inc(split_ready, 1)

    def split_body(split, eng, B, evac, nks=(8, 8, 8, 8), last=False, between=None):
        for c in range(2):
            nB, n_c = (B, 1) if c == 0 else (B + 1, 0)
            for j, unit in enumerate(((B, c, 2, nks[2]), (B, c, 3, nks[3]), (nB, n_c, 0), (nB, n_c, 1))):
                if last and c == 1 and j >= 2:
                    break
                split(eng, *unit)
                if between:
                    between(4 * c + j)
            evac(B, c)

    def pe_unit(pe, B, c, u, rhs, tiles, n, start, stop, gate=False):
        H, L = rhs
        s, kept_at = split_slot(c, u, len(tiles), gate)
        pe.wait_ge(split_ready, 8 * B + 4 * c + u + 1)
        for m in range(2):
            out = PS[:, 4 * c + 2 * (u // 2) + m, 0:n]
            for j, k in enumerate(tiles):
                w_hi = splitH[:, s, kept_at.start + j, m * P:(m + 1) * P]
                w_lo = splitL[:, s, kept_at.start + j, m * P:(m + 1) * P]
                first, final = start and j == 0, stop and j == len(tiles) - 1
                nc.tensor.matmul(out, w_hi, H[:, k, 0:n], start=first, stop=False)
                nc.tensor.matmul(out, w_hi, L[:, k, 0:n], start=False, stop=False)
                last = nc.tensor.matmul(out, w_lo, H[:, k, 0:n], start=False, stop=final)
        last.then_inc(unit_used, 1)

    def pe_step_free(pe, B, c):
        wait_count(pe, set_free[c], B)

    def pe_drained(pe, B):
        pe.wait_ge(set_free[0], B)
        pe.wait_ge(set_free[1], B)

    def pe_wide(pe, B, rhs, n=N, nk=UK, rest=None):
        for c in range(2):
            pe_step_free(pe, B, c)
            for u in range(4):
                if rest and c == 0 and u == 1:
                    pe.wait_ge(*rest)
                pe_unit(pe, B, c, u, rhs, range((u % 2) * nk, (u % 2 + 1) * nk), n, u % 2 == 0, u % 2 == 1)

    def pe_ffn(pe, B0, norm_count):
        B = B0
        for _, n in FFN_BLOCKS:
            with pe.Fori(0, n // 4) as i:
                pe_wide(pe, i + B, (hH, hL), rest=(norm_done, norm_count))
            B += n // 4
            with pe.Fori(0, 2) as i:
                pe_wide(pe, i + B, (hidH, hidL), nk=n // 2, rest=(set_free[1], B))
            B += 2

    def pe_gates(pe, r):
        def body(i):
            for c in range(2):
                B = i + (B_GATE + 4 * r)
                pe_step_free(pe, B, c)
                for u in range(4):
                    if u < 2:
                        pe_unit(pe, B, c, u, (hH, hL), range(u * UK, (u + 1) * UK), N, u == 0, u == 1, True)
                    else:
                        if r == 1 and u == 2:
                            pe.wait_ge(os_copied, i * 2 + (c + 1))
                        pe_unit(pe, B, c, u, BRANCHES[r][2], range((u - 2) * 4, (u - 1) * 4), N, u == 2, u == 3,
                                True)
                    if r == 1 and u == 0 and not (isinstance(i, int) and c == 0):
                        pe_sample_end(pe, i, c - 1)
                    if r == 1 and u == 1:
                        pe.wait_ge(set_free[1 - c], B + c)
                        pe_page(pe, i, c, PE_PAGES[0])

        if r == 1:
            first_apart(pe, 4, body)
            pe_sample_end(pe, 3, 1)
        else:
            with pe.Fori(0, 4) as i:
                body(i)

    def pe_page(pe, i, k, g):
        s = g % 4
        pe.wait_ge(page_full[s], i * 64 + 16 * (DEC * NPAGES // 4 + 2 * k + g // 4 + 1))
        for h in range(A_HEADS):
            last = nc.tensor.matmul(
                PS[:, 4 * (1 - k % 2) + 3, h:h + 1], kvA[:, s, h * P:(h + 1) * P],
                DA["L"][:, bass.ds(i * 2 + k, 1), g, h:h + 1].rearrange("p a h -> p (a h)"),
                start=g == PE_PAGES[0] and h == 0, stop=False, skip_group_check=True)
        last.then_inc(kv_used[s], 1)

    def pe_sample_end(pe, i, k):
        pe_page(pe, i, k, PE_PAGES[1])
        pe.wait_ge(kv_used[2], i * 4 + (DKA.base // 4 + DEC * NPAGES // 4 + 2 * k + 2))
        for h in range(A_HEADS):
            last = nc.tensor.matmul(PS[:, 4 * (1 - k % 2) + 3, h:h + 1], pvSum[:, k % 2, h * P:(h + 1) * P],
                                    ones[:, 0:1], start=False, stop=True, skip_group_check=True)
        last.then_inc(sample_summed, 1)

    def step_made(eng, B, c):
        eng.wait_ge(unit_used, 8 * B + 4 * c + 4)

    def ffn_evac_act(act):
        def evac(B, c):
            step_made(act, B, c)
            nc.scalar.activation(EV[:, 2 * c:2 * c + 2, :], PS[:, 4 * c:4 * c + 2, 0:N],
                                 ACT.Silu).then_inc(silu_ready, 1)
        return evac

    def ffn_up_evac_dve(dve, up0, i):
        def evac(B, c):
            n = i * 2 + (up0 + c + 1)
            dve.wait_ge(silu_ready, n)
            prod = EV[:, 4 + 2 * c:6 + 2 * c, :]
            nc.vector.tensor_tensor(prod, EV[:, 2 * c:2 * c + 2, :], PS[:, 4 * c + 2:4 * c + 4, 0:N],
                                    ALU.mult).then_inc(prod_ready, 1)
            hi = hidH[:, bass.ds(i * 4 + 2 * c, 2), :]
            dve.wait_ge(prod_ready, n)
            nc.vector.tensor_copy(hi, prod).then_inc(hid_hi, 1)
            dve.wait_ge(hid_hi, n)
            nc.vector.tensor_tensor(hidL[:, bass.ds(i * 4 + 2 * c, 2), :], prod, hi.bitcast(F32),
                                    ALU.subtract).then_inc(set_free[c], 1)
        return evac

    def add_evac_dve(dve, i, scale):
        def evac(B, c):
            step_made(dve, B, c)
            x4 = xT[:, bass.ds(i * 8 + 4 * c, 4), :]
            nc.vector.scalar_tensor_tensor(x4, PS[:, 4 * c:4 * c + 4, 0:N], scale, x4,
                                           ALU.mult, ALU.add).then_inc(set_free[c], 1)
        return evac

    def none(B, c):
        pass

    FFN_UPS = 2 * sum(n // 4 for _, n in FFN_BLOCKS)

    def split_ffn(split, eng, B0, which, final):
        B, ups = B0, which * FFN_UPS
        on_act = split is act_split
        for blk, (_, n) in enumerate(FFN_BLOCKS):
            with eng.Fori(0, n // 4) as i:
                ev = ffn_evac_act(eng) if on_act else ffn_up_evac_dve(eng, ups, i)
                split_body(split, eng, i + B, ev)
            B += n // 4
            ups += n // 2
            last = final and blk == len(FFN_BLOCKS) - 1
            with eng.Fori(0, 1 if last else 2) as i:
                split_body(split, eng, i + B, none if on_act else add_evac_dve(eng, i, 0.5))
            if last:
                split_body(split, eng, B + 1, none if on_act else add_evac_dve(eng, 1, 0.5), last=True)
            B += 2

    NORMS = {"mem": 0, "ffn1": 1, "mix": 2, "ffn2": 3, "final": 4}

    def norm_args(name):
        return {"mem": (memT, N_MEM, G_MEM), "ffn1": (xT, N, G_FFN1), "mix": (xT, N, G_MIX),
                "ffn2": (xT, N, G_FFN2), "final": (xT, N, G_FINAL)}[name]

    def act_norm(act, name):
        src, n, _ = norm_args(name)
        q = NORMS[name]
        for r in range(4):
            if 4 * q + r >= 2:
                act.wait_ge(sq_used, 4 * q + r - 1)
            nc.scalar.activation(EV[:, 4 * (r % 2):4 * (r % 2) + 4, 0:n], src[:, 4 * r:4 * r + 4, 0:n],
                                 ACT.Square).then_inc(sq_ready, 1)
        act.wait_ge(ms_ready, q + 1)
        nc.scalar.activation(rt[:, 0:n], rs[:, 0:n], ACT.Sqrt).then_inc(sqrt_ready, 1)
        if name != "final":
            for r in range(4):
                act.wait_ge(norm_rows, 4 * q + r + 1)
                nc.scalar.activation(hH[:, 4 * r:4 * r + 4, 0:n], EV[:, 4 * (r % 2):4 * (r % 2) + 4, 0:n],
                                     ACT.Copy).then_inc(norm_hi, 1)

    def pe_norm(pe, name):
        _, n, _ = norm_args(name)
        q = NORMS[name]
        for r in range(4):
            pe.wait_ge(sq_ready, 4 * q + r + 1)
            for k in range(4):
                last = nc.tensor.matmul(PS[:, 7, 0:n], ones[:, :], EV[:, 4 * (r % 2) + k, 0:n],
                                        start=r == 0 and k == 0, stop=r == 3 and k == 3)
            last.then_inc(sq_used, 1)

    def refine(link, y, m, t):
        link(nc.vector.tensor_tensor(t, y, y, ALU.mult))
        link(nc.vector.scalar_tensor_tensor(t, t, -0.5, m, ALU.mult, ALU.mult))
        link(nc.vector.scalar_tensor_tensor(y, t, 1.5, y, ALU.add, ALU.mult))

    def dve_norm(dve, link, name, out=None):
        src, n, g = norm_args(name)
        q = NORMS[name]
        dve.wait_ge(sq_used, 4 * q + 4)
        nc.vector.tensor_scalar(rs[:, 0:n], PS[:, 7, 0:n], 1.0 / D_MODEL, EPS, ALU.mult,
                                ALU.add).then_inc(ms_ready, 1)
        dve.wait_ge(sqrt_ready, q + 1)
        link(nc.vector.reciprocal(ry[:, 0:n], rt[:, 0:n]))
        refine(link, ry[:, 0:n], rs[:, 0:n], rt[:, 0:n])
        def rows_of(r):
            half = EV[:, 4 * (r % 2):4 * (r % 2) + 4, 0:n] if out is None else out[:, 4 * r:4 * r + 4, 0:n]
            for k in range(4):
                last = nc.vector.scalar_tensor_tensor(half[:, k, :], src[:, 4 * r + k, 0:n],
                                                      gT[:, g + 4 * r + k:g + 4 * r + k + 1],
                                                      ry[:, 0:n], ALU.mult, ALU.mult)
            last.then_inc(norm_rows, 1)

        rows_of(0)
        for r in range(4):
            if r < 3:
                rows_of(r + 1)
            if out is None:
                dve.wait_ge(norm_hi, 4 * q + r + 1)
                last = nc.vector.tensor_tensor(hL[:, 4 * r:4 * r + 4, 0:n], EV[:, 4 * (r % 2):4 * (r % 2) + 4, 0:n],
                                               hH[:, 4 * r:4 * r + 4, 0:n].bitcast(F32), ALU.subtract)
                if r % 2:
                    last.then_inc(norm_done, 1)
                    dve.wait_ge(norm_done, 2 * q + r // 2 + 1)
                else:
                    link(last)

    def pe_retention(pe):
        def att(h):
            if h >= 2:
                pe.wait_ge(att_sb, h - 1)
            for jt in range(2):
                for dt in range(2):
                    last = nc.tensor.matmul(PS[:, 2 + h % 2, jt * SEQ + jt * P:(jt + 1) * SEQ],
                                            krT[:, 2 * h + dt, jt * P:(jt + 1) * P],
                                            qrT[:, 2 * h + dt, jt * P:SEQ], start=dt == 0, stop=dt == 1)
            last.then_inc(att_ps, 1)

        att(0)
        for h in range(R_HEADS):
            if h + 1 < R_HEADS:
                att(h + 1)
            pe.wait_ge(att_sb, h + 1)
            for et in range(2):
                v = lambda jt: vrTok[:, jt, h * R_DV + et * P:h * R_DV + (et + 1) * P]
                nc.tensor.matmul(PS[:, 4, et * SEQ:(et + 1) * SEQ], v(0), attb[:, h % 2, 0, :],
                                 start=True, stop=False)
                last = nc.tensor.matmul(PS[:, 4, et * SEQ + P:(et + 1) * SEQ], v(1), attb[:, h % 2, 1, P:SEQ],
                                        start=False, stop=True)
            last.then_inc(o_ps, 1)
            pe.wait_ge(kd_ready, h + 1)
            if h >= 1:
                pe.wait_ge(s_out, h)
            for dt in range(2):
                for jt in range(2):
                    c0 = h * R_DK + dt * P
                    last = nc.tensor.matmul(PS[:, 6, dt * R_DV:(dt + 1) * R_DV], krTok[:, jt, c0:c0 + P],
                                            vrTok[:, jt, h * R_DV:(h + 1) * R_DV], start=jt == 0, stop=jt == 1)
            last.then_inc(s_ps, 1)
            pe.wait_ge(o_sq, h + 1)
            for et in range(2):
                last = nc.tensor.matmul(PS[:, 5, 0:SEQ], ones[:, :], sqb[:, h % 2, et, :],
                                        start=et == 0, stop=et == 1)
            last.then_inc(ms_ps, 1)
            pe.wait_ge(r_done, h + 1)

    def act_retention(act):
        for h in range(R_HEADS):
            act.wait_ge(o_ps, h + 1)
            nc.scalar.activation(sqb[:, h % 2, :, :], PS[:, 4, :].rearrange("p (a c) -> p a c", a=2),
                                 ACT.Square).then_inc(o_sq, 1)
            act.wait_ge(s_ps, h + 1)
            if h >= 2:
                act.wait_ge(st_sent[h % 2], 16 * (h // 2))
            nc.scalar.activation(st[:, h % 2, :, :], PS[:, 6, :].rearrange("p (a c) -> p a c", a=2),
                                 ACT.Copy).then_inc(s_out, 1)
            act.wait_ge(r_var, h + 1)
            nc.scalar.activation(rt[:, 0:SEQ], rs[:, 0:SEQ], ACT.Sqrt).then_inc(r_sqrt, 1)

    def dve_retention(dve, link):
        def att(h):
            dve.wait_ge(att_ps, h + 1)
            nc.vector.tensor_tensor(attb[:, h % 2, 0, :], PS[:, 2 + h % 2, 0:SEQ], decay[:, h, 0:SEQ], ALU.mult)
            nc.vector.tensor_tensor(attb[:, h % 2, 1, P:SEQ], PS[:, 2 + h % 2, SEQ + P:2 * SEQ],
                                    decay[:, h, SEQ:SEQ + P], ALU.mult).then_inc(att_sb, 1)

        att(0)
        for h in range(R_HEADS):
            for jt in range(2):
                kk = krTok[:, jt, h * R_DK:(h + 1) * R_DK]
                last = nc.vector.tensor_scalar(kk, kk, kdecay[:, h, jt:jt + 1], None, ALU.mult)
            last.then_inc(kd_ready, 1)
            if h + 1 < R_HEADS:
                if h >= 1:
                    dve.wait_ge(o_ps, h)
                att(h + 1)
            dve.wait_ge(ms_ps, h + 1)
            nc.vector.tensor_scalar(rs[:, 0:SEQ], PS[:, 5, 0:SEQ], 1.0 / R_DV, EPS, ALU.mult,
                                    ALU.add).then_inc(r_var, 1)
            dve.wait_ge(r_sqrt, h + 1)
            y = ry[:, 0:SEQ]
            link(nc.vector.reciprocal(y, rt[:, 0:SEQ]))
            refine(link, y, rs[:, 0:SEQ], rt[:, 0:SEQ])
            for et in range(2):
                t = sqb[:, h % 2, et, :]
                link(nc.vector.tensor_tensor(t, PS[:, 4, et * SEQ:(et + 1) * SEQ], y, ALU.mult))
                link(nc.vector.tensor_tensor(t, t, grT[:, 2 * h + et, 0:SEQ], ALU.mult))
                link(nc.vector.tensor_copy(orH[:, 2 * h + et, 0:SEQ], t))
                last = nc.vector.tensor_tensor(orL[:, 2 * h + et, 0:SEQ], t,
                                               orH[:, 2 * h + et, 0:SEQ].bitcast(F32), ALU.subtract)
            last.then_inc(r_done, 1)

    def sp_states(sp):
        def load_state(b, p):
            sp.dma_start(state[p][:, :, :, :], d["state_ret"][bass.ds(b, 1), :, :, :].rearrange(
                "a h (t p) e -> p (a h) t e", p=P)).then_inc(s_in[p], 16)

        def load_v(b, p):
            sp.dma_start(vB[:, p % 2, :], scratch["vr"][bass.ds(b, 1), :].to_broadcast([P, BR_W])
                         ).then_inc(vb_in[p % 2], 16)

        sp.wait_ge(x_kept, 16)
        load_state(0, 0)
        load_state(1, 1)
        sp.wait_ge(kept, 48)
        sp.wait_ge(r_done, R_HEADS)
        load_v(0, 0)
        load_v(1, 1)
        for p in (2, 3):
            load_state(p, p)
            sp.wait_ge(s_new, p - 1)
            load_v(p, p)
        with sp.Fori(1, DEC // 4) as i:
            for p in range(4):
                sp.wait_ge(s_back[p], i * 16)
                sp.wait_ge(s_read, i * 4 + (p - 3))
                load_state(i * 4 + p, p)
                sp.wait_ge(s_new, i * 4 + (p - 1))
                load_v(i * 4 + p, p)

    def act_states(act):
        with act.Fori(0, DEC // 4) as i:
            def back(p):
                act.wait_ge(s_new, i * 4 + (p + 1))
                act.dma_start(o["ret_state_sample"][bass.ds(i * 4 + p, 1), :, :, :].rearrange(
                    "a h (t p) e -> p (a h) t e", p=P), state[p][:, :, :, :]).then_inc(s_back[p], 16)

            for p in range(4):
                act.wait_ge(s_in[p], i * 16 + 16)
                for h in range(R_HEADS):
                    last = nc.scalar.activation(state[p][:, h, :, :], state[p][:, h, :, :], ACT.Copy,
                                                scale=GAMMA[h])
                last.then_inc(s_scaled, 1)
                if p:
                    back(p - 1)
            back(3)

    def dve_states(dve):
        with dve.Fori(0, DEC // 4) as i:
            def out(p):
                dve.wait_ge(s_read, i * 4 + (p + 1))
                nc.vector.tensor_copy(orS[:, :, bass.ds(i * 4 + p, 1)],
                                      PS[:, p % 2, 0:BT].rearrange("p (a c) -> p a c", c=1)).then_inc(os_out, 1)

            for p in range(4):
                dve.wait_ge(s_scaled, i * 4 + (p + 1))
                dve.wait_ge(vb_in[p % 2], i * 32 + 16 * (p // 2 + 1))
                for h in range(R_HEADS):
                    for dt in range(2):
                        s = state[p][:, h, dt, :]
                        last = nc.vector.scalar_tensor_tensor(
                            s, vB[:, p % 2, h * R_DV:(h + 1) * R_DV],
                            krT[:, 2 * h + dt, bass.ds(i * 4 + (SEQ + p), 1)], s, ALU.mult, ALU.add)
                last.then_inc(s_new, 1)
                if p:
                    out(p - 1)
            out(3)

    def pe_states(pe):
        def body(i):
            for p in range(4):
                pe.wait_ge(s_new, i * 4 + (p + 1))
                wait_count(pe, os_out, i * 4 + (p - 1))
                for h in range(R_HEADS):
                    for et in range(2):
                        for dt in range(2):
                            last = nc.tensor.matmul(
                                PS[:, p % 2, 2 * h + et:2 * h + et + 1], state[p][:, h, dt, et * P:(et + 1) * P],
                                qrT[:, 2 * h + dt, bass.ds(i * 4 + (SEQ + p), 1)],
                                start=dt == 0, stop=dt == 1)
                last.then_inc(s_read, 1)

        first_apart(pe, DEC // 4, body)

    def states_away(eng):
        for p in range(4):
            eng.wait_ge(s_back[p], 16 * (DEC // 4))

    class Kind:
        def __init__(self, name, heads, dt, et, causal, qT, kT, vtok, oH, oL, scale, q0):
            self.name, self.heads, self.dt, self.et, self.causal = name, heads, dt, et, causal
            self.qT, self.kT, self.vtok, self.oH, self.oL, self.scale = qT, kT, vtok, oH, oL, scale
            self.q0 = q0

        def keys(self, it):
            return P * (it + 1) if self.causal else SEQ

    KA = Kind("A", A_HEADS, 1, 1, True, qaT, kaT, vaTok, oaH, oaL, A_DH ** -0.5, M_HEADS)
    KM = Kind("M", M_HEADS, 2, 2, False, qmT, mkT, mvTok, omH, omL, M_DH ** -0.5, 0)

    def pe_attend(pe, K):
        def scores(h):
            q = K.q0 + h
            if q >= 2:
                pe.wait_ge(a_p, q - 1)
            for it in range(2):
                for dt in range(K.dt):
                    last = nc.tensor.matmul(PS[:, q % 2, it * SEQ:it * SEQ + K.keys(it)],
                                            K.qT[:, K.dt * h + dt, it * P:(it + 1) * P],
                                            K.kT[:, K.dt * h + dt, 0:K.keys(it)],
                                            start=dt == 0, stop=dt == K.dt - 1)
            last.then_inc(a_s, 1)

        def rest(h):
            q = K.q0 + h
            pe.wait_ge(a_norm, q + 1)
            if q >= 2:
                pe.wait_ge(a_ptc, q - 1)
            for it in range(2):
                for jt in range(K.keys(it) // P):
                    last = nc.tensor.transpose(PS[:, 2 + q % 2, jt * SEQ + it * P:jt * SEQ + (it + 1) * P],
                                               sqb[:, q % 2, it, jt * P:(jt + 1) * P], ident[:, :])
            last.then_inc(a_pt, 1)
            pe.wait_ge(a_ptc, q + 1)
            if q >= 2:
                pe.wait_ge(a_lo, q - 1)
            for et in range(K.et):
                c0 = (h * K.et + et) * P
                for jt in range(2):
                    i0 = jt * P if K.causal else 0
                    last = nc.tensor.matmul(PS[:, 4 + q % 2, et * SEQ + i0:(et + 1) * SEQ],
                                            K.vtok[:, jt, c0:c0 + P], attb[:, q % 2, jt, i0:SEQ],
                                            start=jt == 0, stop=jt == 1)
            last.then_inc(a_o, 1)

        scores(0)
        for h in range(K.heads):
            if h + 1 < K.heads:
                scores(h + 1)
            rest(h)

    def dve_attend(dve, link, K):
        def soft(h):
            q = K.q0 + h
            dve.wait_ge(a_s, q + 1)
            if q >= 2:
                dve.wait_ge(a_pt, q - 1)
            if K.causal:
                dve.wait_ge(bias_in[h % 2], 32 * (h // 2 + 1))
            for it in range(2):
                n = K.keys(it)
                s, ps = sqb[:, q % 2, it, 0:n], PS[:, q % 2, it * SEQ:it * SEQ + n]
                if K.causal:
                    last = nc.vector.scalar_tensor_tensor(s, ps, K.scale, bias[:, h % 2, it, 0:n],
                                                          ALU.mult, ALU.add)
                else:
                    last = nc.vector.tensor_scalar(s, ps, K.scale, None, ALU.mult)
            last.then_inc(a_p, 1)
            dve.wait_ge(a_p, q + 1)
            if q >= 2:
                dve.wait_ge(a_norm, q - 1)
            for it in range(2):
                last = nc.vector.tensor_reduce(MX[:, q % 2, 0, it:it + 1], sqb[:, q % 2, it, 0:K.keys(it)],
                                               AX.X, ALU.max, negate=True)
            last.then_inc(a_max, 1)

        def norm(h):
            q = K.q0 + h
            dve.wait_ge(a_exp, q + 1)
            link(nc.vector.reciprocal(MX[:, q % 2, 1, :], MX[:, q % 2, 1, :]))
            for it in range(2):
                s = sqb[:, q % 2, it, 0:K.keys(it)]
                last = nc.vector.tensor_scalar(s, s, MX[:, q % 2, 1, it:it + 1], None, ALU.mult)
            last.then_inc(a_norm, 1)

        def lo(h):
            q = K.q0 + h
            dve.wait_ge(a_hi, q + 1)
            t = slice(K.et * h, K.et * (h + 1))
            nc.vector.tensor_tensor(K.oL[:, t, 0:SEQ], PS[:, 4 + q % 2, 0:K.et * SEQ].rearrange(
                "p (a c) -> p a c", a=K.et), K.oH[:, t, 0:SEQ].bitcast(F32), ALU.subtract).then_inc(a_lo, 1)

        soft(0)
        for h in range(K.heads):
            norm(h)
            if h + 1 < K.heads:
                soft(h + 1)
            lo(h)

    def act_attend(act, K):
        def exps(h):
            q = K.q0 + h
            act.wait_ge(a_max, q + 1)
            for it in range(2):
                s = sqb[:, q % 2, it, 0:K.keys(it)]
                last = nc.scalar.activation(s, s, ACT.Exp, bias=MX[:, q % 2, 0, it:it + 1],
                                            accum_out=MX[:, q % 2, 1, it:it + 1])
            last.then_inc(a_exp, 1)

        def turn_copy(h):
            q = K.q0 + h
            act.wait_ge(a_pt, q + 1)
            if q >= 2:
                act.wait_ge(a_o, q - 1)
            if K.causal:
                nc.scalar.activation(attb[:, q % 2, 0, :], PS[:, 2 + q % 2, 0:SEQ], ACT.Copy)
                last = nc.scalar.activation(attb[:, q % 2, 1, P:SEQ], PS[:, 2 + q % 2, SEQ + P:2 * SEQ], ACT.Copy)
            else:
                last = nc.scalar.activation(attb[:, q % 2, :, :], PS[:, 2 + q % 2, :].rearrange(
                    "p (a c) -> p a c", a=2), ACT.Copy)
            last.then_inc(a_ptc, 1)

        def hi(h):
            q = K.q0 + h
            act.wait_ge(a_o, q + 1)
            nc.scalar.activation(K.oH[:, K.et * h:K.et * (h + 1), 0:SEQ], PS[:, 4 + q % 2, 0:K.et * SEQ].rearrange(
                "p (a c) -> p a c", a=K.et), ACT.Copy).then_inc(a_hi, 1)

        exps(0)
        for h in range(K.heads):
            turn_copy(h)
            if h + 1 < K.heads:
                exps(h + 1)
            hi(h)

    class Decode:
        def __init__(self, name, pages, heads, kv, qB, t, qscr, base, scale, oT, oL):
            self.name, self.pages, self.heads, self.kv, self.qB, self.t = name, pages, heads, kv, qB, t
            self.qscr, self.base, self.scale, self.oH, self.oL = qscr, base, scale, oT, oL
            self.dh = BR_W // heads
            self.et = self.dh // P
            self.q = 1 if name == "A" else 0

    DKM = Decode("M", 2, M_HEADS, kvM, qBM, DM, "qm", 0, M_DH ** -0.5, omH, omL)
    DKA = Decode("A", NPAGES, A_HEADS, kvA, qBA, DA, "qa", 2 * DEC * 2, A_DH ** -0.5, oaH, oaL)

    def sp_mem_pages(sp, values, i, p):
        K = DKM
        b = i * 2 + p
        if not values:
            wait_count(sp, kq_ready, i * 2 + (p - 1))
            sp.dma_start(K.qB[:, p, :], scratch[K.qscr][bass.ds(b, 1), :].to_broadcast([P, BR_W])
                         ).then_inc(qb_in[p], 16)
        for g in range(K.pages):
            n = p * K.pages + g
            wait_count(sp, kv_used[n], i + values * (DEC // 2))
            src = d["cache_mem_v" if values else "cache_mem_k"][
                bass.ds(b, 1), g * P:(g + 1) * P, :].rearrange("a p c -> (a p) c")
            sp.dma_start(K.kv[:, n, :], src).then_inc(kv_full[n], 16)

    def dve_mem_scores(dve, i, p):
        K = DKM
        dve.wait_ge(qb_in[p], i * 16 + 16)
        wait_count(dve, kq_ready, i * 2 + (p - 1))
        for g in range(K.pages):
            n = p * K.pages + g
            dve.wait_ge(kv_full[n], i * 16 + 16)
            for h in range(K.heads):
                k = K.kv[:, n, h * K.dh:(h + 1) * K.dh]
                last = nc.vector.tensor_tensor_reduce(k, k, K.qB[:, p, h * K.dh:(h + 1) * K.dh], 1.0, 0.0,
                                                      ALU.mult, ALU.add, Sb[:, p, g, h:h + 1])
            last.then_inc(kv_used[n], 1)
        dve.wait_ge(kv_used[n], i + 1)
        nc.vector.tensor_copy(K.t["S"][:, bass.ds(i * 2 + p, 1), :, :],
                              Sb[:, p:p + 1, 0:K.pages, 0:K.heads]).then_inc(kq_ready, 1)

    def dve_softmax(dve, link, K):
        t = K.t
        w = DEC * K.heads
        S, L = t["S"], t["L"]
        by = lambda x: x[:, :, :].unsqueeze(2).to_broadcast([P, DEC, K.pages, K.heads])
        if K.name == "A":
            dve.wait_ge(gate_ps, 1)
            g2 = PS[:, 0, 0:DEC * NPAGES * A_HEADS].rearrange("p (b n two h) -> p b n two h", b=DEC, two=2, h=A_HEADS)
            for n in range(N_BLOCKS):
                nc.vector.tensor_copy(t["gate"][:, :, n, :], g2[:, :, n, 0, :])
            link(nc.vector.tensor_copy(t["excl"][:, :, 0, :], g2[:, :, 0, 1, :]))
            for n in range(N_BLOCKS):
                last = nc.vector.tensor_tensor(t["gate"][:, :, n, :], t["gate"][:, :, n, :], g2[:, :, n, 1, :], ALU.add)
            link(last)
            assert N_BLOCKS == MOBA_TOPK + 1
            for n in range(N_BLOCKS):
                first = True
                for m in range(N_BLOCKS):
                    if m == n:
                        continue
                    dst = t["excl"][:, :, n, :] if first else t["cmp"][:, :, :]
                    link(nc.vector.tensor_tensor(dst, t["gate"][:, :, m, :], t["gate"][:, :, n, :],
                                                 ALU.is_ge if m < n else ALU.is_gt))
                    if not first:
                        link(nc.vector.tensor_tensor(t["excl"][:, :, n, :], t["excl"][:, :, n, :],
                                                     t["cmp"][:, :, :], ALU.mult))
                    first = False
            for b in range(DEC):
                last = nc.vector.scalar_tensor_tensor(L[:, b, :, :], S[:, b, :, :], K.scale, biasD[:, :, :],
                                                      ALU.mult, ALU.add)
            link(last)
            for g in range(NPAGES):
                last = nc.vector.scalar_tensor_tensor(L[:, :, g, :], t["excl"][:, :, g * PAGE // MOBA_BLOCK, :],
                                                      NEG_INF, L[:, :, g, :], ALU.mult, ALU.add)
            link(last)
        else:
            link(nc.vector.tensor_scalar(L[:, :, :, :], S[:, :, :, :], K.scale, None, ALU.mult))
        nc.vector.tensor_reduce(t["mp"][:, :, :], L[:, :, :, :].rearrange("p b g h -> p b h g"),
                                AX.X, ALU.max).then_inc(d_max, 1)
        dve.wait_ge(d_maxall, K.q + 1)
        if K.name == "A":
            link(nc.vector.tensor_scalar(t["om"][:, :, :], PS[:, 1, 0:w].rearrange("p (h b) -> p b h", h=A_HEADS),
                                         K.scale, None, ALU.mult))
            link(nc.vector.tensor_tensor(t["om"][:, :, :], t["om"][:, :, :],
                                         bias0[:, :].unsqueeze(1).to_broadcast([P, DEC, A_HEADS]), ALU.add))
            link(nc.vector.tensor_tensor(t["mx"][:, :, :], t["mx"][:, :, :], t["om"][:, :, :], ALU.max))
            link(nc.vector.tensor_tensor(t["om"][:, :, :], t["om"][:, :, :], t["mx"][:, :, :], ALU.subtract))
        for g in range(K.pages):
            last = nc.vector.tensor_tensor(L[:, :, g, :], L[:, :, g, :], t["mx"][:, :, :], ALU.subtract)
        last.then_inc(d_logit, 1)
        dve.wait_ge(d_exp, K.q + 1)
        nc.vector.tensor_reduce(t["se"][:, :, :], L[:, :, :, :].rearrange("p b g h -> p b h g"),
                                AX.X, ALU.add).then_inc(d_sb, 1)
        dve.wait_ge(sum_ps, K.q + 1)
        tot = PS[:, 3, 0:w].rearrange("p (b h) -> p b h", b=DEC)
        if K.name == "A":
            link(nc.vector.tensor_tensor(t["rd"][:, :, :], tot, t["eo"][:, :, :], ALU.add))
        else:
            link(nc.vector.tensor_copy(t["rd"][:, :, :], tot))
        link(nc.vector.reciprocal(t["x1"][:, :, :], t["rd"][:, :, :]))
        for g in range(K.pages):
            last = nc.vector.tensor_tensor(L[:, :, g, :], L[:, :, g, :], t["x1"][:, :, :], ALU.mult)
        last.then_inc(d_prob, 1)

    def act_softmax(act, K):
        act.wait_ge(d_logit, K.q + 1)
        last = nc.scalar.activation(K.t["L"][:, :, :, :], K.t["L"][:, :, :, :], ACT.Exp)
        if K.name == "A":
            last = nc.scalar.activation(K.t["eo"][:, :, :], K.t["om"][:, :, :], ACT.Exp)
        last.then_inc(d_exp, 1)

    def pool_softmax(pool, K):
        pool.wait_ge(d_max, K.q + 1)
        nc.gpsimd.partition_all_reduce(K.t["mx"][:, :, :].rearrange("p b h -> p (b h)"),
                                       K.t["mp"][:, :, :].rearrange("p b h -> p (b h)"), P,
                                       bass.bass_isa.ReduceOp.max).then_inc(d_maxall, 1)

    def pe_softmax(pe, K):
        w = DEC * K.heads
        if K.name == "A":
            pe.wait_ge(s_in_place, DEC)
            nc.tensor.matmul(PS[:, 1, 0:w], ones[:, :], own[:, :, :].rearrange("p h b -> p (h b)"),
                             start=True, stop=True)
            nc.tensor.matmul(PS[:, 0, 0:DEC * K.pages * K.heads], ones[:, :],
                             K.t["S"][:, :, :, :].rearrange("p b g h -> p (b g h)"), start=True, stop=True
                             ).then_inc(gate_ps, 1)
        pe.wait_ge(d_sb, K.q + 1)
        nc.tensor.matmul(PS[:, 3, 0:w], ones[:, :], K.t["se"][:, :, :].rearrange("p b h -> p (b h)"),
                         start=True, stop=True).then_inc(sum_ps, 1)

    def pe_values(pe, K):
        pe.wait_ge(d_prob, K.q + 1)
        def body(i):
            for p in range(2):
                wait_count(pe, d_os, i * 2 + (p - 1))
                for g in range(K.pages):
                    n = p * K.pages + g
                    s = n % 4
                    pe.wait_ge(kv_full[s], i * (16 * (2 * K.pages // 4)) + 16 * (
                        (K.base + DEC * K.pages + n) // 4 + 1))
                    for t in range(BT):
                        last = nc.tensor.matmul(
                            PS[:, 4 + p, t:t + 1], K.kv[:, s, t * P:(t + 1) * P],
                            K.t["L"][:, bass.ds(i * 2 + p, 1), g, t // K.et:t // K.et + 1].rearrange(
                                "p a h -> p (a h)"),
                            start=g == 0 and t == 0, stop=g == K.pages - 1, skip_group_check=True)
                    last.then_inc(kv_used[s], 1)

        first_apart(pe, DEC // 2, body)

    def dve_values(dve, K):
        with dve.Fori(0, DEC // 2) as i:
            for p in range(2):
                n = K.base + DEC * K.pages + (p + 1) * K.pages - 1
                dve.wait_ge(kv_used[n % 4], i * (2 * K.pages // 4) + (n // 4 + 1))
                nc.vector.tensor_copy(K.t["oS"][:, :, bass.ds(i * 2 + p, 1)],
                                      PS[:, 4 + p, 0:BT].rearrange("p (a c) -> p a c", c=1)).then_inc(d_os, 1)

    def dve_decode_out(dve, link, K, done):
        t = K.t
        o_s = t["oS"][:, :, :]
        if K.name == "A":
            link(nc.vector.tensor_tensor(t["eo"][:, :, :], t["eo"][:, :, :], t["x1"][:, :, :], ALU.mult))
            link(nc.vector.tensor_tensor(t["o2"][:, :, :], vaS[:, :, :], t["eo"][:, :, :].rearrange("p b h -> p h b"),
                                         ALU.mult))
            link(nc.vector.tensor_tensor(o_s, o_s, t["o2"][:, :, :], ALU.add))
        link(nc.vector.tensor_copy(K.oH[:, :, SEQ:N], o_s))
        nc.vector.tensor_tensor(K.oL[:, :, SEQ:N], o_s, K.oH[:, :, SEQ:N].bitcast(F32),
                                ALU.subtract).then_inc(done, 1)

    def copy_evac(eng, dst):
        def evac(B, c):
            step_made(eng, B, c)
            d4 = dst[:, 4 * c:4 * c + 4, :]
            n = d4.shape[-1]
            nc.scalar.activation(d4, PS[:, 4 * c:4 * c + 4, 0:n], ACT.Copy).then_inc(set_free[c], 1)
        return evac

    def silu_evac(eng, dst):
        def evac(B, c):
            step_made(eng, B, c)
            nc.scalar.activation(dst[:, 4 * c:4 * c + 4, :], PS[:, 4 * c:4 * c + 4, 0:N],
                                 ACT.Silu).then_inc(set_free[c], 1)
        return evac

    def rotate_evac(dve, link, dst, scale):
        def evac(B, c):
            step_made(dve, B, c)
            ps = PS[:, 4 * c:4 * c + 4, 0:N].rearrange("p (h two) n -> p h two n", two=2)
            out = dst[:, 4 * c:4 * c + 4, :].rearrange("p (h two) n -> p h two n", two=2)
            for h in range(2):
                e = [EV[:, 4 * h + k, :] for k in range(4)]
                m = lambda dest, half, tab: nc.vector.scalar_tensor_tensor(
                    dest, ps[:, h, half, :], scale, tab[:, :], ALU.mult, ALU.mult)
                m(e[0], 0, cosT)
                m(e[1], 1, sinT)
                m(e[2], 0, sinT)
                link(m(e[3], 1, cosT))
                nc.vector.tensor_tensor(out[:, h, 0, :], e[0], e[1], ALU.subtract)
                last = nc.vector.tensor_tensor(out[:, h, 1, :], e[2], e[3], ALU.add)
                if h == 0:
                    link(last)
            last.then_inc(set_free[c], 1)
        return evac

    def gate_evac_act(act, i, r):
        def evac(B, c):
            step_made(act, B, c)
            for m in range(2):
                g = bass.ds(i * 4 + (G_BIAS + KT * BRANCHES[r][1] + 2 * c + m), 1)
                last = nc.scalar.activation(EV[:, 2 * c + m, :], PS[:, 4 * c + m, 0:N], ACT.Sigmoid,
                                            bias=gT[:, g])
            last.then_inc(sig_ready, 1)
        return evac

    def gate_evac_dve(dve, i, r):
        def evac(B, c):
            acc = accT[:, bass.ds(i * 4 + 2 * c, 2), :]
            gate, proj = EV[:, 2 * c:2 * c + 2, :], PS[:, 4 * c + 2:4 * c + 4, 0:N]
            dve.wait_ge(sig_ready, i * 2 + (8 * r + c + 1))
            if r == 0:
                nc.vector.tensor_tensor(acc, gate, proj, ALU.mult).then_inc(set_free[c], 1)
                return
            done = i * 2 + c if r == 1 else i * 6 + (8 + 3 * c)
            wait_count(dve, merge_step, done)
            nc.vector.tensor_tensor(EV[:, 6:8, :], gate, proj, ALU.mult).then_inc(set_free[c], 1)
            dve.wait_ge(set_free[c], B + 1)
            nc.vector.tensor_tensor(acc, acc, EV[:, 6:8, :], ALU.add).then_inc(merge_step, 1)
            if r == 2:
                hi = mgH[:, bass.ds(i * 4 + 2 * c, 2), :]
                dve.wait_ge(merge_step, done + 1)
                nc.vector.tensor_copy(hi, acc).then_inc(merge_step, 1)
                dve.wait_ge(merge_step, done + 2)
                nc.vector.tensor_tensor(mgL[:, bass.ds(i * 4 + 2 * c, 2), :], acc,
                                        hi.bitcast(F32), ALU.subtract).then_inc(merge_step, 1)
        return evac

    def dve_page(dve, i, c, g):
        s = g % 4
        n0 = DKA.base // 4
        if g == 0:
            dve.wait_ge(q_in[c], i * 16 + 16)
            wait_count(dve, s_in_place, i * 2 + (c - 1))
        dve.wait_ge(page_full[s], i * 64 + 16 * (2 * c + g // 4 + 1))
        for h in range(A_HEADS):
            k = kvA[:, s, h * P:(h + 1) * P]
            last = nc.vector.tensor_tensor_reduce(k, k, qBA[:, c, h * P:(h + 1) * P], 1.0, 0.0,
                                                  ALU.mult, ALU.add, Sb[:, c, g, h:h + 1])
        last.then_inc(kv_used[s], 1)
        if g == NPAGES - 1:
            dve.wait_ge(kv_used[s], i * 4 + (n0 + 2 * c + 2))
            nc.vector.tensor_copy(DA["S"][:, bass.ds(i * 2 + c, 1), :, :], Sb[:, c:c + 1, :, :]
                                  ).then_inc(s_in_place, 1)

    def dve_value_page(dve, i, c, g):
        s = g % 4
        n0 = DKA.base // 4 + DEC * NPAGES // 4
        if g == 0:
            nc.vector.tensor_copy(Sb[:, c:c + 1, :, :], DA["L"][:, bass.ds(i * 2 + c, 1), :, :]
                                  ).then_inc(p_in_place, 1)
            dve.wait_ge(p_in_place, i * 2 + (c + 1))
        else:
            before = DVE_PAGES[DVE_PAGES.index(g) - 1]
            dve.wait_ge(kv_used[before % 4], i * 4 + (n0 + 2 * c + before // 4 + 1))
        dve.wait_ge(page_full[s], i * 64 + 16 * (DEC * NPAGES // 4 + 2 * c + g // 4 + 1))
        if g == 0:
            last = nc.vector.tensor_tensor(
                pvSum[:, c, :].rearrange("p (h e) -> p h e", h=A_HEADS),
                kvA[:, s, :].rearrange("p (h e) -> p h e", h=A_HEADS),
                Sb[:, c, g, :].unsqueeze(2).to_broadcast([P, A_HEADS, P]), ALU.mult)
        else:
            for h in range(A_HEADS):
                acc = pvSum[:, c, h * P:(h + 1) * P]
                last = nc.vector.scalar_tensor_tensor(acc, kvA[:, s, h * P:(h + 1) * P], Sb[:, c, g, h:h + 1],
                                                      acc, ALU.mult, ALU.add)
        last.then_inc(kv_used[s], 1)

    def dve_sample_out(dve, i, k):
        dve.wait_ge(sample_summed, i * 2 + (k + 1))
        nc.vector.tensor_copy(DA["oS"][:, :, bass.ds(i * 2 + k, 1)],
                              PS[:, 4 * (1 - k % 2) + 3, 0:BT].rearrange("p (a c) -> p a c", c=1)
                              ).then_inc(os_copied, 1)

    def split_gates(split, eng, r):
        on_act = split is act_split

        def body(i):
            B = i + (B_GATE + 4 * r)
            for c in range(2):
                nB, n_c = (B, 1) if c == 0 else (B + 1, 0)
                for j, (b, cc, u, nk) in enumerate(((B, c, 2, 4), (B, c, 3, 4), (nB, n_c, 0, UK), (nB, n_c, 1, UK))):
                    split(eng, b, cc, u, nk, True)
                    if not on_act and r == 0:
                        dve_page(eng, i, c, 2 * j)
                        dve_page(eng, i, c, 2 * j + 1)
                    if not on_act and r == 1:
                        if j == 0 and not (isinstance(i, int) and c == 0):
                            dve_sample_out(eng, i, c - 1)
                        for g in ((0, 1), (2,), (4, 5), (6,))[j]:
                            dve_value_page(eng, i, c, g)
                (gate_evac_act if on_act else gate_evac_dve)(eng, i, r)(B, c)

        if on_act or r == 2:
            with eng.Fori(0, 4) as i:
                body(i)
        else:
            first_apart(eng, 4, body)
            if r == 1:
                dve_sample_out(eng, 3, 1)

    class Link:

        def __init__(self, eng, s):
            self.eng, self.s, self.n = eng, s, 0

        def __call__(self, inst):
            self.n += 1
            inst.then_inc(self.s, 1)
            self.eng.wait_ge(self.s, self.n)
            return inst

    @block.sync
    def _(sp):
        sp.dma_start(ident[:, :], d["ident"]).then_inc(ident_in, 16)
        for k, name in enumerate(("ffn1_norm", "mix_norm", "mem_norm", "ffn2_norm", "final_norm")):
            sp.dma_start(grow[KT * k:KT * (k + 1), :], d[name].rearrange("(k p) -> k p", p=P)).then_inc(gain_in, 16)
        sp.dma_start(grow[G_BIAS:P, :], d["b_gate"].rearrange("(k p) -> k p", p=P)).then_inc(gain_in, 16)
        sp.dma_start(mtok[:, :, :], d["mem_prompt"].rearrange("(t p) c -> p t c", p=P)).then_inc(mem_in, 16)
        sp.dma_start(xtok[:, :, :], d["x_prompt"].rearrange("(t p) c -> p t c", p=P)).then_inc(x_in, 16)
        sp.dma_start(stok[0:DEC, :], d["x_sample"]).then_inc(x_in, 16)
        sp_wide(sp, 0, d["w_mem_kv"], 0)
        sp_wide(sp, 1, d["w_mem_kv"], BR_W)
        sp_ffn(sp, B_FFN1, d["ffn1_w1"], d["ffn1_w3"], d["ffn1_w2"])
        with sp.Fori(0, 4) as i:
            sp_wide(sp, i + B_IN_R, d["w_in"], i * BR_W + C_QR)
        sp_wide(sp, B_IN_M, d["w_in"], C_QM, steps=(0,))
        sp_states(sp)
        sp_wide(sp, B_IN_M, d["w_in"], C_QM, steps=(1,))
        sp_wide(sp, B_IN_A, d["w_in"], C_QA, steps=(0,))
        sp.wait_ge(r_all_done, 1)
        states_away(sp)
        sp.wait_ge(kept, 64)
        for b in range(DEC):
            sp_mem_pages(sp, 0, b // 2, b % 2)
            if b >= 1:
                sp_wide_unit(sp, B_IN_A + (b + 3) // 8, d["w_in"], C_QA + BR_W * ((b + 3) // 8),
                             (b + 3) // 4 % 2, (b + 3) % 4)
        sp_wide_unit(sp, B_IN_A + 1, d["w_in"], C_QA + BR_W, 0, 3)
        first_apart(sp, DEC // 2, lambda i: [sp_mem_pages(sp, 1, i, p) for p in range(2)])
        sp_wide(sp, B_IN_A + 1, d["w_in"], C_QA + BR_W, steps=(1,))
        sp_wide(sp, B_IN_A + 2, d["w_in"], C_QA + 2 * BR_W)
        sp.wait_ge(pt_in, 16)
        sp_gates(sp)
        with sp.Fori(0, 2) as i:
            sp_wide(sp, i + B_OUT, d["w_out"], i * BR_W)
        sp_ffn(sp, B_FFN2, d["ffn2_w1"], d["ffn2_w3"], d["ffn2_w2"])
        y0 = turns_of("y")[0][0]
        sp.wait_ge(turn_out, y0 + 8)
        sp.dma_start(o["y_prompt"].rearrange("(t p) c -> p t c", p=P), ytok[:, :, :]).then_inc(y_sent, 16)
        sp.wait_ge(turn_out, y0 + 12)
        sp.dma_start(o["y_sample"], ystok[0:DEC, :]).then_inc(y_sent, 16)
        sp.wait_ge(y_sent, 32)

    @block.gpsimd
    def _(pool):
        nc.gpsimd.memset(ones[:, :], 1.0).then_inc(ones_set, 1)
        pool.dma_start(ptab[0:1, :], d["page_table"]).then_inc(pt_in, 16)
        pool.wait_ge(pt_in, 16)
        pool.wait_ge(turn_out, turns_until("mem_kv"))
        pool.dma_start(o["mem_k_prompt"].rearrange("(t p) c -> p t c", p=P), mkTok[:, :, :]).then_inc(stored, 16)
        pool.dma_start(o["mem_v_prompt"].rearrange("(t p) c -> p t c", p=P), mvTok0[:, :, :]).then_inc(stored, 16)
        pool.dma_start(scratch["mv"].rearrange("(t p) c -> p t c", p=P), mvTok0[:, :, :]).then_inc(kept, 16)
        pool.dma_start(scratch["mkT"], mkT0[:, :, :].rearrange("p a c -> p (a c)")).then_inc(kept, 16)
        pool.wait_ge(kept, 32)
        pool.wait_ge(stored, 32)
        pool.wait_ge(set_free[0], B_IN)
        pool.wait_ge(set_free[1], B_IN)
        pool.dma_start(scratch["x"], xT[:, :, :].rearrange("p a c -> p (a c)")).then_inc(x_kept, 16)
        pool.dma_start(cosT[:, :], d["cos"]).then_inc(rot_in, 16)
        pool.dma_start(sinT[:, :], d["sin"]).then_inc(rot_in, 16)
        pool.dma_start(kdecay[:, :, :], d["kdecay"]).then_inc(decay_in, 16)
        pool.dma_start(decay[:, :, :], d["decay"]).then_inc(decay_in, 16)
        pool.wait_ge(turn_out, turns_until("r"))
        pool.dma_start(scratch["vr"], vrS[0:DEC, :]).then_inc(kept, 16)
        pool.wait_ge(kept, 48)
        for h in range(R_HEADS):
            pool.wait_ge(s_out, h + 1)
            pool.dma_start(o["ret_state_prompt"][h].rearrange("(t p) e -> p t e", p=P),
                           st[:, h % 2, :, :]).then_inc(st_sent[h % 2], 16)
        pool.wait_ge(st_sent[0], 32)
        pool.wait_ge(st_sent[1], 32)
        pool.wait_ge(r_all_done, 1)
        pool.dma_start(mkT[:, :, :].rearrange("p a c -> p (a c)"), scratch["mkT"]).then_inc(mk_in, 16)
        pool.dma_start(mvTok[:, :, :], scratch["mv"].rearrange("(t p) c -> p t c", p=P)).then_inc(mk_in, 16)
        pool.wait_ge(turn_out, turns_until("m"))
        pool.dma_start(scratch["qm"], qmS[0:DEC, :]).then_inc(kept, 16)
        pool.wait_ge(kept, 64)
        pool_softmax(pool, DKM)
        pool.wait_ge(m_done, 1)
        pool.dma_start(t5w[0:T5_BUCKETS, :], d["t5_table"]).then_inc(t5_in, 16)
        pool.dma_start(bkp[0:T5_BUCKETS, :], d["bucket_prompt"]).then_inc(t5_in, 16)
        pool.dma_start(bkd[0:T5_BUCKETS, :], d["bucket_decode"]).then_inc(t5_in, 16)
        pool.wait_ge(t5_ready, 1)
        pool.dma_start(scratch["t5"], t5row[0:A_HEADS, :].unsqueeze(1).to_broadcast([A_HEADS, P, 2 * SEQ])
                       ).then_inc(kept, 16)
        pool.wait_ge(kept, 80)
        pool.wait_ge(turn_out, turns_until("a"))
        pool.dma_start(o["v_prompt"].rearrange("(t p) c -> p t c", p=P), vaTok[:, :, :]).then_inc(stored, 16)
        pool.dma_start(o["k_prompt"].rearrange("(t p) c -> p t c", p=P), kaTok[:, :, :]).then_inc(stored, 16)
        pool.dma_start(o["k_sample"], rows[0:DEC, 0, :]).then_inc(stored, 16)
        pool.dma_start(o["v_sample"], rows[0:DEC, 1, :]).then_inc(stored, 16)
        pool.dma_start(scratch["qa"], rows[0:DEC, 2, :]).then_inc(kept, 16)
        for h in range(A_HEADS):
            if h >= 2:
                pool.wait_ge(a_p, M_HEADS + h - 1)
            for it in range(2):
                diag = bass.AP(tensor=scratch["t5"].tensor, offset=h * P * 2 * SEQ + SEQ - 1 - it * P,
                               ap=[[2 * SEQ - 1, P], [1, SEQ]])
                pool.dma_start(bias[:, h % 2, it, :], diag).then_inc(bias_in[h % 2], 16)
        pool.wait_ge(kept, 96)
        pool.wait_ge(stored, 96)
        pool_softmax(pool, DKA)
        pool.wait_ge(merge_step, 8 + 3 * 8)
        pool.dma_start(xT[:, :, :].rearrange("p a c -> p (a c)"), scratch["x"]).then_inc(x_back, 16)
        pool.wait_ge(x_back, 16)

    @block.tensor
    def _(pe):
        pe.wait_ge(ident_in, 16)
        pe.wait_ge(gain_in, 96)
        pe_turns(pe, "gain")
        pe.wait_ge(mem_in, 16)
        pe_turns(pe, "mem")
        pe.wait_ge(x_in, 32)
        pe_turns(pe, "x")
        pe.wait_ge(ones_set, 1)
        pe_norm(pe, "mem")
        pe.wait_ge(norm_done, 1)
        pe.wait_ge(turn_out, turns_until("x"))
        pe_wide(pe, 0, (hH, hL), N_MEM, rest=(norm_done, 2))
        pe_wide(pe, 1, (hH, hL), N_MEM)
        pe_drained(pe, 2)
        pe_turns(pe, "mem_kv")
        pe.wait_ge(turn_out, turns_until("mem_kv"))
        pe_norm(pe, "ffn1")
        pe.wait_ge(norm_done, 3)
        pe_ffn(pe, B_FFN1, 4)
        pe_drained(pe, B_IN)
        pe_norm(pe, "mix")
        pe.wait_ge(norm_done, 5)
        with pe.Fori(0, 4) as i:
            pe_wide(pe, i + B_IN_R, (hH, hL), rest=(norm_done, 6))
        pe_drained(pe, B_IN_M)
        pe_turns(pe, "r")
        pe.wait_ge(turn_out, turns_until("r"))
        pe_retention(pe)
        pe.wait_ge(s_out, R_HEADS)
        pe_states(pe)
        pe.wait_ge(samp_sq, 1)
        for et in range(2):
            last = nc.tensor.matmul(PS[:, 5, 0:R_HEADS * DEC], ones[:, :],
                                    orS2[:, et:BT:2, :], start=et == 0, stop=et == 1)
        last.then_inc(samp_ms, 1)
        pe.wait_ge(r_all_done, 1)
        pe_wide(pe, B_IN_M, (hH, hL))
        pe_drained(pe, B_IN_A)
        pe_turns(pe, "m")
        pe.wait_ge(turn_out, turns_until("m"))
        pe.wait_ge(mk_in, 32)
        pe_attend(pe, KM)
        pe.wait_ge(a_lo, M_HEADS)
        pe_wide(pe, B_IN_A, (hH, hL))
        pe_drained(pe, B_IN_A + 1)
        pe_softmax(pe, DKM)
        pe_values(pe, DKM)
        pe.wait_ge(m_done, 1)
        with pe.Fori(1, 3) as i:
            pe_wide(pe, i + B_IN_A, (hH, hL))
        pe_drained(pe, B_GATE)
        pe.wait_ge(t5_in, 48)
        nc.tensor.matmul(PS[0:A_HEADS, 3, 0:SEQ], t5w[0:T5_BUCKETS, :], bkp[0:T5_BUCKETS, :], start=True, stop=True)
        for g in range(NPAGES):
            nc.tensor.matmul(PS[:, 2, A_HEADS * g:A_HEADS * (g + 1)], bkd[0:T5_BUCKETS, g * P:(g + 1) * P],
                             t5w[0:T5_BUCKETS, :], start=True, stop=True)
        nc.tensor.matmul(PS[:, 2, 64:64 + A_HEADS], ones[0:1, :], t5w[0:1, :],
                         start=True, stop=True).then_inc(t5_ps, 1)
        pe_turns(pe, "a")
        pe.wait_ge(turn_out, turns_until("a"))
        pe.wait_ge(own_ready, 1)
        pe_attend(pe, KA)
        pe.wait_ge(a_lo, M_HEADS + A_HEADS)
        pe_gates(pe, 0)
        pe_drained(pe, B_GATE + 4)
        pe_softmax(pe, DKA)
        pe.wait_ge(d_prob, 2)
        pe_gates(pe, 1)
        pe.wait_ge(a_done, 1)
        pe_gates(pe, 2)
        pe.wait_ge(merge_step, 8 + 3 * 4)
        with pe.Fori(0, 2) as i:
            pe_wide(pe, i + B_OUT, (mgH, mgL), rest=(merge_step, 8 + 3 * 8))
        pe_drained(pe, B_FFN2)
        pe_norm(pe, "ffn2")
        pe.wait_ge(norm_done, 7)
        pe_ffn(pe, B_FFN2, 8)
        pe_drained(pe, B_END)
        pe_norm(pe, "final")
        pe.wait_ge(norm_rows, 20)
        pe_turns(pe, "y")

    @block.scalar
    def _(act):
        act_turns(act, "gain")
        act_turns(act, "mem")
        act_turns(act, "x")
        act.wait_ge(turn_out, turns_until("x"))
        act_norm(act, "mem")
        act_split(act, 0, 0, 0)
        act_split(act, 0, 0, 1)
        split_body(act_split, act, 0, copy_evac(act, mkT0))
        split_body(act_split, act, 1, copy_evac(act, mvT0))
        act_turns(act, "mem_kv")
        act_norm(act, "ffn1")
        split_ffn(act_split, act, B_FFN1, 0, False)
        act.wait_ge(set_free[0], B_IN)
        act.wait_ge(set_free[1], B_IN)
        act_norm(act, "mix")
        act.wait_ge(stored, 32)
        act.wait_ge(kept, 32)
        split_body(act_split, act, B_IN_R, none)
        split_body(act_split, act, B_IN_R + 1, none)
        split_body(act_split, act, B_IN_R + 2, copy_evac(act, vrT))
        split_body(act_split, act, B_IN_R + 3, silu_evac(act, grT))
        act_turns(act, "r")
        act.wait_ge(kept, 48)
        act_retention(act)
        act_states(act)
        act.wait_ge(samp_var, 1)
        nc.scalar.activation(rt[:, 0:R_HEADS * DEC], rs[:, 0:R_HEADS * DEC], ACT.Sqrt).then_inc(samp_sqrt, 1)
        act.wait_ge(r_all_done, 1)
        split_body(act_split, act, B_IN_M, copy_evac(act, qmT))
        act_turns(act, "m")
        act_attend(act, KM)
        split_body(act_split, act, B_IN_A, copy_evac(act, qaT))
        act_softmax(act, DKM)
        act.wait_ge(m_done, 1)
        states_away(act)
        split_body(act_split, act, B_IN_A + 1, copy_evac(act, kaT))
        split_body(act_split, act, B_IN_A + 2, copy_evac(act, vaT))
        act.wait_ge(kept, 80)
        act.wait_ge(x_kept, 16)
        act_turns(act, "a")
        act_attend(act, KA)
        split_gates(act_split, act, 0)
        act_softmax(act, DKA)
        split_gates(act_split, act, 1)
        split_gates(act_split, act, 2)
        with act.Fori(0, 2) as i:
            split_body(act_split, act, i + B_OUT, none)
        act.wait_ge(set_free[0], B_FFN2)
        act.wait_ge(set_free[1], B_FFN2)
        act_norm(act, "ffn2")
        split_ffn(act_split, act, B_FFN2, 1, True)
        act.wait_ge(set_free[0], B_END)
        act.wait_ge(set_free[1], B_END)
        act_norm(act, "final")
        act_turns(act, "y")

    @block.vector
    def _(dve):
        link = Link(dve, dve_link)
        dve.wait_ge(turn_out, turns_until("x"))
        dve_norm(dve, link, "mem")
        dve_split(dve, 0, 0, 0)
        dve_split(dve, 0, 0, 1)
        split_body(dve_split, dve, 0, none)
        split_body(dve_split, dve, 1, none)
        dve_norm(dve, link, "ffn1")
        split_ffn(dve_split, dve, B_FFN1, 0, False)
        dve.wait_ge(set_free[0], B_IN)
        dve.wait_ge(set_free[1], B_IN)
        dve_norm(dve, link, "mix")
        dve.wait_ge(rot_in, 32)
        dve.wait_ge(stored, 32)
        dve.wait_ge(kept, 32)
        split_body(dve_split, dve, B_IN_R, rotate_evac(dve, link, qrT, 1.0))
        split_body(dve_split, dve, B_IN_R + 1, rotate_evac(dve, link, krT, R_DK ** -0.5))
        split_body(dve_split, dve, B_IN_R + 2, none)
        split_body(dve_split, dve, B_IN_R + 3, none)
        dve.wait_ge(decay_in, 32)
        dve.wait_ge(turn_out, turns_until("r"))
        dve_retention(dve, link)
        dve_states(dve)
        dve.wait_ge(os_out, DEC)
        states_away(dve)
        w = R_HEADS * DEC
        nc.vector.tensor_tensor(orS2[:, :, :], orS[:, :, :], orS[:, :, :], ALU.mult).then_inc(samp_sq, 1)
        dve.wait_ge(samp_ms, 1)
        nc.vector.tensor_scalar(rs[:, 0:w], PS[:, 5, 0:w], 1.0 / R_DV, EPS, ALU.mult, ALU.add).then_inc(samp_var, 1)
        dve.wait_ge(samp_sqrt, 1)
        link(nc.vector.reciprocal(ry[:, 0:w], rt[:, 0:w]))
        refine(link, ry[:, 0:w], rs[:, 0:w], rt[:, 0:w])
        for et in range(2):
            last = nc.vector.tensor_tensor(orS2[:, et:BT:2, :], orS[:, et:BT:2, :],
                                           ry[:, 0:w].rearrange("p (h b) -> p h b", h=R_HEADS), ALU.mult)
        link(last)
        link(nc.vector.tensor_tensor(orS2[:, :, :], orS2[:, :, :], grT[:, :, SEQ:N], ALU.mult))
        link(nc.vector.tensor_copy(orH[:, :, SEQ:N], orS2[:, :, :]))
        nc.vector.tensor_tensor(orL[:, :, SEQ:N], orS2[:, :, :], orH[:, :, SEQ:N].bitcast(F32),
                                ALU.subtract).then_inc(r_all_done, 1)
        split_body(dve_split, dve, B_IN_M, none)
        dve_attend(dve, link, KM)
        split_body(dve_split, dve, B_IN_A, none, between=lambda b: dve_mem_scores(dve, b // 2, b % 2))
        dve.wait_ge(kq_ready, DEC)
        dve_softmax(dve, link, DKM)
        dve_values(dve, DKM)
        dve.wait_ge(d_os, DEC)
        dve_decode_out(dve, link, DKM, m_done)
        for k in range(1, 3):
            split_body(dve_split, dve, B_IN_A + k, none)
        dve.wait_ge(t5_ps, 1)
        nc.vector.memset(t5row[0:A_HEADS, SEQ:2 * SEQ], NEG_INF)
        nc.vector.tensor_copy(biasD[:, :, :].rearrange("p g h -> p (g h)"), PS[:, 2, 0:64])
        nc.vector.tensor_copy(bias0[:, :], PS[:, 2, 64:64 + A_HEADS])
        nc.vector.tensor_copy(t5row[0:A_HEADS, 0:SEQ], PS[0:A_HEADS, 3, 0:SEQ]).then_inc(t5_ready, 1)
        nc.vector.tensor_copy(vaS[:, :, :], vaT[:, :, SEQ:N])
        nc.vector.tensor_tensor(own[:, :, :], qaT[:, :, SEQ:N], kaT[:, :, SEQ:N], ALU.mult).then_inc(own_ready, 1)
        dve.wait_ge(kept, 96)
        dve.wait_ge(stored, 96)
        dve_attend(dve, link, KA)
        dve.wait_ge(x_kept, 16)
        split_gates(dve_split, dve, 0)
        dve.wait_ge(s_in_place, DEC)
        dve_softmax(dve, link, DKA)
        nc.vector.memset(DA["oS"][:, :, :], 0.0).then_inc(os_copied, 1)
        dve.wait_ge(os_copied, 1)
        split_gates(dve_split, dve, 1)
        dve.wait_ge(os_copied, DEC + 1)
        dve_decode_out(dve, link, DKA, a_done)
        split_gates(dve_split, dve, 2)
        dve.wait_ge(x_back, 16)
        with dve.Fori(0, 2) as i:
            split_body(dve_split, dve, i + B_OUT, add_evac_dve(dve, i, 1.0))
        dve.wait_ge(set_free[0], B_FFN2)
        dve.wait_ge(set_free[1], B_FFN2)
        dve_norm(dve, link, "ffn2")
        split_ffn(dve_split, dve, B_FFN2, 1, True)
        dve.wait_ge(set_free[0], B_END)
        dve.wait_ge(set_free[1], B_END)
        dve_norm(dve, link, "final", yT)


_INS = {
    "x_prompt": (SEQ, D_MODEL), "x_sample": (DEC, D_MODEL), "mem_prompt": (N_MEM, D_MODEL),
    "cache_k": (-1, PAGE, BR_W), "cache_v": (-1, PAGE, BR_W),
    "cache_mem_k": (DEC, N_MEM, BR_W), "cache_mem_v": (DEC, N_MEM, BR_W),
    "state_ret": (DEC, R_HEADS, R_DK, R_DV), "page_table": (1, DEC * NPAGES), "t5_table": (T5_BUCKETS, A_HEADS),
    "ffn1_norm": (D_MODEL,), "ffn1_w1": (D_MODEL, D_FF), "ffn1_w3": (D_MODEL, D_FF), "ffn1_w2": (D_FF, D_MODEL),
    "mix_norm": (D_MODEL,), "mem_norm": (D_MODEL,), "w_in": (D_MODEL, 8 * BR_W), "w_mem_kv": (D_MODEL, 2 * BR_W),
    "w_gate": (D_MODEL, 3 * D_MODEL), "b_gate": (3 * D_MODEL,), "w_br_moba": (BR_W, D_MODEL),
    "w_br_ret": (BR_W, D_MODEL), "w_br_mem": (BR_W, D_MODEL), "w_out": (D_MODEL, D_MODEL),
    "ffn2_norm": (D_MODEL,), "ffn2_w1": (D_MODEL, D_FF), "ffn2_w3": (D_MODEL, D_FF), "ffn2_w2": (D_FF, D_MODEL),
    "final_norm": (D_MODEL,),
}
_OUTS = {
    "y_prompt": ((SEQ, D_MODEL), (1, SEQ, D_MODEL)), "y_sample": ((DEC, D_MODEL), (DEC, 1, D_MODEL)),
    "k_prompt": ((SEQ, BR_W), (1, 1, SEQ, A_HEADS, A_DH)), "v_prompt": ((SEQ, BR_W), (1, 1, SEQ, A_HEADS, A_DH)),
    "mem_k_prompt": ((N_MEM, BR_W), (1, 1, N_MEM, M_HEADS, M_DH)),
    "mem_v_prompt": ((N_MEM, BR_W), (1, 1, N_MEM, M_HEADS, M_DH)),
    "ret_state_prompt": ((R_HEADS, R_DK, R_DV), (1, 1, R_HEADS, R_DK, R_DV)),
    "k_sample": ((DEC, BR_W), (1, DEC, 1, A_HEADS, A_DH)), "v_sample": ((DEC, BR_W), (1, DEC, 1, A_HEADS, A_DH)),
    "ret_state_sample": ((DEC, R_HEADS, R_DK, R_DV), (1, DEC, R_HEADS, R_DK, R_DV)),
}


def kernel(**inputs):
    from contextlib import ExitStack
    import concourse.bacc as bacc
    from concourse.bass_utils import run_bass_kernel_spmd

    nc = bacc.Bacc("TRN2", target_bir_lowering=False, num_devices=1)
    arrays = {n: np.ascontiguousarray(inputs[n]).reshape(s) for n, s in _INS.items()}
    arrays.update(constants())
    d = {n: nc.dram_tensor(n, a.shape, mybir.dt.from_np(a.dtype), kind="ExternalInput").ap()
         for n, a in arrays.items()}
    o = {n: nc.dram_tensor(f"out_{n}", s, F32, kind="ExternalOutput").ap() for n, (s, _) in _OUTS.items()}
    with ExitStack() as ctx:
        PS = ctx.enter_context(nc.psum_tensor("PS", [P, 8, 512], F32))
        build(nc, d, o, lambda name: ctx.enter_context(nc.semaphore(name)), PS,
              ctx.enter_context(nc.Block()))
    r = run_bass_kernel_spmd(nc, [arrays], core_ids=[0])
    return tuple(r.results[0][f"out_{n}"].reshape(s) for n, (_, s) in _OUTS.items())
```
